# Optimizing a Trainium2 kernel written in Bass

```python
import math
import jax, jax.numpy as jnp
from jax import lax
import numpy as np

D_MODEL = 1024
BATCH = 1
SEQ = 512
DEPTH = 1

FOX_HEADS = 8
FOX_HEAD_DIM = 64
FOX_WIDTH = FOX_HEADS * FOX_HEAD_DIM
DIFF_HEADS = 4
DIFF_QK_DIM = 64
DIFF_V_DIM = 2 * DIFF_QK_DIM
DIFF_WIDTH = DIFF_HEADS * DIFF_V_DIM
BRANCH_WIDTH = 512
N_BRANCHES = 2

BLOCK_Q = 128
ROPE_THETA = 10000.0
NORM_EPS = 1e-6
SUBLN_EPS = 1e-5

SPLIT_SIZES = [
    FOX_WIDTH,
    FOX_WIDTH,
    FOX_WIDTH,
    FOX_HEADS,
    FOX_WIDTH,
    DIFF_HEADS * 2 * DIFF_QK_DIM,
    DIFF_HEADS * 2 * DIFF_QK_DIM,
    DIFF_WIDTH,
    DIFF_WIDTH,
    N_BRANCHES * D_MODEL,
]
N_IN = sum(SPLIT_SIZES)
SPLIT_POINTS = [int(v) for v in np.cumsum(SPLIT_SIZES)[:-1]]


def lambda_init_for(layer_idx):
    return 0.8 - 0.6 * math.exp(-0.3 * (layer_idx - 1))

def rms_norm(x, g, eps):
    xf = x.astype(jnp.float32)
    y = xf * lax.rsqrt(jnp.mean(xf * xf, axis=-1, keepdims=True) + eps)
    return (y * g.astype(jnp.float32)).astype(x.dtype)

def rope_tables(seq, dim):
    pos = jnp.arange(seq, dtype=jnp.float32)
    inv_freq = ROPE_THETA ** (-jnp.arange(0, dim, 2, dtype=jnp.float32) / dim)
    ang = pos[:, None] * inv_freq[None, :]
    return jnp.cos(ang), jnp.sin(ang)

def apply_rope(x, cos, sin):
    x1, x2 = jnp.split(x, 2, axis=-1)
    c = cos.astype(x.dtype)
    s = sin.astype(x.dtype)
    return jnp.concatenate([x1 * c - x2 * s, x2 * c + x1 * s], axis=-1)

def split_heads(t, n_heads):
    b, s, _ = t.shape
    return t.reshape(b, s, n_heads, -1).transpose(0, 2, 1, 3)

def merge_heads(t):
    b, h, s, d = t.shape
    return t.transpose(0, 2, 1, 3).reshape(b, s, h * d)

def fox_attention(q, k, v, log_f):
    b, h, s, d = q.shape
    nb = s // BLOCK_Q
    scale = 1.0 / math.sqrt(d)
    c = jnp.cumsum(log_f, axis=-1)
    qb = q.reshape(b, h, nb, BLOCK_Q, d).transpose(2, 0, 1, 3, 4)
    cb = c.reshape(b, h, nb, BLOCK_Q).transpose(2, 0, 1, 3)
    kpos = jnp.arange(s)

    def step(args):
        i, qi, ci = args
        qpos = i * BLOCK_Q + jnp.arange(BLOCK_Q)
        logits = jnp.einsum('bhqd,bhkd->bhqk', qi, k).astype(jnp.float32) * scale
        logits = logits + ci[..., :, None] - c[..., None, :]
        logits = jnp.where(kpos[None, :] <= qpos[:, None], logits, -jnp.inf)
        p = jax.nn.softmax(logits, axis=-1)
        return jnp.einsum('bhqk,bhkd->bhqd', p.astype(v.dtype), v)

    out = lax.map(step, (jnp.arange(nb), qb, cb))
    return out.transpose(1, 2, 0, 3, 4).reshape(b, h, s, d)

def diff_attention(q, k, v, lam):
    b, h, _, s, d = q.shape
    nb = s // BLOCK_Q
    scale = 1.0 / math.sqrt(d)
    qb = q.reshape(b, h, 2, nb, BLOCK_Q, d).transpose(3, 0, 1, 2, 4, 5)
    kpos = jnp.arange(s)

    def step(args):
        i, qi = args
        qpos = i * BLOCK_Q + jnp.arange(BLOCK_Q)
        logits = jnp.einsum('bhmqd,bhmkd->bhmqk', qi, k).astype(jnp.float32) * scale
        logits = jnp.where(kpos[None, :] <= qpos[:, None], logits, -jnp.inf)
        p = jax.nn.softmax(logits, axis=-1)
        pd = p[:, :, 0] - lam * p[:, :, 1]
        return jnp.einsum('bhqk,bhkd->bhqd', pd.astype(v.dtype), v)

    out = lax.map(step, (jnp.arange(nb), qb))
    return out.transpose(1, 2, 0, 3, 4).reshape(b, h, s, v.shape[-1])

def first_inputs(seed: int = 0) -> dict:
    key = jax.random.key(seed)
    ks = jax.random.split(key, 13)
    f32 = jnp.float32
    x = jax.random.normal(ks[0], (BATCH, SEQ, D_MODEL), f32)
    g_pre = 1.0 + 0.1 * jax.random.normal(ks[1], (DEPTH, D_MODEL), f32)
    w_in = jax.random.normal(ks[2], (DEPTH, D_MODEL, N_IN), f32) * D_MODEL ** -0.5
    b_forget = jax.random.uniform(ks[3], (DEPTH, FOX_HEADS), f32, minval=1.0, maxval=5.0)
    lambda_q1 = 0.1 * jax.random.normal(ks[4], (DEPTH, DIFF_QK_DIM), f32)
    lambda_k1 = 0.1 * jax.random.normal(ks[5], (DEPTH, DIFF_QK_DIM), f32)
    lambda_q2 = 0.1 * jax.random.normal(ks[6], (DEPTH, DIFF_QK_DIM), f32)
    lambda_k2 = 0.1 * jax.random.normal(ks[7], (DEPTH, DIFF_QK_DIM), f32)
    g_subln = 1.0 + 0.1 * jax.random.normal(ks[8], (DEPTH, DIFF_V_DIM), f32)
    w_branch = jax.random.normal(ks[9], (DEPTH, N_BRANCHES, BRANCH_WIDTH, D_MODEL), f32) * BRANCH_WIDTH ** -0.5
    w_out = jax.random.normal(ks[10], (DEPTH, D_MODEL, D_MODEL), f32) * D_MODEL ** -0.5
    g_post = 1.0 + 0.1 * jax.random.normal(ks[11], (DEPTH, D_MODEL), f32)
    return {"x": x, "g_pre": g_pre, "w_in": w_in, "b_forget": b_forget,
            "lambda_q1": lambda_q1, "lambda_k1": lambda_k1,
            "lambda_q2": lambda_q2, "lambda_k2": lambda_k2,
            "g_subln": g_subln, "w_branch": w_branch, "w_out": w_out,
            "g_post": g_post}

def first_block(x, g_pre, w_in, b_forget, lambda_q1, lambda_k1, lambda_q2, lambda_k2,
              g_subln, w_branch, w_out, g_post):
    b, s, _ = x.shape
    cos, sin = rope_tables(s, DIFF_QK_DIM)
    for l in range(DEPTH):
        lam_init = lambda_init_for(l + 1)
        h = rms_norm(x, g_pre[l], NORM_EPS)
        proj = jnp.einsum('bsd,dn->bsn', h, w_in[l])
        qa, ka, va, fa, za, qb, kb, vb, zb, gates = jnp.split(proj, SPLIT_POINTS, axis=-1)

        log_f = jax.nn.log_sigmoid((fa + b_forget[l]).astype(jnp.float32)).transpose(0, 2, 1)
        ya = fox_attention(split_heads(qa, FOX_HEADS), split_heads(ka, FOX_HEADS),
                           split_heads(va, FOX_HEADS), log_f)
        ya = merge_heads(ya) * jax.nn.silu(za)

        qd = apply_rope(qb.reshape(b, s, DIFF_HEADS, 2, DIFF_QK_DIM).transpose(0, 2, 3, 1, 4), cos, sin)
        kd = apply_rope(kb.reshape(b, s, DIFF_HEADS, 2, DIFF_QK_DIM).transpose(0, 2, 3, 1, 4), cos, sin)
        vd = split_heads(vb, DIFF_HEADS)
        lam = (jnp.exp(jnp.sum(lambda_q1[l].astype(jnp.float32) * lambda_k1[l].astype(jnp.float32)))
               - jnp.exp(jnp.sum(lambda_q2[l].astype(jnp.float32) * lambda_k2[l].astype(jnp.float32)))
               + lam_init)
        yb = diff_attention(qd, kd, vd, lam)
        yb = rms_norm(yb, g_subln[l], SUBLN_EPS) * (1.0 - lam_init)
        yb = merge_heads(yb) * jax.nn.silu(zb)

        gate_a, gate_b = jnp.split(jax.nn.sigmoid(gates), N_BRANCHES, axis=-1)
        merged = (gate_a * jnp.einsum('bsw,wd->bsd', ya, w_branch[l, 0])
                  + gate_b * jnp.einsum('bsw,wd->bsd', yb, w_branch[l, 1]))
        y = jnp.einsum('bsd,de->bse', merged, w_out[l])
        x = x + rms_norm(y, g_post[l], NORM_EPS)
    return x


MEM_LEN = 256
A_HEADS = 8
A_HEAD_DIM = 64
A_WIDTH = A_HEADS * A_HEAD_DIM
MOBA_BLOCK = 256
MOBA_TOPK = 3
Q_BLOCK = 128
G_HEADS = 4
G_WIDTH = D_MODEL - A_WIDTH
G_HEAD_V = G_WIDTH // G_HEADS
G_KEY_WIDTH = G_WIDTH // 2
G_HEAD_K = G_KEY_WIDTH // G_HEADS
G_GATE_RANK = 16
G_GATE_NORM = 16.0
G_CHUNK = 64
MIX_WIDTH = A_WIDTH + G_WIDTH
IN_SPLITS = (A_WIDTH, A_WIDTH, A_WIDTH, G_KEY_WIDTH, G_KEY_WIDTH, G_WIDTH, G_GATE_RANK, G_WIDTH)
IN_COLS = 3 * A_WIDTH + 2 * G_KEY_WIDTH + G_WIDTH + G_GATE_RANK + G_WIDTH
X_HEADS = 4
X_HEAD_DIM = D_MODEL // X_HEADS
D_FF = 4 * D_MODEL
RP_BUCKETS = 32
RP_MAX_DIST = 128
EPS = 1e-6


def rms_norm_2(x, g):
    xf = x.astype(jnp.float32)
    y = xf * lax.rsqrt(jnp.mean(xf * xf, axis=-1, keepdims=True) + EPS)
    return (y * g.astype(jnp.float32)).astype(x.dtype)

def rel_bucket(dist):
    max_exact = RP_BUCKETS // 2
    d = jnp.maximum(dist, 0)
    large = max_exact + (jnp.log(jnp.maximum(d, 1).astype(jnp.float32) / max_exact)
                         / math.log(RP_MAX_DIST / max_exact) * (RP_BUCKETS - max_exact)).astype(jnp.int32)
    large = jnp.minimum(large, RP_BUCKETS - 1)
    return jnp.where(d < max_exact, d, large)

def moba_attention(q, k, v, rp_table):
    B, T, H, dh = q.shape
    nb = -(-T // MOBA_BLOCK)
    pad = nb * MOBA_BLOCK - T
    kp = jnp.pad(k, ((0, 0), (0, pad), (0, 0), (0, 0)))
    vp = jnp.pad(v, ((0, 0), (0, pad), (0, 0), (0, 0)))
    kb = kp.reshape(B, nb, MOBA_BLOCK, H, dh).transpose(0, 3, 1, 2, 4)
    vb = vp.reshape(B, nb, MOBA_BLOCK, H, dh).transpose(0, 3, 1, 2, 4)
    nq = T // Q_BLOCK
    qc = q.reshape(B, nq, Q_BLOCK, H, dh).transpose(0, 1, 3, 2, 4).reshape(B * nq, H, Q_BLOCK, dh)
    scale = dh ** -0.5
    n_sel = min(MOBA_TOPK, nb - 1)
    table_t = rp_table.T.astype(jnp.float32)
    key_off = jnp.arange(MOBA_BLOCK, dtype=jnp.int32)
    hidx = jnp.arange(H)[:, None, None]
    b_ids = jnp.repeat(jnp.arange(B, dtype=jnp.int32), nq)
    qb_ids = jnp.tile(jnp.arange(nq, dtype=jnp.int32), B)
    xs = (qc, b_ids, qb_ids)
    if n_sel > 0:
        pos = jnp.arange(T, dtype=jnp.int32)
        q_blk = pos // MOBA_BLOCK
        kmean = jnp.mean(kb.astype(jnp.float32), axis=3)
        gate = jnp.einsum('bthd,bhnd->bhtn', q.astype(jnp.float32), kmean)
        past = jnp.arange(nb)[None, :] < q_blk[:, None]
        gate = jnp.where(past[None, None], gate, -jnp.inf)
        _, sel = lax.top_k(gate, n_sel)
        valid = sel < q_blk[None, None, :, None]
        sel_c = sel.reshape(B, H, nq, Q_BLOCK, n_sel).transpose(0, 2, 1, 3, 4).reshape(B * nq, H, Q_BLOCK, n_sel)
        valid_c = valid.reshape(B, H, nq, Q_BLOCK, n_sel).transpose(0, 2, 1, 3, 4).reshape(B * nq, H, Q_BLOCK, n_sel)
        xs = xs + (sel_c, valid_c)

    def step(args):
        qi, b, qb = args[0], args[1], args[2]
        kb_b = kb[b]
        vb_b = vb[b]
        q_pos = qb * Q_BLOCK + jnp.arange(Q_BLOCK, dtype=jnp.int32)
        own = (qb * Q_BLOCK) // MOBA_BLOCK
        k_own = lax.dynamic_index_in_dim(kb_b, own, axis=1, keepdims=False)
        v_own = lax.dynamic_index_in_dim(vb_b, own, axis=1, keepdims=False)
        d_own = q_pos[:, None] - (own * MOBA_BLOCK + key_off)[None, :]
        s_own = jnp.einsum('hqd,hld->hql', qi, k_own).astype(jnp.float32) * scale + table_t[:, rel_bucket(d_own)]
        s_own = jnp.where(d_own[None] >= 0, s_own, -jnp.inf)
        if n_sel > 0:
            sel_i, valid_i = args[3], args[4]
            k_sel = kb_b[hidx, sel_i]
            v_sel = vb_b[hidx, sel_i]
            d_sel = q_pos[None, :, None, None] - (sel_i[..., None] * MOBA_BLOCK + key_off)
            s_sel = (jnp.einsum('hqd,hqcld->hqcl', qi, k_sel).astype(jnp.float32) * scale
                     + table_t[hidx[..., None], rel_bucket(d_sel)])
            s_sel = jnp.where(valid_i[..., None], s_sel, -jnp.inf)
            s = jnp.concatenate([s_sel.reshape(H, Q_BLOCK, n_sel * MOBA_BLOCK), s_own], axis=-1)
            p = jax.nn.softmax(s, axis=-1).astype(v.dtype)
            p_sel = p[..., :n_sel * MOBA_BLOCK].reshape(H, Q_BLOCK, n_sel, MOBA_BLOCK)
            p_own = p[..., n_sel * MOBA_BLOCK:]
            return jnp.einsum('hqcl,hqcld->hqd', p_sel, v_sel) + jnp.einsum('hql,hld->hqd', p_own, v_own)
        p_own = jax.nn.softmax(s_own, axis=-1).astype(v.dtype)
        return jnp.einsum('hql,hld->hqd', p_own, v_own)

    o = lax.map(step, xs)
    return o.reshape(B, nq, H, Q_BLOCK, dh).transpose(0, 1, 3, 2, 4).reshape(B, T, H * dh)

def gla_chunked(q, k, v, log_a):
    B, T, H, dk = q.shape
    dv = v.shape[-1]
    nc = T // G_CHUNK
    scale = dk ** -0.5

    def to_chunks(t):
        return t.reshape(B, nc, G_CHUNK, H, t.shape[-1]).transpose(1, 0, 3, 2, 4)

    causal = jnp.tril(jnp.ones((G_CHUNK, G_CHUNK), dtype=bool))

    def body(S, inp):
        qi, ki, vi, gi = inp
        qf = qi.astype(jnp.float32) * scale
        kf = ki.astype(jnp.float32)
        vf = vi.astype(jnp.float32)
        b = jnp.cumsum(gi.astype(jnp.float32), axis=2)
        o_inter = jnp.einsum('bhcd,bhde->bhce', qf * jnp.exp(b), S)
        diff = b[:, :, :, None, :] - b[:, :, None, :, :]
        decay = jnp.exp(jnp.where(causal[None, None, :, :, None], diff, -jnp.inf))
        A = jnp.einsum('bhid,bhjd,bhijd->bhij', qf, kf, decay)
        o_intra = jnp.einsum('bhij,bhje->bhie', A, vf)
        b_last = b[:, :, -1:, :]
        S_new = jnp.exp(b_last[:, :, 0, :])[..., None] * S + jnp.einsum('bhcd,bhce->bhde', kf * jnp.exp(b_last - b), vf)
        return S_new, o_inter + o_intra

    S0 = jnp.zeros((B, H, dk, dv), jnp.float32)
    _, o = lax.scan(body, S0, (to_chunks(q), to_chunks(k), to_chunks(v), to_chunks(log_a)))
    return o.transpose(1, 0, 3, 2, 4).reshape(B, T, H, dv).astype(v.dtype)

def second_inputs(seed: int = 0) -> dict:
    key = jax.random.key(seed)
    ks = jax.random.split(key, 20)

    def nrm(k, shape, scale):
        return jax.random.normal(k, shape, jnp.float32) * scale

    def gain(k, shape):
        return 1.0 + 0.05 * jax.random.normal(k, shape, jnp.float32)

    L = DEPTH
    return {
        "x": nrm(ks[0], (BATCH, SEQ, D_MODEL), 1.0),
        "mem": nrm(ks[1], (BATCH, MEM_LEN, D_MODEL), 1.0),
        "rp_table": nrm(ks[2], (RP_BUCKETS, A_HEADS), 0.5),
        "norm_mix": gain(ks[3], (L, D_MODEL)),
        "w_in": nrm(ks[4], (L, D_MODEL, IN_COLS), D_MODEL ** -0.5),
        "w_gate_up": nrm(ks[5], (L, G_GATE_RANK, G_KEY_WIDTH), G_GATE_RANK ** -0.5),
        "b_gate": nrm(ks[6], (L, G_KEY_WIDTH), 0.1),
        "g_norm": gain(ks[7], (L, G_HEAD_V)),
        "w_out": nrm(ks[8], (L, MIX_WIDTH, D_MODEL), MIX_WIDTH ** -0.5),
        "norm_xattn": gain(ks[9], (L, D_MODEL)),
        "norm_mem": gain(ks[10], (L, D_MODEL)),
        "w_xq": nrm(ks[11], (L, D_MODEL, D_MODEL), D_MODEL ** -0.5),
        "w_xkv": nrm(ks[12], (L, D_MODEL, 2 * D_MODEL), D_MODEL ** -0.5),
        "w_xo": nrm(ks[13], (L, D_MODEL, D_MODEL), D_MODEL ** -0.5),
        "norm_mlp": gain(ks[14], (L, D_MODEL)),
        "w_up": nrm(ks[15], (L, D_MODEL, D_FF), D_MODEL ** -0.5),
        "w_down": nrm(ks[16], (L, D_FF, D_MODEL), D_FF ** -0.5),
        "norm_final": gain(ks[17], (D_MODEL,)),
    }

def second_block(x, mem, rp_table, norm_mix, w_in, w_gate_up, b_gate, g_norm, w_out,
              norm_xattn, norm_mem, w_xq, w_xkv, w_xo, norm_mlp, w_up, w_down, norm_final):
    B, T, _ = x.shape
    M = mem.shape[1]
    offsets = [int(o) for o in np.cumsum(IN_SPLITS)[:-1]]
    for l in range(DEPTH):
        h = rms_norm_2(x, norm_mix[l])
        proj = h @ w_in[l]
        qa, ka, va, qg, kg, vg, glr, rg = jnp.split(proj, offsets, axis=-1)
        o_a = moba_attention(qa.reshape(B, T, A_HEADS, A_HEAD_DIM),
                             ka.reshape(B, T, A_HEADS, A_HEAD_DIM),
                             va.reshape(B, T, A_HEADS, A_HEAD_DIM), rp_table)
        log_a = jax.nn.log_sigmoid((glr @ w_gate_up[l] + b_gate[l]).astype(jnp.float32)) / G_GATE_NORM
        o_g = gla_chunked(qg.reshape(B, T, G_HEADS, G_HEAD_K),
                          kg.reshape(B, T, G_HEADS, G_HEAD_K),
                          vg.reshape(B, T, G_HEADS, G_HEAD_V),
                          log_a.reshape(B, T, G_HEADS, G_HEAD_K))
        o_g = rms_norm_2(o_g, g_norm[l]).reshape(B, T, G_WIDTH) * jax.nn.silu(rg)
        x = x + jnp.concatenate([o_a, o_g], axis=-1) @ w_out[l]
        h = rms_norm_2(x, norm_xattn[l])
        m = rms_norm_2(mem, norm_mem[l])
        qx = (h @ w_xq[l]).reshape(B, T, X_HEADS, X_HEAD_DIM)
        kx, vx = jnp.split(m @ w_xkv[l], 2, axis=-1)
        kx = kx.reshape(B, M, X_HEADS, X_HEAD_DIM)
        vx = vx.reshape(B, M, X_HEADS, X_HEAD_DIM)
        s = jnp.einsum('bthd,bmhd->bhtm', qx, kx).astype(jnp.float32) * (X_HEAD_DIM ** -0.5)
        p = jax.nn.softmax(s, axis=-1).astype(vx.dtype)
        ox = jnp.einsum('bhtm,bmhd->bthd', p, vx).reshape(B, T, D_MODEL)
        x = x + ox @ w_xo[l]
        h = rms_norm_2(x, norm_mlp[l])
        x = x + jnp.square(jax.nn.relu(h @ w_up[l])) @ w_down[l]
    return rms_norm_2(x, norm_final)


def setup_inputs(seed=0):
    out = dict(first_inputs(seed))
    for name, value in second_inputs(seed + 1).items():
        if name != "x":
            out[name + "_2"] = value
    return out


def reference(
    x, g_pre, w_in, b_forget, lambda_q1, lambda_k1, lambda_q2, lambda_k2, g_subln, w_branch,
    w_out, g_post, mem_2, rp_table_2, norm_mix_2, w_in_2, w_gate_up_2, b_gate_2, g_norm_2,
    w_out_2, norm_xattn_2, norm_mem_2, w_xq_2, w_xkv_2, w_xo_2, norm_mlp_2, w_up_2, w_down_2,
    norm_final_2,
):
    x = first_block(
        x, g_pre, w_in, b_forget, lambda_q1, lambda_k1, lambda_q2, lambda_k2, g_subln, w_branch,
        w_out, g_post,
    )
    return second_block(
        x, mem_2, rp_table_2, norm_mix_2, w_in_2, w_gate_up_2, b_gate_2, g_norm_2, w_out_2,
        norm_xattn_2, norm_mem_2, w_xq_2, w_xkv_2, w_xo_2, norm_mlp_2, w_up_2, w_down_2,
        norm_final_2,
    )


_drawn_inputs = setup_inputs


def setup_inputs(seed=0):
    import zlib

    import numpy as np

    out = dict(_drawn_inputs(seed))
    spreads = {}
    factors = {'b_gate_2': 3.925,
     'g_norm_2': 4.151,
     'norm_xattn_2': 8.0,
     'norm_mem_2': 8.0,
     'norm_mlp_2': 6.568}
    for name, (base, spread) in spreads.items():
        noise = np.random.default_rng([zlib.crc32(name.encode()), seed]).standard_normal(out[name].shape)
        drawn = base * np.exp(spread * noise) if base else spread * noise
        out[name] = __import__('jax').numpy.asarray(drawn.astype(out[name].dtype))
    for name, factor in factors.items():
        out[name] = (out[name] * factor).astype(out[name].dtype)
    return out
```

```python
from contextlib import ExitStack
import math

import numpy as np

import concourse.bass as bass
from concourse import mybir

F32 = mybir.dt.float32
F32R = mybir.dt.float32r
BF16 = mybir.dt.bfloat16
I32 = mybir.dt.int32
ALU = mybir.AluOpType
ACT = mybir.ActivationFunctionType
AX = mybir.AxisListType.X

P = 128
T = 512
NT = T // P
D = 1024
KT = D // P
MEM = 256
HD = 64
FF_CHUNKS = 4
EPS = 1e-6
SUBLN_EPS = 1e-5
LAM_INIT = 0.8 - 0.6 * math.exp(-0.3 * 0)
FAR = -1.0e30
PT_STRIDE = 384
PT_COLS = PT_STRIDE * 3 + T
P_OFF = [0, 128, 384, 768]
P_COLS = 1280
BIAS_COLS = 384
LEVELS = [64, 32, 16, 8, 4, 2, 1]

C1 = {"qa": 0, "ka": 512, "va": 1024, "fa": 1536, "za": 1544, "qb": 2056, "kb": 2568, "vb": 3080, "zb": 3592,
      "gA": 4104, "gB": 5128}
C2 = {"qa": 0, "ka": 512, "va": 1024, "qg": 1536, "kg": 1792, "vg": 2048, "glr": 2560, "rg": 2576}


class Plan:

    def __init__(self):
        self.unit0, self.step0, self.group0 = {}, {}, {}
        self.unit_last_step = []
        self.group_step, self.kind, self.act_n, self.dve_n = [], [], [], []
        self.steps = 0

    def start(self, name):
        self.unit0[name] = len(self.unit_last_step)
        self.step0[name] = self.steps
        self.group0[name] = len(self.kind)

    def group(self, kind):
        self.kind.append(kind)
        self.act_n.append((self.act_n[-1] if self.act_n else 0) + ("A" in kind))
        self.dve_n.append((self.dve_n[-1] if self.dve_n else 0) + ("D" in kind))
        self.steps += 1
        self.group_step.append(self.steps)

    def t_units(self, n, kind, groups=2):
        for _ in range(n):
            for _ in range(groups):
                self.group(kind)
            self.unit_last_step.append(self.steps)

    def m_units(self, pairs, kind, tiles=NT):
        for _ in range(pairs):
            self.steps += 1
            self.unit_last_step.append(self.steps)
            for _ in range(tiles):
                self.group(kind)
            self.unit_last_step.append(self.steps)


def make_plan():
    p = Plan()

    def phase(name, fill, *args, **kw):
        p.start(name)
        fill(*args, **kw)

    def groups(n, kind):
        for _ in range(n):
            p.group(kind)

    phase("fa", p.t_units, 1, "D", groups=1)
    phase("qa", p.t_units, 2, "AD")
    phase("ka", p.t_units, 2, "AD")
    phase("va", p.m_units, 1, "AD")
    phase("fox_pv", groups, 8, "AD")
    phase("za", p.t_units, 2, "AD")
    phase("qb", p.t_units, 2, "AD")
    phase("kb", p.t_units, 2, "AD")
    phase("vb", p.m_units, 1, "AD")
    phase("diff_pv", groups, 4, "A")
    phase("subln", groups, 4, "A")
    phase("zb", p.t_units, 2, "AD")
    p.start("gates")
    for _ in range(4):
        p.t_units(2, "A")
        p.t_units(1, "D", groups=4)
    phase("out1", p.m_units, 2, "AD")
    phase("bias", groups, 1, "D")
    phase("glr", p.t_units, 1, "A", groups=1)
    phase("qg", p.t_units, 1, "A")
    phase("gup", groups, 2, "D")
    phase("kg", p.t_units, 1, "A")
    phase("vg", p.m_units, 1, "A")
    phase("rg", p.t_units, 2, "A")
    phase("levels", groups, 4 * (len(LEVELS) + 1), "D")
    phase("cross", groups, 8, "A")
    phase("gla_pv", groups, 4, "A")
    phase("gnorm", groups, 4, "A")
    phase("qa2", p.t_units, 2, "AD")
    phase("ka2", p.t_units, 2, "AD")
    phase("va2", p.m_units, 1, "AD")
    phase("moba_pv", groups, 8, "AD")
    phase("out2", p.m_units, 2, "D")
    phase("kx", p.t_units, 4, "AD")
    phase("vx", p.m_units, 2, "AD", tiles=2)
    phase("xq", p.t_units, 4, "AD")
    phase("x_pv", groups, 8, "AD")
    phase("xo", p.m_units, 2, "D")
    p.start("mlp")
    for _ in range(FF_CHUNKS):
        p.t_units(4, "AD")
        p.m_units(2, "D")
    return p


PLAN = make_plan()
S0 = {"fox": 0, "diff": 32, "moba": 64, "x": 96}
R0 = {"norm1": 0, "fox": 8, "diff": 40, "mix": 56, "moba": 64, "mem": 96, "nx": 100, "x": 108, "nmlp": 124}
H0 = {"norm1": 0, "mix": 4, "mem": 8, "nx": 10, "nmlp": 14}
Q0 = {"norm1": 0, "mix": 4, "mem": 8, "nx": 10, "nmlp": 14, "final": 18}
V0 = {"fox": 0, "diff": 32, "moba": 48, "x": 80}
N0 = {"norm1": 0, "post": 4, "mix": 8, "mem": 12, "nx": 14, "nmlp": 18, "final": 22}


def shape_constants():
    half = HD // 2
    inv_freq = np.float32(10000.0) ** (-np.arange(0, HD, 2, dtype=np.float32) / np.float32(HD))
    angle = (np.arange(T, dtype=np.float32)[None, :] * inv_freq.astype(np.float32)[:, None]).astype(np.float64)
    rope_cos = np.tile(np.cos(angle), (P // half, 1)).astype(np.float32)
    rope_sin = np.tile(np.concatenate([-np.sin(angle), np.sin(angle)]), (P // HD, 1)).astype(np.float32)
    dist = np.maximum(256 - np.arange(BIAS_COLS), 0)
    large = 16 + (np.log(np.maximum(dist, 1).astype(np.float32) / np.float32(16)) / np.float32(math.log(128 / 16))
                  * np.float32(16)).astype(np.int32)
    bucket = np.where(dist < 16, dist, np.minimum(large, 31))
    one_hot = (np.arange(32)[:, None] == bucket[None, :]).astype(np.float32)
    j, i = np.arange(P)[:, None], np.arange(P)[None, :]
    masks = [(j // (2 * s) == i // (2 * s)) & (j % (2 * s) < s) & (i % (2 * s) >= s) for s in LEVELS] + [j == i]
    level_masks = np.stack(masks, axis=1).astype(np.int32)
    return {"rope_cos": rope_cos, "rope_sin": rope_sin, "bucket_one_hot": one_hot, "level_masks": level_masks}


class Offsets:

    def __init__(self, unit=0, step=0, act=0, dve=0):
        self.unit, self.step, self.act, self.dve = unit, step, act, dve


HERE = Offsets()


def gate_offsets(i):
    return Offsets(unit=i * 6, step=i * 16, act=i * 8, dve=i * 8)


def mlp_offsets(i):
    return Offsets(unit=i * 8, step=i * 18, act=i * 8, dve=i * 16)


def two_blocks_kernel(nc, a, out):
    w_in = a["w_in"][0]
    w_in_2 = a["w_in_2"][0]
    w_branch = a["w_branch"].rearrange("l b w d -> (l b w) d")
    w_out = a["w_out"][0]
    w_out_2 = a["w_out_2"][0]
    w_xq, w_xkv, w_xo = a["w_xq_2"][0], a["w_xkv_2"][0], a["w_xo_2"][0]
    w_up, w_down = a["w_up_2"][0], a["w_down_2"][0]
    x_in = a["x"].rearrange("b (t p) d -> p (b t) d", p=P)
    mem_in = a["mem_2"].rearrange("b (t p) d -> p (b t) d", p=P)
    x_out = out.rearrange("b (t p) d -> p (b t) d", p=P)
    x1_dram = a["x1_dram"].rearrange("(t p) d -> p t d", p=P)
    bias_dram = a["bias_dram"]
    G, K_, ST, AN, DN = PLAN.group0, PLAN.kind, PLAN.group_step, PLAN.act_n, PLAN.dve_n
    U0 = PLAN.unit0

    with ExitStack() as ctx:
        def region(*sets):
            made, size = {}, 0
            for bufs in sets:
                with ExitStack() as one:
                    used = 0
                    for name, shape, dt in bufs:
                        made[name] = one.enter_context(nc.sbuf_tensor(name, shape, dt))
                        used += math.prod(shape[1:]) * {F32: 4, F32R: 4, BF16: 2, I32: 4}[dt]
                    size = max(size, used)
            ctx.enter_context(nc.sbuf_tensor(f"region_of_{sets[0][0][0]}", [P, (size + 31) // 32 * 8], F32))
            return made

        def sb(name, shape, dt):
            return ctx.enter_context(nc.sbuf_tensor(name, shape, dt))

        def sem(name):
            return ctx.enter_context(nc.semaphore(name))

        w_raw = [sb(f"w_raw{i}", [P, 2048], F32) for i in range(2)]
        w_hi = [sb(f"w_hi{i}", [P, 2048], F32R) for i in range(2)]
        w_lo = [sb(f"w_lo{i}", [P, 2048], F32R) for i in range(2)]
        B = {}
        act8 = [P, KT, T]
        B |= region([("h_hi", act8, F32R), ("h_lo", act8, F32R)], [("moba_tmp", [P, 2, T], F32)])
        B |= region(
            [("q_st", act8, F32R), ("k_hh", act8, F32R), ("k_ll", act8, F32R), ("v_hl", [P, NT, 2 * T], F32R)],
            [("y_hi", act8, F32R), ("y_lo", act8, F32R), ("m_hi", act8, F32R), ("m_lo", act8, F32R)],
            [("g_q", [P, 2, T], F32), ("g_k", [P, 2, T], F32), ("g_b", [P, 2, T], F32), ("g_d", [P, 2, 2, T], F32),
             ("g_z", [P, 2, 2, T], F32), ("g_qe", [P, 2, T], F32), ("g_kd", [P, 2, T], F32),
             ("g_kx", [P, 2, 3, P], F32), ("g_v", [P, NT, T], F32), ("g_keep", [P, T], F32),
             ("g_mask", [P, len(LEVELS) + 1, P], I32), ("g_up", [P, 256], F32), ("g_lr", [P, T], F32),
             ("g_x", [P, 2, T], F32), ("beta", [P, BIAS_COLS], F32), ("one_hot", [P, BIAS_COLS], F32)],
            [("xq_hi", act8, F32R), ("xq_lo", act8, F32R), ("xk_hi", [P, KT, MEM], F32R),
             ("xk_lo", [P, KT, MEM], F32R), ("xv_hi", [P, 2, D], F32R), ("xv_lo", [P, 2, D], F32R)],
            [("u_hi", act8, F32R), ("u_lo", act8, F32R)])
        small = [P, T]
        B |= region(
            [("pt_hi", [P, 2, PT_COLS], F32R), ("pt_lo", [P, 2, PT_COLS], F32R), ("p0", [P, P_COLS], F32),
             ("px", [P, P_COLS + 2 * T], F32)],
            [("x_m", [P, NT, D], F32), ("h_m", [P, 2, D], F32), ("y_m", [P, NT, D], F32)],
            [("rope_c", small, F32), ("rope_s", small, F32), ("t_a", [P, 2, T], F32), ("t_b", [P, 2, T], F32),
             ("t_c", [P, 2, T], F32), ("t_sq", [P, 2, T], F32), ("t_r", [P, 2, T], F32), ("t_g", [P, 4, T], F32)],
            [("g_a", [P, 4, PT_COLS], F32)],
            [("h_m2", [P, 2, D], F32), ("gain2", [P, 2, D], F32), ("junk2", [P, D], BF16),
             ("mem_hi", [P, KT, MEM], F32R), ("mem_lo", [P, KT, MEM], F32R)],
            [("pad_x", [P, 4608], F32), ("xpt_hi", [P, 2, 2 * T], F32R), ("xpt_lo", [P, 2, 2 * T], F32R),
             ("xp", [P, NT, MEM], F32)],
            [("pad_f", [P, 4608], F32), ("relu", [P, 2, T], F32), ("u_f", [P, 2, T], F32)])
        B |= region(
            [("y_0", [P, NT, T], F32), ("y_1", [P, NT, T], F32)],
            [("gain", [P, 2, D], F32), ("junk", [P, D], BF16), ("lam_v", [P, 4, HD], F32)],
            [("x_res", [P, NT, D], F32)])
        ident = sb("ident", [P, P], F32)
        flip = sb("flip", [P, P], F32)
        ones = sb("ones", [P, P], F32)
        ident_b = sb("ident_b", [P, P], BF16)
        future_b = sb("future_b", [P, P], BF16)
        pick = sb("pick", [P, 8], F32R)
        c_row = sb("c_row", [P, T], F32R)
        b_forget = sb("b_forget", [P, 1], F32)
        g_subln = sb("g_subln", [P, 1], F32)
        b_gate = sb("b_gate", [P, 2], F32)
        g_gain = sb("g_gain", [P, 1], F32)
        rp_table = sb("rp_table", [P, 8], F32)
        lam_d = sb("lam_d", [P, 2], F32)
        lam_e = sb("lam_e", [P, 2], F32)
        neg_lam = sb("neg_lam", [P, 1], F32)
        minus_half = sb("minus_half", [P, 1], F32)
        eps_n = sb("eps_n", [P, 2], F32)
        sumsq = sb("sumsq", [P, 26, 2], F32)
        var = sb("var", [P, 26], F32)
        rstd = sb("rstd", [P, 26], F32)
        neg_max = sb("neg_max", [P, 112], F32)
        denom = sb("denom", [P, 112], F32)
        rden = sb("rden", [P, 112], F32)
        g_tail = sb("g_tail", [P, 2, NT], F32)

        lin = ctx.enter_context(nc.psum_tensor("lin", [P, 4, T], F32))
        sc = ctx.enter_context(nc.psum_tensor("sc", [P, 2, T], F32))
        tr = ctx.enter_context(nc.psum_tensor("tr", [P, 2, T], F32))

        w_loaded = [sem(f"w_loaded{i}") for i in range(2)]
        w_slot_free = sem("w_slot_free")
        w_claimed = sem("w_claimed")
        w_split = sem("w_split")
        lin_step = sem("lin_step")
        act_evac = sem("act_evac")
        dve_evac = sem("dve_evac")
        consts_made = sem("consts_made")
        small_in = sem("small_in")
        x_in_s = [sem(f"x_in{t}") for t in range(NT)]
        sq_done = sem("sq_done")
        var_done = sem("var_done")
        rstd_done = sem("rstd_done")
        h_ready = sem("h_ready")
        tr_done = sem("tr_done")
        tr_hi = sem("tr_hi")
        tr_lo = sem("tr_lo")
        s_done = sem("s_done")
        s_max = sem("s_max")
        s_exp = sem("s_exp")
        s_rec = sem("s_rec")
        s_norm = sem("s_norm")
        pd_done = sem("pd_done")
        y_norm = sem("y_norm")
        dve_self = sem("dve_self")
        act_self = sem("act_self")
        pool_self = sem("pool_self")
        small_in2 = sem("small_in2")
        gain_in = [sem(f"gain_in{i}") for i in range(6)]
        lam_exp = sem("lam_exp")
        lam_ready = sem("lam_ready")
        fa_ln = sem("fa_ln")
        c_ready = sem("c_ready")
        rope_in = sem("rope_in")
        rot_mul = sem("rot_mul")
        rope_done = sem("rope_done")
        rope_hi = sem("rope_hi")
        rope_lo = sem("rope_lo")
        sq_t = sem("sq_t")
        y_hi_s = sem("y_hi_s")
        y_lo_s = sem("y_lo_s")
        mg_sum = sem("mg_sum")
        mg_hi = sem("mg_hi")
        mg_lo = sem("mg_lo")
        x_again = sem("x_again")
        x1_ready = sem("x1_ready")
        x1_parked = sem("x1_parked")
        x1_back = sem("x1_back")
        gla_in = sem("gla_in")
        gla_const = sem("gla_const")
        beta_ready = sem("beta_ready")
        beta_out = sem("beta_out")
        bias_in = sem("bias_in")
        gla_ln = sem("gla_ln")
        gd_done = sem("gd_done")
        ge_done = sem("ge_done")
        gz_done = sem("gz_done")
        mem_in_s = sem("mem_in_s")
        u_sum = sem("u_sum")
        u_hi_s = sem("u_hi_s")
        u_lo_s = sem("u_lo_s")
        final_ready = sem("final_ready")
        out_done = sem("out_done")

        def as_f32(ap):
            return ap.bitcast(F32)

        def blocks(buf, slot, i):
            base = buf[:, slot, P * i:P * i + P]
            return bass.AP(base.tensor, base.offset, [list(base.ap[0]), [PT_STRIDE, i + 1], [1, P]])

        def diagonal(buf, slot):
            return buf[:, slot, :].rearrange("p (a b) -> p a b", b=P)[:, 0:13:4, :]

        bias_tiles = B["px"][:, 0:8 * 256].rearrange("p (h c) -> p h c", h=8)
        fox_tmp = B["px"][:, P_COLS:P_COLS + 2 * T].rearrange("p (s t) -> p s t", s=2)

        def t_source(w, c0, width=256):
            return w[:, c0:c0 + width].rearrange("(k p) n -> p k n", p=P)

        def m_sources(w, c0):
            return [w[T * kh:T * kh + T, c0:c0 + T].rearrange("(k p) n -> p k n", p=P) for kh in range(2)]

        units_1 = ([t_source(w_in, C1["fa"], P)]
                   + [t_source(w_in, C1[n] + 256 * u) for n in ("qa", "ka") for u in range(2)]
                   + m_sources(w_in, C1["va"])
                   + [t_source(w_in, C1[n] + 256 * u) for n in ("za", "qb", "kb") for u in range(2)]
                   + m_sources(w_in, C1["vb"])
                   + [t_source(w_in, C1["zb"] + 256 * u) for u in range(2)])
        units_2 = (m_sources(w_out, 0) + m_sources(w_out, T)
                   + [t_source(w_in_2, C2["glr"], P), t_source(w_in_2, C2["qg"]), t_source(w_in_2, C2["kg"])]
                   + m_sources(w_in_2, C2["vg"])
                   + [t_source(w_in_2, C2[n] + 256 * u) for n in ("rg", "qa", "ka") for u in range(2)]
                   + m_sources(w_in_2, C2["va"])
                   + m_sources(w_out_2, 0) + m_sources(w_out_2, T)
                   + [t_source(w_xkv, 256 * u) for u in range(4)]
                   + m_sources(w_xkv, D) + m_sources(w_xkv, D + T)
                   + [t_source(w_xq, 256 * u) for u in range(4)]
                   + m_sources(w_xo, 0) + m_sources(w_xo, T))
        assert U0["gates"] == len(units_1) and U0["mlp"] == U0["out1"] + len(units_2) and U0["mlp"] % 2 == 0
        assert U0["gates"] % 2 == 1

        block = ctx.enter_context(nc.Block())

        @block.sync
        def _(sp):
            def load_unit(u, src, off=None):
                if u >= 2:
                    sp.wait_ge(w_split, 2 * (u - 1) + 2 * (off or HERE).unit)
                if off is not None:
                    sp.sem_inc(w_slot_free, 1)
                k, n = src.shape[1], src.shape[2]
                dst = w_raw[u % 2][:, 0:k * n].rearrange("p (k n) -> p k n", k=k)
                sp.dma_start(dst, src).then_inc(w_loaded[u % 2], 16)

            for t in range(NT):
                sp.dma_start(B["x_m"][:, t, :], x_in[:, t, :]).then_inc(x_in_s[t], 16)
            for u, src in enumerate(units_1):
                load_unit(u, src)
            with sp.Fori(0, 2) as i:
                off = gate_offsets(i)
                for c in range(2):
                    for n, w, c0 in ((0, w_in, C1["gA"]), (1, w_in, C1["gB"]), (2, w_branch, 0)):
                        cols = bass.ds(i * 512 + (c0 + 256 * c), 256)
                        load_unit(U0["gates"] + 3 * c + n, w[:, cols].rearrange("(k p) n -> p k n", p=P), off)
            for u, src in enumerate(units_2):
                load_unit(U0["out1"] + u, src)
            with sp.Fori(0, FF_CHUNKS) as i:
                off = mlp_offsets(i)
                for c in range(4):
                    cols = bass.ds(i * D + 256 * c, 256)
                    load_unit(U0["mlp"] + c, w_up[:, cols].rearrange("(k p) n -> p k n", p=P), off)
                for j in range(2):
                    for kh in range(2):
                        rows = bass.ds(i * D + T * kh, T)
                        src = w_down[rows, T * j:T * j + T].rearrange("(k p) n -> p k n", p=P)
                        load_unit(U0["mlp"] + 4 + 2 * j + kh, src, off)
            for t in range(NT):
                sp.wait_ge(final_ready, t + 1)
                sp.dma_start(x_out[:, t, :], B["x_res"][:, t, :]).then_inc(out_done, 16)
            sp.wait_ge(out_done, 16 * NT)
            sp.wait_ge(x1_parked, 16 * NT)
            sp.wait_ge(beta_out, 16)

        @block.gpsimd
        def _(pool):
            own = [0]

            def link(ins):
                own[0] += 1
                ins.then_inc(pool_self, 1)
                pool.wait_ge(pool_self, own[0])

            def split_unit(u, cols=2048, off=None):
                o = off or HERE
                pool.wait_ge(w_loaded[u % 2], 16 * (u // 2 + 1) + o.unit * 8)
                if u >= 2:
                    pool.wait_ge(lin_step, PLAN.unit_last_step[u - 2] + o.step)
                if off is not None:
                    pool.sem_inc(w_claimed, 1)
                raw, hi, lo = (b[u % 2][:, 0:cols] for b in (w_raw, w_hi, w_lo))
                pool.tensor_scalar(hi, raw, 1.0, 1.0, ALU.mult, ALU.mult).then_inc(w_split, 1)
                pool.wait_ge(w_split, 2 * u + 1 + o.unit * 2)
                pool.tensor_tensor(lo, raw, as_f32(hi), ALU.subtract).then_inc(w_split, 1)

            def root(n):
                pool.wait_ge(var_done, n + 1)
                pool.tensor_tensor(rstd[:, n:n + 1], var[:, n:n + 1], minus_half[:, :], ALU.pow)\
                    .then_inc(rstd_done, 1)

            def normalise(v, s, p):
                pool.wait_ge(s_rec, v + 1)
                pool.tensor_scalar(p, p, rden[:, s:s + 1], 1.0, ALU.mult, ALU.mult).then_inc(s_norm, 1)

            for buf, value in ((ident[:, :], 0.0), (flip[:, :], 0.0), (ones[:, :], 1.0), (ident_b[:, :], 0.0),
                               (future_b[:, :], 0.0), (as_f32(c_row[:, :]), 0.0), (minus_half[:, :], -0.5),
                               (eps_n[:, 0:1], SUBLN_EPS), (eps_n[:, 1:2], EPS)):
                link(pool.memset(buf, value))
            for buf, sign, base in ((ident, -1, 0), (flip, 1, 1 - P), (ident_b, -1, 0)):
                link(pool.affine_select(out=buf[:, :], in_=buf[:, :], compare_op=ALU.not_equal, fill=1.0,
                                        base=base, pattern=[[sign, P]], channel_multiplier=1))
            pool.affine_select(out=future_b[:, :], in_=future_b[:, :], compare_op=ALU.is_ge, fill=FAR, base=0,
                               pattern=[[-1, P]], channel_multiplier=1).then_inc(consts_made, 1)

            split_unit(0, KT * P)
            for t in range(NT):
                root(N0["norm1"] + t)
            for u in range(1, U0["za"] + 2):
                split_unit(u)
            for m in range(32):
                i, n = m % 4, P * (m % 4 + 1)
                normalise(V0["fox"] + m, S0["fox"] + m, B["p0"][:, P_OFF[i]:P_OFF[i] + n])
            split_unit(U0["za"] + 2)
            split_unit(U0["za"] + 3)
            for c in range(8):
                pool.wait_ge(act_evac, AN[G["qb"] + c])
                if c == 0:
                    pool.wait_ge(rope_in, 32)
                t_b = B["t_b"][:, c % 2, :]
                pool.tensor_tensor(t_b, t_b, B["rope_s"][:, :], ALU.mult).then_inc(rot_mul, 1)
                if c % 2 == 1:
                    split_unit(U0["qb"] + 2 + c // 2)
            for u in range(U0["qb"] + 6, U0["zb"] + 2):
                split_unit(u)
            for w in range(16):
                i, n = w % 4, P * (w % 4 + 1)
                normalise(V0["diff"] + w, S0["diff"] + 2 * w, B["p0"][:, P_OFF[i]:P_OFF[i] + n])
            with pool.Fori(0, 2) as it:
                for c in range(6):
                    split_unit(U0["gates"] + c, off=gate_offsets(it))
            for u in range(U0["out1"], U0["glr"]):
                split_unit(u)
            split_unit(U0["glr"], KT * P)
            for t in range(NT):
                root(N0["post"] + t)
            for t in range(NT):
                root(N0["mix"] + t)
            split_unit(U0["glr"] + 1)
            pool.wait_ge(lin_step, ST[G["bias"] - 1])
            link(pool.memset(B["g_keep"][:, :], 1.0))
            link(pool.memset(B["g_keep"][:, 0:T:P], 0.0))
            pool.wait_ge(x1_parked, 16 * NT)
            pool.wait_ge(tr_done, R0["mix"] + 8)
            for h in range(4):
                ins = pool.memset(diagonal(B["g_a"], h), 0.0)
            ins.then_inc(gla_const, 1)
            for u in range(U0["glr"] + 2, U0["out2"] + 2):
                split_unit(u)
            for m in range(32):
                i, n = m % 4, P * (m % 4 + 1)
                normalise(V0["moba"] + m, S0["moba"] + m, B["p0"][:, P_OFF[i]:P_OFF[i] + n])
            for t in range(2):
                root(N0["mem"] + t)
            for u in range(U0["out2"] + 2, U0["kx"] + 2):
                split_unit(u)
            for t in range(NT):
                root(N0["nx"] + t)
            for u in range(U0["kx"] + 2, U0["xo"] + 2):
                split_unit(u)
            for m in range(16):
                normalise(V0["x"] + m, S0["x"] + m, B["xp"][:, m % 4, :])
            split_unit(U0["xo"] + 2)
            split_unit(U0["xo"] + 3)
            split_unit(U0["mlp"])
            for t in range(NT):
                root(N0["nmlp"] + t)
            split_unit(U0["mlp"] + 1)
            with pool.Fori(0, FF_CHUNKS - 1) as it:
                for c in range(2, 10):
                    split_unit(U0["mlp"] + c, off=mlp_offsets(it))
            for c in range(2, 8):
                split_unit(U0["mlp"] + 8 * (FF_CHUNKS - 1) + c)
            for t in range(NT):
                root(N0["final"] + t)

        @block.tensor
        def _(pe):
            def bank(g, cols=T):
                return lin[:, g % 4, 0:cols]

            def claim(g, off=HERE):
                k = g - 4
                if k < 0:
                    return
                if "D" in K_[k]:
                    pe.wait_ge(dve_evac, DN[k] + off.dve)
                else:
                    pe.wait_ge(act_evac, AN[k] + off.act)

            def three(o, lh, ll, rh, rl, start, stop):
                pe.matmul(o, lh, rh, start=start, stop=False)
                pe.matmul(o, lh, rl, start=False, stop=False)
                return pe.matmul(o, ll, rh, start=False, stop=stop)

            def t_unit(u, g, rh, rl, off=HERE, tiles=2, cols=T):
                pe.wait_ge(w_split, 2 * u + 2 + off.unit * 2)
                wh, wl = (b[u % 2][:, 0:KT * P * tiles].rearrange("p (k n) -> p k n", k=KT) for b in (w_hi, w_lo))
                for n in range(tiles):
                    claim(g + n, off)
                    for k in range(KT):
                        c = slice(P * n, P * n + P)
                        mm = three(bank(g + n, cols), wh[:, k, c], wl[:, k, c], rh[:, k, 0:cols], rl[:, k, 0:cols],
                                   k == 0, k == KT - 1)
                    mm.then_inc(lin_step, 1)

            def branch_unit(u, g, off):
                pe.wait_ge(w_split, 2 * u + 2 + off.unit * 2)
                wh, wl = (b[u % 2][:, :].rearrange("p (k n) -> p k n", k=KT) for b in (w_hi, w_lo))
                for n in range(2):
                    for br in range(2):
                        q = g + 2 * n + br
                        claim(q, off)
                        for k in range(4 * br, 4 * br + 4):
                            c = slice(P * n, P * n + P)
                            mm = three(bank(q), wh[:, k, c], wl[:, k, c], B["y_hi"][:, k, :], B["y_lo"][:, k, :],
                                       k % 4 == 0, k % 4 == 3)
                        mm.then_inc(lin_step, 1)

            def m_pair(u, g, lh, ll, off=HERE, tiles=NT):
                for kh in range(2):
                    pe.wait_ge(w_split, 2 * (u + kh) + 2 + off.unit * 2)
                    wh, wl = (b[(u + kh) % 2][:, :].rearrange("p (k n) -> p k n", k=4) for b in (w_hi, w_lo))
                    for t in range(tiles):
                        if kh == 0:
                            claim(g + t, off)
                        for k in range(4):
                            c = slice(P * t, P * t + P)
                            mm = three(bank(g + t), lh[:, 4 * kh + k, c], ll[:, 4 * kh + k, c], wh[:, k, :],
                                       wl[:, k, :], kh == 0 and k == 0, kh == 1 and k == 3)
                        if kh == 1 or t == tiles - 1:
                            mm.then_inc(lin_step, 1)

            def turn_tile(name, t, src):
                pe.wait_ge(h_ready, H0[name] + t + 1)
                for half in range(2):
                    r = R0[name] + 2 * t + half
                    if r >= 2:
                        pe.wait_ge(tr_lo, r - 1)
                    for b in range(4):
                        c = P * (4 * half + b)
                        mm = pe.transpose(tr[:, r % 2, P * b:P * b + P], src[:, c:c + P], ident[:, :])
                    mm.then_inc(tr_done, 1)

            def turn_probs(r, src, n):
                if r >= 2:
                    pe.wait_ge(tr_lo, r - 1)
                for j in range(n):
                    mm = pe.transpose(tr[:, r % 2, P * j:P * j + P], src(j), ident[:, :])
                mm.then_inc(tr_done, 1)

            def stacked_scores(s, h, i, extra=None):
                if s >= 2:
                    pe.wait_ge(s_exp, s - 1)
                n = P * (i + 1)
                o = sc[:, s % 2, 0:n]
                q = B["q_st"][:, h, P * i:P * i + P]
                pe.matmul(o, q, B["k_hh"][:, h, 0:n], start=True, stop=False)
                extra(o, n)
                pe.matmul(o, q, B["k_ll"][:, h, 0:n], start=False, stop=True).then_inc(s_done, 1)

            def mask(o, i):
                pe.matmul(o[:, P * i:P * i + P], ident_b[:, :], future_b[:, :], start=False, stop=False)

            def p_tile(i, j):
                c = P_OFF[i] + P * j
                return B["p0"][:, c:c + P]

            def stacked_values(g, r, h):
                claim(g)
                pe.wait_ge(tr_lo, r)
                for j in range(NT):
                    c = slice(T * j, T * j + T - P * j)
                    v = B["v_hl"][:, j, P * h:P * h + P]
                    o = lin[:, g % 4, P * j:T]
                    pe.matmul(o, v, B["pt_hi"][:, h % 2, c], start=(j == 0), stop=False)
                    mm = pe.matmul(o, v, B["pt_lo"][:, h % 2, c], start=False, stop=(j == NT - 1))
                mm.then_inc(lin_step, 1)

            def attention(tiles, lag, scores, turn, values):
                for m in range(tiles + 5):
                    if m < tiles:
                        scores(m)
                    if 0 <= m - lag < tiles:
                        turn(m - lag)
                    if m >= 8 and m % 4 == 0:
                        values((m - 8) // 4)

            pe.wait_ge(consts_made, 1)
            for t in range(NT):
                turn_tile("norm1", t, B["h_m"][:, t % 2, :])
            pe.wait_ge(tr_lo, R0["norm1"] + 8)
            hh, hl = B["h_hi"], B["h_lo"]
            t_unit(0, G["fa"], hh, hl, tiles=1)
            for name in ("qa", "ka"):
                for u in range(2):
                    t_unit(U0[name] + u, G[name] + 2 * u, hh, hl)
            m_pair(U0["va"], G["va"], hh, hl)

            pe.wait_ge(dve_evac, DN[G["va"] + 3])
            pe.wait_ge(c_ready, 1)

            def fox_scores(m):
                h, i = m // 4, m % 4

                def extra(o, n):
                    mask(o, i)
                    pe.matmul(o, pick[:, h:h + 1].to_broadcast([P, P]), c_row[:, 0:n], start=False, stop=False)

                stacked_scores(S0["fox"] + m, h, i, extra)

            def fox_turn(m):
                pe.wait_ge(s_norm, V0["fox"] + m + 1)
                turn_probs(R0["fox"] + m, lambda j: p_tile(m % 4, j), m % 4 + 1)

            attention(32, 3, fox_scores, fox_turn,
                      lambda h: stacked_values(G["fox_pv"] + h, R0["fox"] + 4 * h + 4, h))
            for name in ("za", "qb", "kb"):
                for u in range(2):
                    t_unit(U0[name] + u, G[name] + 2 * u, hh, hl)
            m_pair(U0["vb"], G["vb"], hh, hl)

            pe.wait_ge(rope_lo, 8)
            pe.wait_ge(dve_evac, DN[G["vb"] + 3])

            def diff_scores(w):
                h, i = w // 4, w % 4
                for m in range(2):
                    stacked_scores(S0["diff"] + 2 * w + m, 2 * h + m, i, lambda o, n: mask(o, i))

            def diff_turn(w):
                pe.wait_ge(pd_done, w + 1)
                turn_probs(R0["diff"] + w, lambda j: p_tile(w % 4, j), w % 4 + 1)

            def diff_values(h):
                g = G["diff_pv"] + h
                claim(g)
                pe.wait_ge(tr_lo, R0["diff"] + 4 * h + 4)
                for j in range(NT):
                    c = slice(T * j, T * j + T - P * j)
                    v = B["v_hl"][:, j, :]
                    mm = three(lin[:, g % 4, P * j:T], v[:, P * h:P * h + P], v[:, T + P * h:T + P * h + P],
                               B["pt_hi"][:, h % 2, c], B["pt_lo"][:, h % 2, c], j == 0, j == NT - 1)
                mm.then_inc(lin_step, 1)

            attention(16, 3, diff_scores, diff_turn, diff_values)
            for h in range(4):
                g = G["subln"] + h
                claim(g)
                pe.wait_ge(sq_t, h + 1)
                pe.matmul(bank(g), ones[:, :], B["t_sq"][:, h % 2, :], start=True, stop=True).then_inc(lin_step, 1)
            for u in range(2):
                t_unit(U0["zb"] + u, G["zb"] + 2 * u, hh, hl)
            with pe.Fori(0, 2) as it:
                off = gate_offsets(it)
                for c in range(2):
                    u, g = U0["gates"] + 3 * c, G["gates"] + 8 * c
                    t_unit(u, g, hh, hl, off)
                    t_unit(u + 1, g + 2, hh, hl, off)
                    pe.wait_ge(y_lo_s, 8)
                    branch_unit(u + 2, g + 4, off)
            pe.wait_ge(mg_lo, 8)
            for j in range(2):
                m_pair(U0["out1"] + 2 * j, G["out1"] + 4 * j, B["m_hi"], B["m_lo"])

            g = G["bias"]
            claim(g)
            pe.wait_ge(gla_in, 48)
            pe.wait_ge(small_in, 16 * 5)
            pe.matmul(lin[0:8, g % 4, 0:BIAS_COLS], rp_table[0:32, :], B["one_hot"][0:32, :], start=True, stop=True)\
                .then_inc(lin_step, 1)
            for t in range(NT):
                turn_tile("mix", t, B["h_m"][:, t % 2, :])
            pe.wait_ge(tr_lo, R0["mix"] + 8)
            t_unit(U0["glr"], G["glr"], hh, hl, tiles=1)
            t_unit(U0["qg"], G["qg"], hh, hl)
            pe.wait_ge(act_evac, AN[G["glr"]])
            for dt in range(2):
                g = G["gup"] + dt
                claim(g)
                pe.matmul(bank(g), B["g_up"][0:16, P * dt:P * dt + P], B["g_lr"][0:16, :], start=True, stop=True)\
                    .then_inc(lin_step, 1)
            t_unit(U0["kg"], G["kg"], hh, hl)
            m_pair(U0["vg"], G["vg"], hh, hl)
            for u in range(2):
                t_unit(U0["rg"] + u, G["rg"] + 2 * u, hh, hl)
            for lev in range(len(LEVELS) + 1):
                for h in range(4):
                    g = G["levels"] + 4 * lev + h
                    rows = slice(HD * (h % 2), HD * (h % 2) + HD)
                    claim(g)
                    if lev < len(LEVELS):
                        pe.wait_ge(gz_done, lev + 1)
                        key = query = B["g_z"][rows, lev % 2, h // 2, :]
                    else:
                        key, query = B["g_k"][rows, h // 2, :], B["g_q"][rows, h // 2, :]
                    for t in range(NT):
                        c = slice(P * t, P * t + P)
                        mm = pe.matmul(lin[:, g % 4, c], key[:, c], query[:, c], start=True, stop=True)
                    mm.then_inc(lin_step, 1)
            pe.wait_ge(gz_done, len(LEVELS) + 1)
            for h in range(4):
                rows = slice(HD * (h % 2), HD * (h % 2) + HD)
                kd, kx, qe = B["g_kd"][rows, h // 2, :], B["g_kx"][rows, h // 2], B["g_qe"][rows, h // 2, :]
                own = [kd[:, P * j:P * j + P] for j in range(3)]
                for part, pairs in enumerate(([(own[0], 1), (kx[:, 0], 2), (kx[:, 1], 3)],
                                              [(own[1], 2), (kx[:, 2], 3), (own[2], 3)])):
                    g = G["cross"] + 2 * h + part
                    claim(g)
                    for n, (key, i) in enumerate(pairs):
                        mm = pe.matmul(lin[:, g % 4, P * n:P * n + P], key, qe[:, P * i:P * i + P],
                                       start=True, stop=True)
                    mm.then_inc(lin_step, 1)
            for h in range(4):
                g = G["gla_pv"] + h
                claim(g)
                pe.wait_ge(act_evac, AN[G["cross"] + 2 * h + 1])
                pe.wait_ge(dve_evac, DN[G["levels"] + 4 * len(LEVELS) + h])
                for j in range(NT):
                    mm = pe.matmul(lin[:, g % 4, P * j:T], B["g_v"][:, j, P * h:P * h + P],
                                   B["g_a"][:, h, T * j:T * j + T - P * j], start=(j == 0), stop=(j == NT - 1))
                mm.then_inc(lin_step, 1)
            for h in range(4):
                g = G["gnorm"] + h
                claim(g)
                pe.wait_ge(sq_t, 4 + h + 1)
                pe.matmul(bank(g), ones[:, :], B["g_d"][:, 0, h % 2, :], start=True, stop=True).then_inc(lin_step, 1)
            for name in ("qa", "ka"):
                for u in range(2):
                    t_unit(U0[name + "2"] + u, G[name + "2"] + 2 * u, hh, hl)
            m_pair(U0["va2"], G["va2"], hh, hl)

            pe.wait_ge(dve_evac, DN[G["va2"] + 3])
            pe.wait_ge(bias_in, 16)

            def moba_scores(m):
                h, i = m // 4, m % 4
                near = max(i - 1, 0)

                def extra(o, n):
                    pe.matmul(o[:, P * near:n], flip[:, :], bias_tiles[:, h, 256 - (n - P * near):256],
                              start=False, stop=False)

                stacked_scores(S0["moba"] + m, h, i, extra)

            def moba_turn(m):
                pe.wait_ge(s_norm, V0["moba"] + m + 1)
                turn_probs(R0["moba"] + m, lambda j: p_tile(m % 4, j), m % 4 + 1)

            attention(32, 3, moba_scores, moba_turn,
                      lambda h: stacked_values(G["moba_pv"] + h, R0["moba"] + 4 * h + 4, h))
            pe.wait_ge(y_lo_s, 16)
            for j in range(2):
                m_pair(U0["out2"] + 2 * j, G["out2"] + 4 * j, B["y_hi"], B["y_lo"])

            for t in range(2):
                turn_tile("mem", t, B["h_m2"][:, t, :])
            pe.wait_ge(tr_lo, R0["mem"] + 4)
            for u in range(4):
                t_unit(U0["kx"] + u, G["kx"] + 2 * u, B["mem_hi"], B["mem_lo"], cols=MEM)
            for j in range(2):
                m_pair(U0["vx"] + 2 * j, G["vx"] + 2 * j, B["mem_hi"], B["mem_lo"], tiles=2)
            for t in range(NT):
                turn_tile("nx", t, B["h_m2"][:, t % 2, :])
            pe.wait_ge(tr_lo, R0["nx"] + 8)
            for u in range(4):
                t_unit(U0["xq"] + u, G["xq"] + 2 * u, hh, hl)
            pe.wait_ge(dve_evac, DN[G["xq"] + 7])

            def x_scores(m):
                h, i = m // 4, m % 4
                s = S0["x"] + m
                pe.wait_ge(s_exp, s - 1)
                for kk in range(2):
                    f = 2 * h + kk
                    c = slice(P * i, P * i + P)
                    mm = three(sc[:, s % 2, 0:MEM], B["xq_hi"][:, f, c], B["xq_lo"][:, f, c], B["xk_hi"][:, f, :],
                               B["xk_lo"][:, f, :], kk == 0, kk == 1)
                mm.then_inc(s_done, 1)

            def x_turn(m):
                pe.wait_ge(s_norm, V0["x"] + m + 1)
                turn_probs(R0["x"] + m, lambda j: B["xp"][:, m % 4, P * j:P * j + P], 2)

            def x_values(h):
                pe.wait_ge(tr_lo, R0["x"] + 4 * h + 4)
                for dv in range(2):
                    g = G["x_pv"] + 2 * h + dv
                    claim(g)
                    for j in range(2):
                        c = slice(256 * h + P * dv, 256 * h + P * dv + P)
                        k = slice(T * j, T * j + T)
                        mm = three(bank(g), B["xv_hi"][:, j, c], B["xv_lo"][:, j, c], B["xpt_hi"][:, h % 2, k],
                                   B["xpt_lo"][:, h % 2, k], j == 0, j == 1)
                    mm.then_inc(lin_step, 1)

            attention(16, 3, x_scores, x_turn, x_values)
            pe.wait_ge(dve_evac, DN[G["x_pv"] + 7])
            for j in range(2):
                m_pair(U0["xo"] + 2 * j, G["xo"] + 4 * j, hh, hl)

            for t in range(NT):
                turn_tile("nmlp", t, B["h_m2"][:, t % 2, :])
            pe.wait_ge(tr_lo, R0["nmlp"] + 8)
            with pe.Fori(0, FF_CHUNKS) as it:
                off = mlp_offsets(it)
                for u in range(4):
                    t_unit(U0["mlp"] + u, G["mlp"] + 2 * u, hh, hl, off)
                pe.wait_ge(u_lo_s, it * 8 + 8)
                for j in range(2):
                    m_pair(U0["mlp"] + 4 + 2 * j, G["mlp"] + 8 + 4 * j, B["u_hi"], B["u_lo"], off)

        @block.scalar
        def _(act):
            own = [0]

            def link(ins):
                own[0] += 1
                ins.then_inc(act_self, 1)
                act.wait_ge(act_self, own[0])

            def step(g, off=HERE):
                act.wait_ge(lin_step, ST[g] + off.step)

            def bank(g, cols=T):
                return lin[:, g % 4, 0:cols]

            def after_vector(g, off=HERE):
                act.wait_ge(dve_evac, DN[g] + off.dve)

            def load(dst, src, s):
                act.dma_start(dst, src).then_inc(s, 16)

            def row(name):
                return a[name][0:1, :].partition_broadcast(P) if len(a[name].shape) == 2 else \
                    a[name].rearrange("(o d) -> o d", o=1).partition_broadcast(P)

            def column(name):
                return a[name].rearrange("l d -> d l")

            def square_sum(q, n, x, junk, half=0):
                if q > 0:
                    act.wait_ge(sq_done, q)
                act.activation(junk, x, ACT.Square, accum_out=sumsq[:, n, half:half + 1]).then_inc(sq_done, 1)

            def turned_hi(r, out):
                act.wait_ge(tr_done, r + 1)
                act.activation(out, tr[:, r % 2, :].rearrange("p (b c) -> p b c", b=4), ACT.Copy).then_inc(tr_hi, 1)

            def turned_tile_hi(name, t, buf):
                for half in range(2):
                    turned_hi(R0[name] + 2 * t + half, buf[:, 4 * half:4 * half + 4, P * t:P * t + P])

            def q_hi(x, c, scale):
                act.activation(B["q_st"][0:64, 2 * c, :], x[0:64], ACT.Copy, scale=scale)
                return act.activation(B["q_st"][64:128, 2 * c + 1, :], x[64:128], ACT.Copy, scale=scale)

            def k_hi(x, c):
                for head in range(2):
                    rows = slice(64 * head, 64 * head + 64)
                    for half in range(2):
                        ins = act.activation(B["k_hh"][64 * half:64 * half + 64, 2 * c + head, :], x[rows], ACT.Copy)
                return ins

            def exponentials(s, p, n):
                act.wait_ge(s_max, s + 1)
                act.activation(p, sc[:, s % 2, 0:n], ACT.Exp, bias=neg_max[:, s:s + 1],
                               accum_out=denom[:, s:s + 1]).then_inc(s_exp, 1)

            def probs_hi(r, m, heads_before, g_pv):
                h, i = m // 4, m % 4
                act.wait_ge(tr_done, r + 1)
                if h >= 2:
                    act.wait_ge(lin_step, ST[g_pv + heads_before(h)])
                act.activation(blocks(B["pt_hi"], h % 2, i),
                               tr[:, r % 2, 0:P * (i + 1)].rearrange("p (j c) -> p j c", c=P), ACT.Copy)\
                    .then_inc(tr_hi, 1)

            def attention(tiles, hi, exps, values):
                for m in range(tiles + 6):
                    if 0 <= m - 4 < tiles:
                        hi(m - 4)
                    if m < tiles:
                        exps(m)
                    if m >= 9 and m % 4 == 1:
                        values((m - 9) // 4)

            def lower_half(g, tmp):
                act.activation(tmp, lin[64:128, g % 4, :], ACT.Copy).then_inc(act_evac, 1)

            def soft_log(x, t1, t2, done):
                link(act.activation(t1, x, ACT.Abs))
                link(act.activation(t2, t1, ACT.Exp, scale=-1.0))
                act.activation(t1, t2, ACT.Ln, bias=ones[0:t1.shape[0], 0:1]).then_inc(done, 1)

            def copy_lin(g, out, scale=1.0):
                step(g)
                act.activation(out, bank(g), ACT.Copy, scale=scale).then_inc(act_evac, 1)

            def head_roots(g0, y, sq, root, eps, free):
                for h in range(4):
                    if h >= 2:
                        step(g0 + h - 2)
                    act.activation(sq[:, h % 2, :], y[:, h, :], ACT.Square).then_inc(sq_t, 1)
                for h in range(4):
                    step(g0 + h)
                    if h >= 2:
                        act.wait_ge(y_norm, free + h - 1)
                    act.activation(root[:, h % 2, :], bank(g0 + h), ACT.Sqrt, scale=1.0 / P, bias=eps)\
                        .then_inc(act_evac, 1)

            load(B["gain"][:, 0, :], row("g_pre"), gain_in[0])
            for n, name in enumerate(("lambda_q1", "lambda_k1", "lambda_q2", "lambda_k2")):
                load(B["lam_v"][:, n, :], row(name), small_in2)
            with nc.allow_non_contiguous_dma(reason="one column of a few hundred bytes each"):
                load(b_forget[0:8, :], column("b_forget"), small_in)
                load(g_subln[:, :], column("g_subln"), small_in)
                load(b_gate[:, :], a["b_gate_2"].rearrange("l (t p) -> p (l t)", p=P), small_in)
                load(g_gain[:, :], column("g_norm_2"), small_in)
            load(rp_table[0:32, :], a["rp_table_2"], small_in)

            act.wait_ge(consts_made, 1)
            for t in range(NT):
                act.wait_ge(x_in_s[t], 16)
                square_sum(Q0["norm1"] + t, N0["norm1"] + t, B["x_m"][:, t, :], B["junk"][:, :])
            act.wait_ge(lam_ready, 1)
            act.activation(lam_e[:, :], lam_d[:, :], ACT.Exp).then_inc(lam_exp, 1)
            for t in range(NT):
                turned_tile_hi("norm1", t, B["h_hi"])
            act.wait_ge(dve_evac, DN[G["fa"]])
            soft_log(B["y_0"][0:8, 0, :], B["y_0"][0:8, 1, :], B["y_0"][0:8, 2, :], fa_ln)
            for c in range(4):
                step(G["qa"] + c)
                q_hi(bank(G["qa"] + c), c, HD ** -0.5).then_inc(act_evac, 1)
            for c in range(4):
                step(G["ka"] + c)
                k_hi(bank(G["ka"] + c), c).then_inc(act_evac, 1)

            def v_heads(g0):
                for t in range(NT):
                    step(g0 + t)
                    out = B["v_hl"][:, t, :].rearrange("p (h s d) -> p h s d", h=8, s=2)[:, :, 0, :]
                    act.activation(out, bank(g0 + t).rearrange("p (h d) -> p h d", h=8), ACT.Copy)\
                        .then_inc(act_evac, 1)

            v_heads(G["va"])

            def causal_exps(name, r0):
                def f(m):
                    i, n = m % 4, P * (m % 4 + 1)
                    if m >= 4:
                        act.wait_ge(tr_done, R0[name] + m - 3)
                    exponentials(S0[name] + m, B["p0"][:, P_OFF[i]:P_OFF[i] + n], n)
                return f

            def stacked_out(g0, tmp):
                def f(h):
                    step(g0 + h)
                    if h >= 2:
                        after_vector(g0 + h - 2)
                    lower_half(g0 + h, tmp[0:64, h % 2, :])
                return f

            attention(32, lambda m: probs_hi(R0["fox"] + m, m, lambda h: h - 2, G["fox_pv"]),
                      causal_exps("fox", R0["fox"]), stacked_out(G["fox_pv"], fox_tmp))

            load(B["rope_c"][:, :], a["rope_cos"], rope_in)
            load(B["rope_s"][:, :], a["rope_sin"], rope_in)
            for c in range(4):
                g = G["za"] + c
                step(g)
                after_vector(g - 2)
                act.activation(B["t_c"][:, c % 2, :], bank(g), ACT.Silu).then_inc(act_evac, 1)

            def rope_hi_part(c):
                act.wait_ge(rope_done, c + 1)
                x = B["t_a"][:, c % 2, :]
                ins = q_hi(x, c, HD ** -0.5) if c < 4 else k_hi(x, c - 4)
                ins.then_inc(rope_hi, 1)

            for c in range(8):
                g = G["qb"] + c
                step(g)
                if c >= 2:
                    act.wait_ge(rope_done, c - 1)
                for quarter in range(4):
                    rows = slice(32 * quarter, 32 * quarter + 32)
                    other = 32 * (quarter ^ 1)
                    ins = act.activation(B["t_b"][rows, c % 2, :], lin[other:other + 32, g % 4, :], ACT.Copy)
                ins.then_inc(act_evac, 1)
                if c >= 1:
                    rope_hi_part(c - 1)
            rope_hi_part(7)
            for t in range(NT):
                step(G["vb"] + t)
                act.activation(B["v_hl"][:, t, 0:T], bank(G["vb"] + t), ACT.Copy).then_inc(act_evac, 1)

            def diff_exps(w):
                i, n = w % 4, P * (w % 4 + 1)
                if w >= 4:
                    act.wait_ge(tr_done, R0["diff"] + w - 3)
                for m, buf in enumerate((B["p0"], B["px"])):
                    exponentials(S0["diff"] + 2 * w + m, buf[:, P_OFF[i]:P_OFF[i] + n], n)

            attention(16, lambda w: probs_hi(R0["diff"] + w, w, lambda h: h - 2, G["diff_pv"]), diff_exps,
                      lambda h: copy_lin(G["diff_pv"] + h, B["y_1"][:, h, :]))
            head_roots(G["subln"], B["y_1"], B["t_sq"], B["t_r"], eps_n[:, 0:1], 0)
            for c in range(4):
                g = G["zb"] + c
                step(g)
                if c >= 2:
                    after_vector(g - 2)
                act.activation(B["t_c"][:, c % 2, :], bank(g), ACT.Silu).then_inc(act_evac, 1)

            def split_y(k):
                src = B["y_0"][:, k, :] if k < 4 else B["y_1"][:, k - 4, :]
                act.activation(B["y_hi"][:, k, :], src, ACT.Copy).then_inc(y_hi_s, 1)

            after_vector(G["zb"] + 3)
            for k in range(8):
                split_y(k)
            with act.Fori(0, 2) as it:
                off = gate_offsets(it)
                for c in range(2):
                    g = G["gates"] + 8 * c
                    for n in range(4):
                        act.wait_ge(lin_step, ST[g + n] + off.step)
                        act.wait_ge(dve_evac, DN[g - 1] + off.dve)
                        act.activation(B["t_g"][:, n, :], bank(g + n), ACT.Sigmoid).then_inc(act_evac, 1)
                    for n in range(2):
                        act.wait_ge(mg_sum, it * 4 + (2 * c + n + 1))
                        act.activation(B["m_hi"][:, bass.ds(it * 4 + (2 * c + n), 1), :],
                                       B["t_c"][:, n:n + 1, :], ACT.Copy).then_inc(mg_hi, 1)

            act.wait_ge(y_lo_s, 8)
            load(B["gain"][:, 0, :], row("g_post"), gain_in[1])
            load(B["gain"][:, 1, :], row("norm_mix_2"), gain_in[2])
            act.wait_ge(mg_lo, 8)
            for t in range(NT):
                load(B["x_m"][:, t, :], x_in[:, t, :], x_again)
            for j in range(2):
                for t in range(NT):
                    g = G["out1"] + 4 * j + t
                    step(g)
                    if g > G["out1"]:
                        act.wait_ge(act_evac, AN[g] - 1)
                    act.activation(B["junk"][:, 0:T], bank(g), ACT.Square,
                                   accum_out=sumsq[:, N0["post"] + t, j:j + 1]).then_inc(act_evac, 1)
            load(B["one_hot"][0:32, :], a["bucket_one_hot"], gla_in)
            load(B["g_up"][0:16, :], a["w_gate_up_2"][0], gla_in)
            load(B["g_mask"][:, :, :], a["level_masks"], gla_in)
            for t in range(NT):
                act.wait_ge(x1_ready, t + 1)
                square_sum(Q0["mix"] + t, N0["mix"] + t, B["x_m"][:, t, :], B["junk"][:, :])
                act.dma_start(x1_dram[:, t, :], B["x_m"][:, t, :]).then_inc(x1_parked, 16)
            act.wait_ge(beta_ready, 1)
            act.dma_start(bias_dram, B["beta"][0:8, :]).then_inc(beta_out, 16)
            for t in range(NT):
                turned_tile_hi("mix", t, B["h_hi"])
            act.wait_ge(beta_out, 16)
            with nc.allow_non_contiguous_dma(reason="overlapping rows: entry (p, c) is distance entry 1 + p + c"):
                act.dma_start(bias_tiles, bass.AP(bias_dram.tensor, 1, [[1, P], [BIAS_COLS, 8], [1, 256]]))\
                    .then_inc(bias_in, 16)
            step(G["glr"])
            act.activation(B["g_lr"][0:16, :], lin[0:16, G["glr"] % 4, :], ACT.Copy).then_inc(act_evac, 1)
            for c in range(2):
                copy_lin(G["qg"] + c, B["g_q"][:, c, :], HD ** -0.5)
            act.wait_ge(dve_evac, DN[G["gup"] + 1])
            soft_log(B["g_x"][:, :, :], B["g_d"][:, 0], B["g_d"][:, 1], gla_ln)
            for c in range(2):
                copy_lin(G["kg"] + c, B["g_k"][:, c, :])

            def level_exp(lev):
                act.wait_ge(gd_done, lev + 1)
                d = B["g_d"][:, lev % 2]
                act.activation(d, d, ACT.Exp).then_inc(ge_done, 1)

            for lev in range(2):
                level_exp(lev)
            for t in range(NT):
                copy_lin(G["vg"] + t, B["g_v"][:, t, :])
            for lev in range(2, 4):
                level_exp(lev)
            for c in range(4):
                g = G["rg"] + c
                step(g)
                act.activation(B["y_0"][:, c, :], bank(g), ACT.Silu).then_inc(act_evac, 1)
            for lev in range(4, len(LEVELS) + 2):
                level_exp(lev)
            act.wait_ge(gd_done, len(LEVELS) + 2)
            act.activation(g_tail[:, :, :], B["g_b"][:, :, P - 1:T:P], ACT.Exp).then_inc(ge_done, 1)
            act.wait_ge(gla_const, 1)
            for h in range(4):
                g = G["cross"] + 2 * h
                step(g)
                act.activation(B["g_a"][:, h, P:4 * P], lin[:, g % 4, 0:3 * P], ACT.Copy).then_inc(act_evac, 1)
                step(g + 1)
                c = PT_STRIDE + 2 * P
                act.activation(B["g_a"][:, h, c:c + 2 * P], lin[:, (g + 1) % 4, 0:2 * P], ACT.Copy)
                c = 2 * PT_STRIDE + 3 * P
                act.activation(B["g_a"][:, h, c:c + P], lin[:, (g + 1) % 4, 2 * P:3 * P], ACT.Copy)\
                    .then_inc(act_evac, 1)
            for h in range(4):
                copy_lin(G["gla_pv"] + h, B["y_1"][:, h, :])
            act.wait_ge(act_evac, AN[G["gla_pv"] + 3])
            head_roots(G["gnorm"], B["y_1"], B["g_d"][:, 0], B["g_d"][:, 1], eps_n[:, 1:2], 4)
            act.wait_ge(y_norm, 8)
            for c in range(4):
                step(G["qa2"] + c)
                q_hi(bank(G["qa2"] + c), c, HD ** -0.5).then_inc(act_evac, 1)
            for c in range(4):
                step(G["ka2"] + c)
                k_hi(bank(G["ka2"] + c), c).then_inc(act_evac, 1)
            v_heads(G["va2"])
            attention(32, lambda m: probs_hi(R0["moba"] + m, m, lambda h: h - 2, G["moba_pv"]),
                      causal_exps("moba", R0["moba"]), stacked_out(G["moba_pv"], B["moba_tmp"]))
            for t in range(2):
                load(B["h_m2"][:, t, :], mem_in[:, t, :], mem_in_s)
            load(B["gain2"][:, 0, :], row("norm_mem_2"), gain_in[3])
            load(B["gain2"][:, 1, :], row("norm_xattn_2"), gain_in[3])
            after_vector(G["moba_pv"] + 7)
            for k in range(8):
                split_y(k)
            act.wait_ge(y_lo_s, 16)
            load(B["x_res"][:, :, :], x1_dram, x1_back)
            act.wait_ge(mem_in_s, 32)
            for t in range(2):
                square_sum(Q0["mem"] + t, N0["mem"] + t, B["h_m2"][:, t, :], B["junk2"][:, :])
            for t in range(NT):
                after_vector(G["out2"] + 4 + t)
                square_sum(Q0["nx"] + t, N0["nx"] + t, B["x_res"][:, t, :], B["junk2"][:, :])
                if t < 2:
                    turned_tile_hi("mem", t, B["mem_hi"])
            act.wait_ge(h_ready, H0["mem"] + 2)
            load(B["gain2"][:, 0, :], row("norm_mlp_2"), gain_in[4])
            for c in range(8):
                step(G["kx"] + c)
                act.activation(B["xk_hi"][:, c, :], bank(G["kx"] + c, MEM), ACT.Copy).then_inc(act_evac, 1)
            for j in range(2):
                for t in range(2):
                    copy_lin(G["vx"] + 2 * j + t, B["xv_hi"][:, t, T * j:T * j + T])
            for t in range(NT):
                turned_tile_hi("nx", t, B["h_hi"])
            act.wait_ge(h_ready, H0["nx"] + 4)
            load(B["gain2"][:, 1, :], row("norm_final_2"), gain_in[5])
            for c in range(8):
                copy_lin(G["xq"] + c, B["xq_hi"][:, c, :], (D // 4) ** -0.5)

            def x_exps(m):
                if m >= 4:
                    act.wait_ge(tr_done, R0["x"] + m - 3)
                exponentials(S0["x"] + m, B["xp"][:, m % 4, :], MEM)

            def x_hi(m):
                h, i, r = m // 4, m % 4, R0["x"] + m
                act.wait_ge(tr_done, r + 1)
                if h >= 2:
                    step(G["x_pv"] + 2 * (h - 2) + 1)
                out = B["xpt_hi"][:, h % 2, :].rearrange("p (j q) -> p j q", j=2)[:, :, P * i:P * i + P]
                act.activation(out, tr[:, r % 2, 0:MEM].rearrange("p (j c) -> p j c", j=2), ACT.Copy)\
                    .then_inc(tr_hi, 1)

            def x_out_hi(h):
                for dv in range(2):
                    copy_lin(G["x_pv"] + 2 * h + dv, B["h_hi"][:, 2 * h + dv, :])

            attention(16, x_hi, x_exps, x_out_hi)
            for t in range(NT):
                after_vector(G["xo"] + 4 + t)
                square_sum(Q0["nmlp"] + t, N0["nmlp"] + t, B["x_res"][:, t, :], B["junk2"][:, :])
            for t in range(NT):
                turned_tile_hi("nmlp", t, B["h_hi"])
            with act.Fori(0, FF_CHUNKS) as it:
                off = mlp_offsets(it)
                for c in range(8):
                    g = G["mlp"] + c
                    act.wait_ge(lin_step, ST[g] + off.step)
                    act.wait_ge(dve_evac, (DN[g - 2] if c >= 2 else DN[G["mlp"] - 1]) + off.dve)
                    act.activation(B["relu"][:, c % 2, :], bank(g), ACT.Relu).then_inc(act_evac, 1)
                    act.wait_ge(dve_evac, DN[g] + off.dve)
                    act.activation(B["u_hi"][:, c, :], B["u_f"][:, c % 2, :], ACT.Copy).then_inc(u_hi_s, 1)
            for t in range(NT):
                act.wait_ge(dve_evac, DN[len(K_) - 4 + t])
                square_sum(Q0["final"] + t, N0["final"] + t, B["x_res"][:, t, :], B["junk2"][:, :])

        @block.vector
        def _(dve):
            own = [0]

            def link(ins):
                own[0] += 1
                ins.then_inc(dve_self, 1)
                dve.wait_ge(dve_self, own[0])

            def step(g, off=HERE):
                dve.wait_ge(lin_step, ST[g] + off.step)

            def bank(g, cols=T):
                return lin[:, g % 4, 0:cols]

            def after_scalar(g, off=HERE):
                dve.wait_ge(act_evac, AN[g] + off.act)

            def variance(n, halves=1):
                src = sumsq[:, n, 0:1]
                if halves == 2:
                    link(dve.tensor_tensor(src, src, sumsq[:, n, 1:2], ALU.add))
                dve.tensor_scalar(var[:, n:n + 1], src, 1.0 / D, EPS, ALU.mult, ALU.add).then_inc(var_done, 1)

            def normed(name, t, out, x, gain):
                if t >= 2:
                    dve.wait_ge(tr_done, R0[name] + 2 * (t - 1))
                dve.wait_ge(rstd_done, N0[name] + t + 1)
                n = N0[name] + t
                dve.scalar_tensor_tensor(out, x, rstd[:, n:n + 1], gain, ALU.mult, ALU.mult).then_inc(h_ready, 1)

            def turned_tile_lo(name, t, hi, lo):
                for half in range(2):
                    r = R0[name] + 2 * t + half
                    k, c = slice(4 * half, 4 * half + 4), slice(P * t, P * t + P)
                    dve.wait_ge(tr_hi, r + 1)
                    dve.tensor_tensor(lo[:, k, c], tr[:, r % 2, :].rearrange("p (b c) -> p b c", b=4),
                                      as_f32(hi[:, k, c]), ALU.subtract).then_inc(tr_lo, 1)

            def lo_part(out, x, hi, scale=1.0):
                if scale == 1.0:
                    return dve.tensor_tensor(out, x, as_f32(hi), ALU.subtract)
                return dve.scalar_tensor_tensor(out, x, scale, as_f32(hi), ALU.mult, ALU.subtract)

            def q_lo(x, c, scale):
                q = B["q_st"]
                lo_part(q[64:128, 2 * c, :], x[0:64], q[0:64, 2 * c, :], scale)
                return lo_part(q[0:64, 2 * c + 1, :], x[64:128], q[64:128, 2 * c + 1, :], scale)

            def k_lo(x, c):
                for head in range(2):
                    rows = slice(64 * head, 64 * head + 64)
                    for half in range(2):
                        ins = lo_part(B["k_ll"][64 * half:64 * half + 64, 2 * c + head, :], x[rows],
                                      B["k_hh"][rows, 2 * c + head, :])
                return ins

            def row_max(s, n):
                dve.wait_ge(s_done, s + 1)
                dve.reduce_max(neg_max[:, s:s + 1], sc[:, s % 2, 0:n], AX, negate=True).then_inc(s_max, 1)

            def invert(s):
                dve.wait_ge(s_exp, s + 1)
                dve.reciprocal(rden[:, s:s + 1], denom[:, s:s + 1]).then_inc(s_rec, 1)

            def probs_lo(r, m):
                h, i = m // 4, m % 4
                dve.wait_ge(tr_hi, r + 1)
                dve.tensor_tensor(blocks(B["pt_lo"], h % 2, i),
                                  tr[:, r % 2, 0:P * (i + 1)].rearrange("p (j c) -> p j c", c=P),
                                  as_f32(blocks(B["pt_hi"], h % 2, i)), ALU.subtract).then_inc(tr_lo, 1)

            def attention(tiles, maxima, lo, inverses, values):
                for m in range(tiles + 6):
                    if m < tiles:
                        maxima(m)
                    if 0 <= m - 4 < tiles:
                        lo(m - 4)
                    if 0 <= m - 1 < tiles:
                        inverses(m - 1)
                    if m >= 9 and m % 4 == 1:
                        values((m - 9) // 4)

            def stacked_out(g0, tmp):
                def f(h):
                    g = g0 + h
                    after_scalar(g)
                    dve.tensor_tensor(B["y_0"][64 * (h % 2):64 * (h % 2) + 64, h // 2, :], lin[0:64, g % 4, :],
                                      tmp[0:64, h % 2, :], ALU.add).then_inc(dve_evac, 1)
                return f

            def causal_max(name):
                return lambda m: row_max(S0[name] + m, P * (m % 4 + 1))

            def soft_sum(x, t1, done, ready):
                dve.wait_ge(done, ready)
                link(dve.scalar_tensor_tensor(x, x, 0.0, t1, ALU.min, ALU.subtract))

            def v_heads(g0):
                for t in range(NT):
                    after_scalar(g0 + t)
                    v = B["v_hl"][:, t, :].rearrange("p (h s d) -> p h s d", h=8, s=2)
                    dve.tensor_tensor(v[:, :, 1, :], bank(g0 + t).rearrange("p (h d) -> p h d", h=8),
                                      as_f32(v[:, :, 0, :]), ALU.subtract).then_inc(dve_evac, 1)

            def head_norms(g0, y, root, free):
                for h in range(4):
                    after_scalar(g0 + h)
                    link(dve.reciprocal(root[:, h % 2, :], root[:, h % 2, :]))
                    dve.tensor_tensor(y[:, h, :], y[:, h, :], root[:, h % 2, :], ALU.mult).then_inc(y_norm, 1)

            def split_y(k):
                src = B["y_0"][:, k % 8, :] if k % 8 < 4 else B["y_1"][:, k % 8 - 4, :]
                dve.wait_ge(y_hi_s, k + 1)
                lo_part(B["y_lo"][:, k % 8, :], src, B["y_hi"][:, k % 8, :]).then_inc(y_lo_s, 1)

            dve.wait_ge(consts_made, 1)
            dve.wait_ge(small_in, 16 * 5)
            dve.tensor_tensor(pick[:, :], ident[:, 0:8], ident[:, 32:40], ALU.add)
            link(dve.tensor_scalar(g_subln[:, :], g_subln[:, :], 1.0 - LAM_INIT, None, ALU.mult))
            for t in range(NT):
                dve.wait_ge(sq_done, Q0["norm1"] + t + 1)
                variance(N0["norm1"] + t)
            dve.wait_ge(small_in2, 16 * 4)
            pairs = B["lam_v"][:, :, :].rearrange("p (a b) d -> p a b d", b=2)
            link(dve.tensor_tensor(pairs[:, :, 0, :], pairs[:, :, 0, :], pairs[:, :, 1, :], ALU.mult))
            dve.tensor_reduce(lam_d[:, :], pairs[:, :, 0, :], AX, ALU.add).then_inc(lam_ready, 1)
            dve.wait_ge(gain_in[0], 16)
            for t in range(NT):
                normed("norm1", t, B["h_m"][:, t % 2, :], B["x_m"][:, t, :], B["gain"][:, 0, :])
                if t >= 1:
                    turned_tile_lo("norm1", t - 1, B["h_hi"], B["h_lo"])
            turned_tile_lo("norm1", 3, B["h_hi"], B["h_lo"])
            dve.wait_ge(lam_exp, 1)
            link(dve.scalar_tensor_tensor(neg_lam[:, :], lam_e[:, 1:2], LAM_INIT, lam_e[:, 0:1], ALU.subtract,
                                          ALU.subtract))
            g = G["fa"]
            step(g)
            fx, ft, fc = (B["y_0"][0:8, n, :] for n in (0, 1, 3))
            f_one = B["y_1"][0:8, 0, :]
            dve.wait_ge(h_ready, H0["norm1"] + 4)
            dve.memset(f_one, 1.0)
            dve.tensor_scalar(fx, lin[0:8, g % 4, :], b_forget[0:8, :], None, ALU.add).then_inc(dve_evac, 1)
            soft_sum(fx, ft, fa_ln, 1)
            link(dve.tensor_tensor_scan(fc, f_one, fx, 0.0, ALU.mult, ALU.add))
            link(dve.tensor_scalar(c_row[0:8, :], fc, -1.0, None, ALU.mult))
            dve.scalar_tensor_tensor(c_row[32:40, :], fc, -1.0, as_f32(c_row[0:8, :]), ALU.mult, ALU.subtract)\
                .then_inc(c_ready, 1)
            for c in range(4):
                after_scalar(G["qa"] + c)
                q_lo(bank(G["qa"] + c), c, HD ** -0.5).then_inc(dve_evac, 1)
            for c in range(4):
                after_scalar(G["ka"] + c)
                k_lo(bank(G["ka"] + c), c).then_inc(dve_evac, 1)
            v_heads(G["va"])
            attention(32, causal_max("fox"), lambda m: probs_lo(R0["fox"] + m, m),
                      lambda m: invert(S0["fox"] + m), stacked_out(G["fox_pv"], fox_tmp))
            dve.wait_ge(dve_evac, DN[G["fox_pv"] + 7])
            for c in range(4):
                after_scalar(G["za"] + c)
                y = B["y_0"][:, c, :]
                dve.tensor_tensor(y, y, B["t_c"][:, c % 2, :], ALU.mult).then_inc(dve_evac, 1)
            dve.wait_ge(rope_in, 32)

            def rope_lo_part(c):
                dve.wait_ge(rope_hi, c + 1)
                x = B["t_a"][:, c % 2, :]
                ins = q_lo(x, c, HD ** -0.5) if c < 4 else k_lo(x, c - 4)
                ins.then_inc(rope_lo, 1)

            for c in range(8):
                g = G["qb"] + c
                after_scalar(g)
                if c >= 2:
                    dve.wait_ge(rope_lo, c - 1)
                x = B["t_a"][:, c % 2, :]
                dve.tensor_tensor(x, bank(g), B["rope_c"][:, :], ALU.mult).then_inc(dve_evac, 1)
                if c >= 1:
                    rope_lo_part(c - 1)
                dve.wait_ge(rot_mul, c + 1)
                dve.wait_ge(dve_evac, DN[g])
                dve.tensor_tensor(x, x, B["t_b"][:, c % 2, :], ALU.add).then_inc(rope_done, 1)
            rope_lo_part(7)
            for t in range(NT):
                after_scalar(G["vb"] + t)
                v = B["v_hl"][:, t, :]
                lo_part(v[:, T:2 * T], bank(G["vb"] + t), v[:, 0:T]).then_inc(dve_evac, 1)

            def diff_max(w):
                for m in range(2):
                    row_max(S0["diff"] + 2 * w + m, P * (w % 4 + 1))

            def diff_invert(w):
                s = S0["diff"] + 2 * w
                dve.wait_ge(s_exp, s + 2)
                dve.reciprocal(rden[:, s:s + 2], denom[:, s:s + 2]).then_inc(s_rec, 1)
                dve.wait_ge(s_rec, V0["diff"] + w + 1)
                link(dve.tensor_scalar(rden[:, s + 1:s + 2], rden[:, s + 1:s + 2], neg_lam[:, :], None, ALU.mult))

            def difference(w):
                i, s = w % 4, S0["diff"] + 2 * w
                c = slice(P_OFF[i], P_OFF[i] + P * (i + 1))
                dve.wait_ge(s_norm, V0["diff"] + w + 1)
                dve.scalar_tensor_tensor(B["p0"][:, c], B["px"][:, c], rden[:, s + 1:s + 2], B["p0"][:, c],
                                         ALU.mult, ALU.add).then_inc(pd_done, 1)

            for w in range(16 + 4):
                if 0 <= w - 2 < 16:
                    difference(w - 2)
                if w < 16:
                    diff_max(w)
                if 0 <= w - 4 < 16:
                    probs_lo(R0["diff"] + w - 4, w - 4)
                if 0 <= w - 1 < 16:
                    diff_invert(w - 1)
            head_norms(G["subln"], B["y_1"], B["t_r"], 0)
            dve.wait_ge(y_norm, 4)
            for c in range(4):
                after_scalar(G["zb"] + c)
                y = B["y_1"][:, c, :]
                dve.scalar_tensor_tensor(y, y, g_subln[:, :], B["t_c"][:, c % 2, :], ALU.mult, ALU.mult)\
                    .then_inc(dve_evac, 1)
            for k in range(8):
                split_y(k)
            with dve.Fori(0, 2) as it:
                off = gate_offsets(it)
                for c in range(2):
                    for n in range(2):
                        g = G["gates"] + 8 * c + 4 + 2 * n
                        dve.wait_ge(act_evac, AN[g] + off.act)
                        for br, buf in enumerate(("t_a", "t_b")):
                            step(g + br, off)
                            dve.tensor_tensor(B[buf][:, n, :], bank(g + br), B["t_g"][:, 2 * br + n, :], ALU.mult)\
                                .then_inc(dve_evac, 1)
                        dve.wait_ge(dve_evac, DN[g + 1] + off.dve)
                        dve.tensor_tensor(B["t_c"][:, n, :], B["t_a"][:, n, :], B["t_b"][:, n, :], ALU.add)\
                            .then_inc(mg_sum, 1)
                        dve.wait_ge(mg_hi, it * 4 + (2 * c + n + 1))
                        tile = bass.ds(it * 4 + (2 * c + n), 1)
                        dve.tensor_tensor(B["m_lo"][:, tile, :], B["t_c"][:, n:n + 1, :],
                                          as_f32(B["m_hi"][:, tile, :]), ALU.subtract).then_inc(mg_lo, 1)
            dve.wait_ge(mg_lo, 8)
            for j in range(2):
                for t in range(NT):
                    g = G["out1"] + 4 * j + t
                    after_scalar(g)
                    dve.tensor_copy(B["y_m"][:, t, T * j:T * j + T], bank(g)).then_inc(dve_evac, 1)
            for t in range(NT):
                variance(N0["post"] + t, halves=2)
            dve.wait_ge(gain_in[1], 16)
            dve.wait_ge(gain_in[2], 16)
            dve.wait_ge(x_again, 64)
            dve.wait_ge(dve_evac, DN[G["out1"] + 7])
            for t in range(NT):
                n = N0["post"] + t
                dve.wait_ge(rstd_done, n + 1)
                y = B["y_m"][:, t, :]
                link(dve.scalar_tensor_tensor(y, y, rstd[:, n:n + 1], B["gain"][:, 0, :], ALU.mult, ALU.mult))
                dve.tensor_tensor(B["x_m"][:, t, :], B["x_m"][:, t, :], y, ALU.add).then_inc(x1_ready, 1)
            for t in range(NT):
                dve.wait_ge(sq_done, Q0["mix"] + t + 1)
                variance(N0["mix"] + t)
            g = G["bias"]
            step(g)
            link(dve.tensor_copy(B["g_x"][0:8, 0, 0:1], lin[0:8, g % 4, 0:1]))
            dve.tensor_scalar(B["beta"][0:8, :], lin[0:8, g % 4, 0:BIAS_COLS], B["g_x"][0:8, 0, 0:1], None,
                              ALU.subtract).then_inc(dve_evac, 1)
            dve.wait_ge(dve_evac, DN[g])
            dve.memset(B["beta"][0:8, 257:BIAS_COLS], FAR).then_inc(beta_ready, 1)
            for t in range(NT):
                normed("mix", t, B["h_m"][:, t % 2, :], B["x_m"][:, t, :], B["gain"][:, 1, :])
                if t >= 1:
                    turned_tile_lo("mix", t - 1, B["h_hi"], B["h_lo"])
            turned_tile_lo("mix", 3, B["h_hi"], B["h_lo"])
            for dt in range(2):
                g = G["gup"] + dt
                step(g)
                dve.tensor_scalar(B["g_x"][:, dt, :], bank(g), b_gate[:, dt:dt + 1], None, ALU.add)\
                    .then_inc(dve_evac, 1)
            soft_sum(B["g_x"][:, :, :], B["g_d"][:, 0], gla_ln, 1)
            link(dve.tensor_scalar(B["g_x"][:, :, :], B["g_x"][:, :, :], 1.0 / 16.0, None, ALU.mult))
            dve.wait_ge(gla_const, 1)
            for dt in range(2):
                link(dve.tensor_tensor_scan(B["g_b"][:, dt, :], B["g_keep"][:, :], B["g_x"][:, dt, :], 0.0,
                                            ALU.mult, ALU.add))

            def halves(buf, s):
                v = buf.rearrange("p t q -> p (t q)").rearrange("p (n c) -> p n c", c=2 * s)
                return v[:, :, 0:s], v[:, :, s:2 * s]

            def level_distance(lev):
                s = LEVELS[lev]
                n = 2 * T // (2 * s)
                first, second = halves(B["g_b"][:, :, :], s)
                middle = first[:, :, s - 1:s].to_broadcast([P, n, s])
                d_first, d_second = halves(B["g_d"][:, lev % 2], s)
                if lev >= 2:
                    dve.wait_ge(gz_done, lev - 1)
                dve.tensor_tensor(d_first, middle, first, ALU.subtract)
                dve.tensor_tensor(d_second, second, middle, ALU.subtract).then_inc(gd_done, 1)

            def level_operands(lev):
                s = LEVELS[lev]
                dve.wait_ge(ge_done, lev + 1)
                if lev >= 2:
                    step(G["levels"] + 4 * (lev - 2) + 3)
                e_first, e_second = halves(B["g_d"][:, lev % 2], s)
                z_first, z_second = halves(B["g_z"][:, lev % 2], s)
                dve.tensor_tensor(z_first, e_first, halves(B["g_k"][:, :, :], s)[0], ALU.mult)
                dve.tensor_tensor(z_second, e_second, halves(B["g_q"][:, :, :], s)[1], ALU.mult).then_inc(gz_done, 1)

            def level_scores(lev):
                for h in range(4):
                    g = G["levels"] + 4 * lev + h
                    step(g)
                    if lev > 0:
                        dve.wait_ge(dve_evac, DN[g - 4])
                    dve.copy_predicated(diagonal(B["g_a"], h),
                                        B["g_mask"][:, lev:lev + 1, :].to_broadcast([P, NT, P]),
                                        bank(g).rearrange("p (t q) -> p t q", q=P)).then_inc(dve_evac, 1)

            for lev in range(2):
                level_distance(lev)
            dve.wait_ge(act_evac, AN[G["kg"] + 1])
            dve.wait_ge(gla_in, 48)
            for lev in range(2):
                level_operands(lev)
            for lev in range(2, 4):
                level_distance(lev)
            for lev in range(len(LEVELS)):
                level_scores(lev)
                if lev + 2 < len(LEVELS):
                    level_operands(lev + 2)
                if lev + 4 < len(LEVELS):
                    level_distance(lev + 4)
                if lev == 4:
                    dve.wait_ge(gz_done, len(LEVELS) - 1)
                    last = B["g_b"][:, :, P - 1:T:P].rearrange("p t (n o) -> p t n o", o=1)
                    b4 = B["g_b"][:, :, :].rearrange("p t (n c) -> p t n c", c=P)
                    for dt in range(2):
                        ins = dve.tensor_tensor(B["g_d"][:, 1, dt, :].rearrange("p (n c) -> p n c", c=P),
                                                last[:, dt].to_broadcast([P, NT, P]), b4[:, dt], ALU.subtract)
                    ins.then_inc(gd_done, 1)
            level_scores(len(LEVELS))
            dve.wait_ge(gz_done, len(LEVELS))
            dve.tensor_copy(B["g_d"][:, 0], B["g_b"][:, :, :]).then_inc(gd_done, 1)
            dve.wait_ge(ge_done, len(LEVELS) + 3)
            dve.tensor_tensor(B["g_qe"][:, :, :], B["g_d"][:, 0], B["g_q"][:, :, :], ALU.mult)
            link(dve.tensor_tensor(B["g_kd"][:, :, :], B["g_d"][:, 1], B["g_k"][:, :, :], ALU.mult))
            for dt in range(2):
                kd, kx = B["g_kd"][:, dt, :], B["g_kx"][:, dt]
                link(dve.tensor_scalar(kx[:, 0, :], kd[:, 0:P], g_tail[:, dt, 1:2], None, ALU.mult))
                dve.tensor_scalar(kx[:, 1, :], kx[:, 0, :], g_tail[:, dt, 2:3], None, ALU.mult)
                ins = dve.tensor_scalar(kx[:, 2, :], kd[:, P:2 * P], g_tail[:, dt, 2:3], None, ALU.mult)
            ins.then_inc(gz_done, 1)
            head_norms(G["gnorm"], B["y_1"], B["g_d"][:, 1], 4)
            dve.wait_ge(y_norm, 8)
            for h in range(4):
                y = B["y_1"][:, h, :]
                link(dve.scalar_tensor_tensor(y, y, g_gain[:, :], B["y_0"][:, h, :], ALU.mult, ALU.mult))
            for c in range(4):
                after_scalar(G["qa2"] + c)
                q_lo(bank(G["qa2"] + c), c, HD ** -0.5).then_inc(dve_evac, 1)
            for c in range(4):
                after_scalar(G["ka2"] + c)
                k_lo(bank(G["ka2"] + c), c).then_inc(dve_evac, 1)
            v_heads(G["va2"])
            attention(32, causal_max("moba"), lambda m: probs_lo(R0["moba"] + m, m),
                      lambda m: invert(S0["moba"] + m), stacked_out(G["moba_pv"], B["moba_tmp"]))
            for k in range(8, 16):
                split_y(k)
            for t in range(2):
                dve.wait_ge(sq_done, Q0["mem"] + t + 1)
                variance(N0["mem"] + t)
            dve.wait_ge(gain_in[3], 32)
            for t in range(2):
                normed("mem", t, B["h_m2"][:, t, :], B["h_m2"][:, t, :], B["gain2"][:, 0, :])

            def add_to_x(g, t, j, off=HERE):
                step(g, off)
                x = B["x_res"][:, t, T * j:T * j + T]
                dve.tensor_tensor(x, x, bank(g), ALU.add).then_inc(dve_evac, 1)

            dve.wait_ge(x1_back, 16)
            for j in range(2):
                for t in range(NT):
                    add_to_x(G["out2"] + 4 * j + t, t, j)
            for t in range(NT):
                dve.wait_ge(sq_done, Q0["nx"] + t + 1)
                variance(N0["nx"] + t)
                if t < 2:
                    turned_tile_lo("mem", t, B["mem_hi"], B["mem_lo"])
            for t in range(2):
                if t == 0:
                    dve.wait_ge(tr_done, R0["mem"] + 4)
                normed("nx", t, B["h_m2"][:, t, :], B["x_res"][:, t, :], B["gain2"][:, 1, :])
            for c in range(8):
                after_scalar(G["kx"] + c)
                lo_part(B["xk_lo"][:, c, :], bank(G["kx"] + c, MEM), B["xk_hi"][:, c, :]).then_inc(dve_evac, 1)
            for j in range(2):
                for t in range(2):
                    g, c = G["vx"] + 2 * j + t, slice(T * j, T * j + T)
                    after_scalar(g)
                    lo_part(B["xv_lo"][:, t, c], bank(g), B["xv_hi"][:, t, c]).then_inc(dve_evac, 1)
            for t in range(2, NT):
                normed("nx", t, B["h_m2"][:, t % 2, :], B["x_res"][:, t, :], B["gain2"][:, 1, :])
                turned_tile_lo("nx", t - 2, B["h_hi"], B["h_lo"])
            for t in range(2, NT):
                turned_tile_lo("nx", t, B["h_hi"], B["h_lo"])
            for c in range(8):
                g = G["xq"] + c
                after_scalar(g)
                lo_part(B["xq_lo"][:, c, :], bank(g), B["xq_hi"][:, c, :], (D // 4) ** -0.5).then_inc(dve_evac, 1)

            def x_lo(m):
                h, i, r = m // 4, m % 4, R0["x"] + m
                dve.wait_ge(tr_hi, r + 1)
                hi, lo = (b[:, h % 2, :].rearrange("p (j q) -> p j q", j=2)[:, :, P * i:P * i + P]
                          for b in (B["xpt_hi"], B["xpt_lo"]))
                dve.tensor_tensor(lo, tr[:, r % 2, 0:MEM].rearrange("p (j c) -> p j c", j=2), as_f32(hi),
                                  ALU.subtract).then_inc(tr_lo, 1)

            def x_out_lo(h):
                for dv in range(2):
                    g = G["x_pv"] + 2 * h + dv
                    after_scalar(g)
                    lo_part(B["h_lo"][:, 2 * h + dv, :], bank(g), B["h_hi"][:, 2 * h + dv, :]).then_inc(dve_evac, 1)

            attention(16, lambda m: row_max(S0["x"] + m, MEM), x_lo, lambda m: invert(S0["x"] + m), x_out_lo)
            for j in range(2):
                for t in range(NT):
                    add_to_x(G["xo"] + 4 * j + t, t, j)
            for t in range(NT):
                dve.wait_ge(sq_done, Q0["nmlp"] + t + 1)
                variance(N0["nmlp"] + t)
            dve.wait_ge(gain_in[4], 16)
            dve.wait_ge(gain_in[5], 16)
            for t in range(NT):
                if t == 0:
                    dve.wait_ge(tr_done, R0["nx"] + 8)
                normed("nmlp", t, B["h_m2"][:, t % 2, :], B["x_res"][:, t, :], B["gain2"][:, 0, :])
                if t >= 1:
                    turned_tile_lo("nmlp", t - 1, B["h_hi"], B["h_lo"])
            turned_tile_lo("nmlp", 3, B["h_hi"], B["h_lo"])
            with dve.Fori(0, FF_CHUNKS) as it:
                off = mlp_offsets(it)
                for c in range(8):
                    g = G["mlp"] + c
                    dve.wait_ge(act_evac, AN[g] + off.act)
                    u = B["u_f"][:, c % 2, :]
                    r = B["relu"][:, c % 2, :]
                    dve.scalar_tensor_tensor(u, bank(g), 0.0, r, ALU.max, ALU.mult).then_inc(dve_evac, 1)
                    dve.wait_ge(u_hi_s, it * 8 + (c + 1))
                    lo_part(B["u_lo"][:, c, :], u, B["u_hi"][:, c, :]).then_inc(u_lo_s, 1)
                for j in range(2):
                    for t in range(NT):
                        add_to_x(G["mlp"] + 8 + 4 * j + t, t, j, off)
            for t in range(NT):
                dve.wait_ge(sq_done, Q0["final"] + t + 1)
                variance(N0["final"] + t)
            for t in range(NT):
                n = N0["final"] + t
                dve.wait_ge(rstd_done, n + 1)
                x = B["x_res"][:, t, :]
                dve.scalar_tensor_tensor(x, x, rstd[:, n:n + 1], B["gain2"][:, 1, :], ALU.mult, ALU.mult)\
                    .then_inc(final_ready, 1)


INPUTS = ["x", "g_pre", "w_in", "b_forget", "lambda_q1", "lambda_k1", "lambda_q2", "lambda_k2", "g_subln",
          "w_branch", "w_out", "g_post", "mem_2", "rp_table_2", "norm_mix_2", "w_in_2", "w_gate_up_2", "b_gate_2",
          "g_norm_2", "w_out_2", "norm_xattn_2", "norm_mem_2", "w_xq_2", "w_xkv_2", "w_xo_2", "norm_mlp_2",
          "w_up_2", "w_down_2", "norm_final_2"]


def kernel(**inputs):
    import concourse.bacc as bacc
    from concourse.bass_utils import run_bass_kernel_spmd as run

    nc = bacc.Bacc("TRN2", target_bir_lowering=False, num_devices=1)
    arrays = {name: np.ascontiguousarray(inputs[name]) for name in INPUTS}
    arrays |= shape_constants()
    tensors = {name: nc.dram_tensor(f"in_{name}", v.shape, mybir.dt.from_np(v.dtype), kind="ExternalInput").ap()
               for name, v in arrays.items()}
    tensors["x1_dram"] = nc.dram_tensor("x1_dram", (T, D), F32, kind="Internal").ap()
    tensors["bias_dram"] = nc.dram_tensor("bias_dram", (8, BIAS_COLS), F32, kind="Internal").ap()
    out = nc.dram_tensor("out_0", (1, T, D), F32, kind="ExternalOutput").ap()
    two_blocks_kernel(nc, tensors, out)
    result = run(nc, [{f"in_{name}": v for name, v in arrays.items()}], core_ids=[0])
    return result.results[0]["out_0"]
```

```python
from contextlib import ExitStack
import math

import numpy as np

import concourse.bass as bass
from concourse import mybir

F32 = mybir.dt.float32
F32R = mybir.dt.float32r
BF16 = mybir.dt.bfloat16
I32 = mybir.dt.int32
ALU = mybir.AluOpType
ACT = mybir.ActivationFunctionType
AX = mybir.AxisListType.X

P = 128
T = 512
NT = T // P
D = 1024
KT = D // P
MEM = 256
HD = 64
FF_CHUNKS = 4
EPS = 1e-6
SUBLN_EPS = 1e-5
LAM_INIT = 0.8 - 0.6 * math.exp(-0.3 * 0)
FAR = -1.0e30
PT_STRIDE = 384
PT_COLS = PT_STRIDE * 3 + T
P_OFF = [0, 128, 384, 768]
P_COLS = 1280
BIAS_COLS = 384
LEVELS = [64, 32, 16, 8, 4, 2, 1]

C1 = {"qa": 0, "ka": 512, "va": 1024, "fa": 1536, "za": 1544, "qb": 2056, "kb": 2568, "vb": 3080, "zb": 3592,
      "gA": 4104, "gB": 5128}
C2 = {"qa": 0, "ka": 512, "va": 1024, "qg": 1536, "kg": 1792, "vg": 2048, "glr": 2560, "rg": 2576}


class Plan:

    def __init__(self):
        self.units, self.groups = {}, {}
        self.unit_name, self.unit_last_step = [], []
        self.group_step, self.kind, self.act_n, self.dve_n = [], [], [], []
        self.steps = 0

    def unit(self, name):
        of_phase = self.units.setdefault(name, [])
        self.unit_name.append((name, len(of_phase)))
        of_phase.append(len(self.unit_last_step))
        self.unit_last_step.append(self.steps)

    def group(self, name, kind, n=1):
        for _ in range(n):
            self.groups.setdefault(name, []).append(len(self.kind))
            self.kind.append(kind)
            self.act_n.append((self.act_n[-1] if self.act_n else 0) + ("A" in kind))
            self.dve_n.append((self.dve_n[-1] if self.dve_n else 0) + ("D" in kind))
            self.steps += 1
            self.group_step.append(self.steps)

    def t_units(self, name, kind, units=1, groups=2):
        for _ in range(units):
            self.group(name, kind, groups)
            self.unit(name)

    def m_units(self, name, kind, pairs=1, tiles=NT):
        for _ in range(pairs):
            self.steps += 1
            self.unit(name)
            self.group(name, kind, tiles)
            self.unit(name)

    def attention(self, name, kind, tiles, per_head, filling):
        names = [f for f in FILLING[filling] for _ in range(2)]
        for m in range(tiles + 5):
            k = fill_ends(filling, m)
            if k is not None:
                self.group(names[k], FILL_KIND[names[k]])
                if k % 2 == 1:
                    self.unit(names[k])
            if values_head(m) is not None:
                self.group(name, kind, per_head)


FILLING = {"fox": ["qa", "ka", "za", "za"], "diff": ["zb", "zb"], "moba": ["qa2", "ka2"], "x": ["xq", "xq"]}
FILL_SPAN = {"fox": 4, "diff": 4, "moba": 4, "x": 2}
FILL_KIND = {"qa": "AD", "ka": "AD", "za": "A", "zb": "A", "qa2": "AD", "ka2": "AD", "xq": "AD"}


def fill_ends(attention, m):
    k, rest = divmod(m + 1, FILL_SPAN[attention])
    return k - 1 if rest == 0 and 0 < k <= 2 * len(FILLING[attention]) else None


def values_head(m):
    return (m - 8) // 4 if m >= 8 and m % 4 == 0 else None


def make_plan():
    p = Plan()
    p.t_units("fa", "D", groups=1)
    p.t_units("qa", "AD")
    p.t_units("ka", "AD")
    p.m_units("va", "AD")
    p.attention("fox_pv", "AD", 32, 1, "fox")
    p.t_units("qb", "AD", 2)
    p.t_units("kb", "AD", 2)
    p.m_units("vb", "AD")
    p.attention("diff_pv", "A", 16, 1, "diff")
    p.group("subln", "A", 4)
    for _ in range(4):
        p.t_units("gates", "A", 2)
        p.t_units("gates", "D", groups=4)
    p.m_units("out1", "AD", 2)
    p.group("bias", "D")
    p.t_units("glr", "A", groups=1)
    p.t_units("qg", "A")
    p.group("gup", "D", 2)
    p.t_units("kg", "A")
    p.m_units("vg", "A")
    p.t_units("rg", "A", 2)
    p.group("levels", "D", 4 * (len(LEVELS) + 1))
    p.group("cross", "A", 8)
    p.group("gla_pv", "A", 4)
    p.group("gnorm", "A", 4)
    p.t_units("qa2", "AD")
    p.t_units("ka2", "AD")
    p.m_units("va2", "AD")
    p.attention("moba_pv", "AD", 32, 1, "moba")
    p.m_units("out2", "D", 2)
    p.t_units("kx", "AD", 4)
    p.m_units("vx", "AD", 2, tiles=2)
    p.t_units("xq", "AD", 2)
    p.attention("x_pv", "AD", 16, 2, "x")
    p.m_units("xo", "D", 2)
    for _ in range(FF_CHUNKS):
        p.t_units("mlp", "AD", 4)
        p.m_units("mlp", "D", 2)
    return p


PLAN = make_plan()
S0 = {"fox": 0, "diff": 32, "moba": 64, "x": 96}
R0 = {"norm1": 0, "fox": 8, "diff": 40, "mix": 56, "moba": 64, "mem": 96, "nx": 100, "x": 108, "nmlp": 124}
H0 = {"norm1": 0, "mix": 4, "mem": 8, "nx": 10, "nmlp": 14}
Q0 = {"norm1": 0, "mix": 4, "mem": 8, "nx": 10, "nmlp": 14, "final": 18}
V0 = {"fox": 0, "diff": 32, "moba": 48, "x": 80}
N0 = {"norm1": 0, "post": 4, "mix": 8, "mem": 12, "nx": 14, "nmlp": 18, "final": 22}


def shape_constants():
    half = HD // 2
    inv_freq = np.float32(10000.0) ** (-np.arange(0, HD, 2, dtype=np.float32) / np.float32(HD))
    angle = (np.arange(T, dtype=np.float32)[None, :] * inv_freq.astype(np.float32)[:, None]).astype(np.float64)
    rope_cos = np.tile(np.cos(angle), (P // half, 1)).astype(np.float32)
    rope_sin = np.tile(np.concatenate([-np.sin(angle), np.sin(angle)]), (P // HD, 1)).astype(np.float32)
    dist = np.maximum(256 - np.arange(BIAS_COLS), 0)
    large = 16 + (np.log(np.maximum(dist, 1).astype(np.float32) / np.float32(16)) / np.float32(math.log(128 / 16))
                  * np.float32(16)).astype(np.int32)
    bucket = np.where(dist < 16, dist, np.minimum(large, 31))
    one_hot = (np.arange(32)[:, None] == bucket[None, :]).astype(np.float32)
    j, i = np.arange(P)[:, None], np.arange(P)[None, :]
    masks = [(j // (2 * s) == i // (2 * s)) & (j % (2 * s) < s) & (i % (2 * s) >= s) for s in LEVELS] + [j == i]
    level_masks = np.stack(masks, axis=1).astype(np.int32)
    return {"rope_cos": rope_cos, "rope_sin": rope_sin, "bucket_one_hot": one_hot, "level_masks": level_masks}


class Offsets:

    def __init__(self, unit=0, step=0, act=0, dve=0):
        self.unit, self.step, self.act, self.dve = unit, step, act, dve


HERE = Offsets()


def gate_offsets(i):
    return Offsets(unit=i * 6, step=i * 16, act=i * 8, dve=i * 8)


def mlp_offsets(i):
    return Offsets(unit=i * 8, step=i * 18, act=i * 8, dve=i * 16)


def two_blocks_kernel(nc, a, out):
    w_in = a["w_in"][0]
    w_in_2 = a["w_in_2"][0]
    w_branch = a["w_branch"].rearrange("l b w d -> (l b w) d")
    w_out = a["w_out"][0]
    w_out_2 = a["w_out_2"][0]
    w_xq, w_xkv, w_xo = a["w_xq_2"][0], a["w_xkv_2"][0], a["w_xo_2"][0]
    w_up, w_down = a["w_up_2"][0], a["w_down_2"][0]
    x_in = a["x"].rearrange("b (t p) d -> p (b t) d", p=P)
    mem_in = a["mem_2"].rearrange("b (t p) d -> p (b t) d", p=P)
    x_out = out.rearrange("b (t p) d -> p (b t) d", p=P)
    x1_dram = a["x1_dram"].rearrange("(t p) d -> p t d", p=P)
    bias_dram = a["bias_dram"]
    G, K_, ST, AN, DN = PLAN.groups, PLAN.kind, PLAN.group_step, PLAN.act_n, PLAN.dve_n
    U = PLAN.units

    with ExitStack() as ctx:
        def region(*sets):
            made, size = {}, 0
            for bufs in sets:
                with ExitStack() as one:
                    used = 0
                    for name, shape, dt in bufs:
                        made[name] = one.enter_context(nc.sbuf_tensor(name, shape, dt))
                        used += math.prod(shape[1:]) * {F32: 4, F32R: 4, BF16: 2, I32: 4}[dt]
                    size = max(size, used)
            ctx.enter_context(nc.sbuf_tensor(f"region_of_{sets[0][0][0]}", [P, (size + 31) // 32 * 8], F32))
            return made

        def sb(name, shape, dt):
            return ctx.enter_context(nc.sbuf_tensor(name, shape, dt))

        def sem(name):
            return ctx.enter_context(nc.semaphore(name))

        w_raw = [sb(f"w_raw{i}", [P, 2048], F32) for i in range(2)]
        w_hi = [sb(f"w_hi{i}", [P, 2048], F32R) for i in range(2)]
        w_lo = [sb(f"w_lo{i}", [P, 2048], F32R) for i in range(2)]
        B = {}
        act8 = [P, KT, T]
        B["h_hi"], B["h_lo"] = sb("h_hi", act8, F32R), sb("h_lo", act8, F32R)
        B |= region(
            [("q_st", act8, F32R), ("k_hh", act8, F32R), ("k_lo", [P, 4, T], F32R),
             ("v_hl", [P, NT, 2 * T], F32R), ("z_b", [P, 4, T], F32)],
            [("y_hi", act8, F32R), ("y_lo", act8, F32R), ("m_hi", act8, F32R), ("m_lo", act8, F32R)],
            [("g_q", [P, 2, T], F32), ("g_k", [P, 2, T], F32), ("g_b", [P, 2, T], F32), ("g_d", [P, 2, 2, T], F32),
             ("g_z", [P, 2, 2, T], F32), ("g_qe", [P, 2, T], F32), ("g_kd", [P, 2, T], F32),
             ("g_kx", [P, 2, 3, P], F32), ("g_v", [P, NT, T], F32), ("g_keep", [P, T], F32),
             ("g_mask", [P, len(LEVELS) + 1, P], I32), ("g_up", [P, 256], F32), ("g_lr", [P, T], F32),
             ("g_x", [P, 2, T], F32), ("beta", [P, BIAS_COLS], F32), ("one_hot", [P, BIAS_COLS], F32)],
            [("xq_hi", act8, F32R), ("xq_lo", act8, F32R), ("xk_hi", [P, KT, MEM], F32R),
             ("xk_lo", [P, KT, MEM], F32R), ("xv_hi", [P, 2, D], F32R), ("xv_lo", [P, 2, D], F32R)],
            [("u_hi", act8, F32R), ("u_lo", act8, F32R)])
        small = [P, T]
        B |= region(
            [("pt_hi", [P, 2, PT_COLS], F32R), ("pt_lo", [P, 2, PT_COLS], F32R), ("p0", [P, P_COLS], F32),
             ("px", [P, P_COLS + 2 * T], F32)],
            [("x_m", [P, NT, D], F32), ("h_m", [P, 2, D], F32), ("y_m", [P, NT, D], F32)],
            [("rope_c", small, F32), ("rope_s", small, F32), ("t_a", [P, 2, T], F32), ("t_b", [P, 2, T], F32),
             ("t_c", [P, 2, T], F32), ("t_sq", [P, 2, T], F32), ("t_r", [P, 2, T], F32), ("t_g", [P, 4, T], F32)],
            [("g_a", [P, 4, PT_COLS], F32)],
            [("h_m2", [P, 2, D], F32), ("gain2", [P, 2, D], F32), ("junk2", [P, D], BF16),
             ("mem_hi", [P, KT, MEM], F32R), ("mem_lo", [P, KT, MEM], F32R)],
            [("pad_x", [P, 4608], F32), ("xpt_hi", [P, 2, 2 * T], F32R), ("xpt_lo", [P, 2, 2 * T], F32R),
             ("xp", [P, NT, MEM], F32)],
            [("pad_f", [P, 4608], F32), ("relu", [P, 2, T], F32), ("u_f", [P, 2, T], F32)])
        B |= region(
            [("y_0", [P, NT, T], F32), ("y_1", [P, NT, T], F32)],
            [("gain", [P, 2, D], F32), ("junk", [P, D], BF16), ("lam_v", [P, 4, HD], F32)],
            [("x_res", [P, NT, D], F32)])
        ident = sb("ident", [P, P], F32)
        flip = sb("flip", [P, P], F32)
        ones = sb("ones", [P, P], F32)
        ident_b = sb("ident_b", [P, P], BF16)
        future_b = sb("future_b", [P, P], BF16)
        pick = sb("pick", [P, 8], F32R)
        c_row = sb("c_row", [P, T], F32R)
        b_forget = sb("b_forget", [P, 1], F32)
        g_subln = sb("g_subln", [P, 1], F32)
        b_gate = sb("b_gate", [P, 2], F32)
        g_gain = sb("g_gain", [P, 1], F32)
        rp_table = sb("rp_table", [P, 8], F32)
        lam_d = sb("lam_d", [P, 2], F32)
        lam_e = sb("lam_e", [P, 2], F32)
        neg_lam = sb("neg_lam", [P, 1], F32)
        minus_half = sb("minus_half", [P, 1], F32)
        eps_n = sb("eps_n", [P, 2], F32)
        sumsq = sb("sumsq", [P, 26, 2], F32)
        var = sb("var", [P, 26], F32)
        rstd = sb("rstd", [P, 26], F32)
        neg_max = sb("neg_max", [P, 112], F32)
        denom = sb("denom", [P, 112], F32)
        rden = sb("rden", [P, 112], F32)
        g_tail = sb("g_tail", [P, 2, NT], F32)

        lin = ctx.enter_context(nc.psum_tensor("lin", [P, 4, T], F32))
        sc = ctx.enter_context(nc.psum_tensor("sc", [P, 2, T], F32))
        tr = ctx.enter_context(nc.psum_tensor("tr", [P, 2, T], F32))

        w_loaded = [sem(f"w_loaded{i}") for i in range(2)]
        w_slot_free = sem("w_slot_free")
        w_claimed = sem("w_claimed")
        w_split = sem("w_split")
        lin_step = sem("lin_step")
        act_evac = sem("act_evac")
        dve_evac = sem("dve_evac")
        consts_made = sem("consts_made")
        small_in = sem("small_in")
        x_in_s = [sem(f"x_in{t}") for t in range(NT)]
        sq_done = sem("sq_done")
        var_done = sem("var_done")
        rstd_done = sem("rstd_done")
        h_ready = sem("h_ready")
        tr_done = sem("tr_done")
        tr_hi = sem("tr_hi")
        tr_lo = sem("tr_lo")
        s_done = sem("s_done")
        s_max = sem("s_max")
        s_exp = sem("s_exp")
        s_rec = sem("s_rec")
        s_norm = sem("s_norm")
        pd_done = sem("pd_done")
        y_norm = sem("y_norm")
        dve_self = sem("dve_self")
        act_self = sem("act_self")
        pool_self = sem("pool_self")
        small_in2 = sem("small_in2")
        gain_in = [sem(f"gain_in{i}") for i in range(6)]
        lam_exp = sem("lam_exp")
        lam_ready = sem("lam_ready")
        fa_ln = sem("fa_ln")
        c_ready = sem("c_ready")
        za_silu = sem("za_silu")
        zb_silu = sem("zb_silu")
        ya_gated = sem("ya_gated")
        yb_gated = sem("yb_gated")
        rope_in = sem("rope_in")
        rot_mul = sem("rot_mul")
        rope_done = sem("rope_done")
        rope_hi = sem("rope_hi")
        rope_lo = sem("rope_lo")
        sq_t = sem("sq_t")
        y_hi_s = sem("y_hi_s")
        y_lo_s = sem("y_lo_s")
        mg_sum = sem("mg_sum")
        mg_hi = sem("mg_hi")
        mg_lo = sem("mg_lo")
        x_again = sem("x_again")
        x1_ready = sem("x1_ready")
        x1_parked = sem("x1_parked")
        x1_back = sem("x1_back")
        gla_in = sem("gla_in")
        gla_const = sem("gla_const")
        beta_ready = sem("beta_ready")
        beta_out = sem("beta_out")
        bias_in = sem("bias_in")
        gla_ln = sem("gla_ln")
        gd_done = sem("gd_done")
        ge_done = sem("ge_done")
        gz_done = sem("gz_done")
        mem_in_s = sem("mem_in_s")
        u_sum = sem("u_sum")
        u_hi_s = sem("u_hi_s")
        u_lo_s = sem("u_lo_s")
        final_ready = sem("final_ready")
        out_done = sem("out_done")

        def as_f32(ap):
            return ap.bitcast(F32)

        def blocks(buf, slot, i):
            base = buf[:, slot, P * i:P * i + P]
            return bass.AP(base.tensor, base.offset, [list(base.ap[0]), [PT_STRIDE, i + 1], [1, P]])

        def diagonal(buf, slot):
            return buf[:, slot, :].rearrange("p (a b) -> p a b", b=P)[:, 0:13:4, :]

        bias_tiles = B["px"][:, 0:8 * 256].rearrange("p (h c) -> p h c", h=8)
        fox_tmp = B["px"][:, P_COLS:P_COLS + 2 * T].rearrange("p (s t) -> p s t", s=2)

        def t_source(w, c0, width=256):
            return w[:, c0:c0 + width].rearrange("(k p) n -> p k n", p=P)

        def m_source(w, c0, n):
            r, c = T * (n % 2), c0 + T * (n // 2)
            return w[r:r + T, c:c + T].rearrange("(k p) n -> p k n", p=P)

        def source(name, n):
            if name in ("fa", "glr"):
                return t_source(*((w_in, C1[name]) if name == "fa" else (w_in_2, C2[name])), P)
            if name in ("qa", "ka", "za", "qb", "kb", "zb"):
                return t_source(w_in, C1[name] + 256 * n)
            if name in ("qg", "kg", "rg", "qa2", "ka2"):
                return t_source(w_in_2, C2[name[0:2]] + 256 * n)
            if name in ("kx", "xq"):
                return t_source(w_xkv if name == "kx" else w_xq, 256 * n)
            w, c0 = {"va": (w_in, C1["va"]), "vb": (w_in, C1["vb"]), "out1": (w_out, 0), "vg": (w_in_2, C2["vg"]),
                     "va2": (w_in_2, C2["va"]), "out2": (w_out_2, 0), "vx": (w_xkv, D), "xo": (w_xo, 0)}[name]
            return m_source(w, c0, n)

        assert U["mlp"][0] % 2 == 0 and U["gates"][0] % 2 == 1

        block = ctx.enter_context(nc.Block())

        @block.sync
        def _(sp):
            def load_unit(u, src, off=None):
                if u >= 2:
                    sp.wait_ge(w_split, 2 * (u - 1) + 2 * (off or HERE).unit)
                if off is not None:
                    sp.sem_inc(w_slot_free, 1)
                k, n = src.shape[1], src.shape[2]
                dst = w_raw[u % 2][:, 0:k * n].rearrange("p (k n) -> p k n", k=k)
                sp.dma_start(dst, src).then_inc(w_loaded[u % 2], 16)

            for t in range(NT):
                sp.dma_start(B["x_m"][:, t, :], x_in[:, t, :]).then_inc(x_in_s[t], 16)
            for u in range(U["gates"][0]):
                load_unit(u, source(*PLAN.unit_name[u]))
            with sp.Fori(0, 2) as i:
                off = gate_offsets(i)
                for c in range(2):
                    for n, w, c0 in ((0, w_in, C1["gA"]), (1, w_in, C1["gB"]), (2, w_branch, 0)):
                        cols = bass.ds(i * 512 + (c0 + 256 * c), 256)
                        load_unit(U["gates"][3 * c + n], w[:, cols].rearrange("(k p) n -> p k n", p=P), off)
            for u in range(U["out1"][0], U["mlp"][0]):
                load_unit(u, source(*PLAN.unit_name[u]))
            with sp.Fori(0, FF_CHUNKS) as i:
                off = mlp_offsets(i)
                for c in range(4):
                    cols = bass.ds(i * D + 256 * c, 256)
                    load_unit(U["mlp"][c], w_up[:, cols].rearrange("(k p) n -> p k n", p=P), off)
                for j in range(2):
                    for kh in range(2):
                        rows = bass.ds(i * D + T * kh, T)
                        src = w_down[rows, T * j:T * j + T].rearrange("(k p) n -> p k n", p=P)
                        load_unit(U["mlp"][4 + 2 * j + kh], src, off)
            for t in range(NT):
                sp.wait_ge(final_ready, t + 1)
                sp.dma_start(x_out[:, t, :], B["x_res"][:, t, :]).then_inc(out_done, 16)
            sp.wait_ge(out_done, 16 * NT)
            sp.wait_ge(x1_parked, 16 * NT)
            sp.wait_ge(beta_out, 16)

        @block.gpsimd
        def _(pool):
            own = [0]

            def link(ins):
                own[0] += 1
                ins.then_inc(pool_self, 1)
                pool.wait_ge(pool_self, own[0])

            def unit_cols(u):
                return KT * P if PLAN.unit_name[u][0] in ("fa", "glr") else 2048

            def split_piece(u, n):
                if n == 0:
                    pool.wait_ge(w_loaded[u % 2], 16 * (u // 2 + 1))
                    pool.wait_ge(lin_step, PLAN.unit_last_step[u - 2])
                if n == 4:
                    pool.wait_ge(w_split, 2 * u + 1)
                c = slice(T * (n % 4), T * (n % 4) + T)
                raw, hi, lo = (b[u % 2][:, c] for b in (w_raw, w_hi, w_lo))
                if n < 4:
                    ins = pool.tensor_scalar(hi, raw, 1.0, 1.0, ALU.mult, ALU.mult)
                else:
                    ins = pool.tensor_tensor(lo, raw, as_f32(hi), ALU.subtract)
                if n % 4 == 3:
                    ins.then_inc(w_split, 1)

            def split_between(first, tiles, pieces, norm):
                for m in range(tiles):
                    norm(m)
                    unit, k = divmod(m, len(pieces))
                    for n in range(sum(pieces[:k]), sum(pieces[:k + 1])):
                        split_piece(first + unit, n)

            def split_unit(u, off=None, left=None):
                o = off or HERE
                pool.wait_ge(w_loaded[u % 2], 16 * (u // 2 + 1) + o.unit * 8)
                if u >= 2:
                    pool.wait_ge(lin_step, (left or PLAN.unit_last_step[u - 2]) + o.step)
                if off is not None:
                    pool.sem_inc(w_claimed, 1)
                raw, hi, lo = (b[u % 2][:, 0:unit_cols(u)] for b in (w_raw, w_hi, w_lo))
                pool.tensor_scalar(hi, raw, 1.0, 1.0, ALU.mult, ALU.mult).then_inc(w_split, 1)
                pool.wait_ge(w_split, 2 * u + 1 + o.unit * 2)
                pool.tensor_tensor(lo, raw, as_f32(hi), ALU.subtract).then_inc(w_split, 1)

            def root(n):
                pool.wait_ge(var_done, n + 1)
                pool.tensor_tensor(rstd[:, n:n + 1], var[:, n:n + 1], minus_half[:, :], ALU.pow)\
                    .then_inc(rstd_done, 1)

            def normalise(v, s, p):
                pool.wait_ge(s_rec, v + 1)
                pool.tensor_scalar(p, p, rden[:, s:s + 1], 1.0, ALU.mult, ALU.mult).then_inc(s_norm, 1)

            for buf, value in ((ident[:, :], 0.0), (flip[:, :], 0.0), (ones[:, :], 1.0), (ident_b[:, :], 0.0),
                               (future_b[:, :], 0.0), (as_f32(c_row[:, :]), 0.0), (minus_half[:, :], -0.5),
                               (eps_n[:, 0:1], SUBLN_EPS), (eps_n[:, 1:2], EPS)):
                link(pool.memset(buf, value))
            for buf, sign, base in ((ident, -1, 0), (flip, 1, 1 - P), (ident_b, -1, 0)):
                link(pool.affine_select(out=buf[:, :], in_=buf[:, :], compare_op=ALU.not_equal, fill=1.0,
                                        base=base, pattern=[[sign, P]], channel_multiplier=1))
            pool.affine_select(out=future_b[:, :], in_=future_b[:, :], compare_op=ALU.is_ge, fill=FAR, base=0,
                               pattern=[[-1, P]], channel_multiplier=1).then_inc(consts_made, 1)

            split_unit(0)
            for t in range(NT):
                root(N0["norm1"] + t)
            for u in range(1, U["qa"][1] + 1):
                split_unit(u)

            def causal_norm(name):
                def f(m):
                    i, n = m % 4, P * (m % 4 + 1)
                    normalise(V0[name] + m, S0[name] + m, B["p0"][:, P_OFF[i]:P_OFF[i] + n])
                return f

            split_between(U["ka"][1], 32, (2, 2, 1, 1, 1, 1, 0, 0), causal_norm("fox"))
            split_unit(U["qb"][1])
            for c in range(8):
                pool.wait_ge(act_evac, AN[G["qb"][0] + c])
                if c == 0:
                    pool.wait_ge(rope_in, 32)
                t_b = B["t_b"][:, c % 2, :]
                pool.tensor_tensor(t_b, t_b, B["rope_s"][:, :], ALU.mult).then_inc(rot_mul, 1)
                if c % 2 == 1:
                    split_unit(U["kb"][0] + c // 2)
            split_unit(U["zb"][0])

            def diff_norm(w):
                i, n = w % 4, P * (w % 4 + 1)
                normalise(V0["diff"] + w, S0["diff"] + 2 * w, B["p0"][:, P_OFF[i]:P_OFF[i] + n])

            split_between(U["zb"][1], 16, (2, 2, 1, 1, 1, 1, 0, 0), diff_norm)
            with pool.Fori(0, 2) as it:
                for c in range(1, 7):
                    split_unit(U["gates"][c], off=gate_offsets(it),
                               left=ST[G["subln"][3]] if c == 1 else None)
            for u in range(U["out1"][1], U["glr"][0] + 1):
                split_unit(u)
            for t in range(NT):
                root(N0["post"] + t)
            for t in range(NT):
                root(N0["mix"] + t)
            split_unit(U["glr"][0] + 1)
            pool.wait_ge(lin_step, ST[G["out1"][7]])
            link(pool.memset(B["g_keep"][:, :], 1.0))
            link(pool.memset(B["g_keep"][:, 0:T:P], 0.0))
            pool.wait_ge(x1_parked, 16 * NT)
            pool.wait_ge(tr_done, R0["mix"] + 8)
            for h in range(4):
                ins = pool.memset(diagonal(B["g_a"], h), 0.0)
            ins.then_inc(gla_const, 1)
            for u in range(U["glr"][0] + 2, U["qa2"][1] + 1):
                split_unit(u)
            split_between(U["ka2"][1], 24, (2, 2, 1, 1, 1, 1, 0, 0), causal_norm("moba"))
            for m in range(24, 32):
                causal_norm("moba")(m)
            for t in range(2):
                root(N0["mem"] + t)
            for u in range(U["out2"][2], U["kx"][2]):
                split_unit(u)
            for t in range(NT):
                root(N0["nx"] + t)
            for u in range(U["kx"][2], U["xq"][2] + 1):
                split_unit(u)

            def x_norm(m):
                normalise(V0["x"] + m, S0["x"] + m, B["xp"][:, m % 4, :])

            split_between(U["xq"][3], 12, (3, 3, 2, 0), x_norm)
            for m in range(12, 16):
                x_norm(m)
            for u in range(U["xo"][2], U["mlp"][1]):
                split_unit(u)
            for t in range(NT):
                root(N0["nmlp"] + t)
            split_unit(U["mlp"][1])
            with pool.Fori(0, FF_CHUNKS - 1) as it:
                for c in range(2, 10):
                    split_unit(U["mlp"][c], off=mlp_offsets(it))
            for c in range(2, 8):
                split_unit(U["mlp"][8 * (FF_CHUNKS - 1) + c])
            for t in range(NT):
                root(N0["final"] + t)

        @block.tensor
        def _(pe):
            def bank(g, cols=T):
                return lin[:, g % 4, 0:cols]

            def claim(g, off=HERE):
                k = g - 4
                if k < 0:
                    return
                if "D" in K_[k]:
                    pe.wait_ge(dve_evac, DN[k] + off.dve)
                else:
                    pe.wait_ge(act_evac, AN[k] + off.act)

            def three(o, lh, ll, rh, rl, start, stop):
                pe.matmul(o, lh, rh, start=start, stop=False)
                pe.matmul(o, lh, rl, start=False, stop=False)
                return pe.matmul(o, ll, rh, start=False, stop=stop)

            def t_product(name, n, k0, k1, rh, rl, off=HERE, per_unit=2, cols=T):
                g, u, c = G[name][n], U[name][n // per_unit], slice(P * (n % per_unit), P * (n % per_unit) + P)
                if k0 == 0:
                    claim(g, off)
                    pe.wait_ge(w_split, 2 * u + 2 + off.unit * 2)
                wh, wl = (b[u % 2][:, 0:KT * P * per_unit].rearrange("p (k n) -> p k n", k=KT) for b in (w_hi, w_lo))
                for k in range(k0, k1):
                    mm = three(bank(g, cols), wh[:, k, c], wl[:, k, c], rh[:, k, 0:cols], rl[:, k, 0:cols],
                               k == 0, k == KT - 1)
                if k1 == KT:
                    mm.then_inc(lin_step, 1)

            def gate_group(unit, group, n, off):
                g, u, c = G["gates"][group], U["gates"][unit], slice(P * n, P * n + P)
                if group < 4:
                    pe.wait_ge(act_evac, AN[g - 4] + off.act)
                    pe.wait_ge(dve_evac, DN[G["subln"][3]] - 3 + group + off.dve)
                else:
                    claim(g, off)
                pe.wait_ge(w_split, 2 * u + 2 + off.unit * 2)
                wh, wl = (b[u % 2][:, :].rearrange("p (k n) -> p k n", k=KT) for b in (w_hi, w_lo))
                for k in range(KT):
                    mm = three(bank(g), wh[:, k, c], wl[:, k, c], hh[:, k, :], hl[:, k, :], k == 0, k == KT - 1)
                mm.then_inc(lin_step, 1)

            def t_groups(name, n0, n1, rh, rl, **kw):
                for n in range(n0, n1):
                    t_product(name, n, 0, KT, rh, rl, **kw)

            def branch_unit(u, g, off):
                pe.wait_ge(w_split, 2 * u + 2 + off.unit * 2)
                wh, wl = (b[u % 2][:, :].rearrange("p (k n) -> p k n", k=KT) for b in (w_hi, w_lo))
                for n in range(2):
                    for br in range(2):
                        q = g + 2 * n + br
                        claim(q, off)
                        for k in range(4 * br, 4 * br + 4):
                            c = slice(P * n, P * n + P)
                            mm = three(bank(q), wh[:, k, c], wl[:, k, c], B["y_hi"][:, k, :], B["y_lo"][:, k, :],
                                       k % 4 == 0, k % 4 == 3)
                        mm.then_inc(lin_step, 1)

            def m_pair(name, u0, g0, lh, ll, off=HERE, tiles=NT, ready=lambda kh: None):
                u, g = U[name][u0], G[name][g0]
                for kh in range(2):
                    ready(kh)
                    pe.wait_ge(w_split, 2 * (u + kh) + 2 + off.unit * 2)
                    wh, wl = (b[(u + kh) % 2][:, :].rearrange("p (k n) -> p k n", k=4) for b in (w_hi, w_lo))
                    for t in range(tiles):
                        if kh == 0:
                            claim(g + t, off)
                        for k in range(4):
                            c = slice(P * t, P * t + P)
                            mm = three(bank(g + t), lh[:, 4 * kh + k, c], ll[:, 4 * kh + k, c], wh[:, k, :],
                                       wl[:, k, :], kh == 0 and k == 0, kh == 1 and k == 3)
                        if kh == 1 or t == tiles - 1:
                            mm.then_inc(lin_step, 1)

            def turn_tile(name, t, src):
                pe.wait_ge(h_ready, H0[name] + t + 1)
                for half in range(2):
                    r = R0[name] + 2 * t + half
                    if r >= 2:
                        pe.wait_ge(tr_lo, r - 1)
                    for b in range(4):
                        c = P * (4 * half + b)
                        mm = pe.transpose(tr[:, r % 2, P * b:P * b + P], src[:, c:c + P], ident[:, :])
                    mm.then_inc(tr_done, 1)

            def turn_probs(r, src, n):
                if r >= 2:
                    pe.wait_ge(tr_lo, r - 1)
                for j in range(n):
                    mm = pe.transpose(tr[:, r % 2, P * j:P * j + P], src(j), ident[:, :])
                mm.then_inc(tr_done, 1)

            def stacked_scores(s, h, i, extra=None):
                if s >= 2:
                    pe.wait_ge(s_exp, s - 1)
                n = P * (i + 1)
                o = sc[:, s % 2, 0:n]
                q = B["q_st"][:, h, P * i:P * i + P]
                rows = slice(64 * (h % 2), 64 * (h % 2) + 64)
                pe.matmul(o, q, B["k_hh"][:, h, 0:n], start=True, stop=False)
                extra(o, n)
                pe.matmul(o, q[rows], B["k_lo"][rows, h // 2, 0:n], start=False, stop=True).then_inc(s_done, 1)

            def heads_ready(q, k, h):
                pe.wait_ge(dve_evac, max(DN[G[q][h // 2]], DN[G[k][h // 2]]))

            def mask(o, i):
                pe.matmul(o[:, P * i:P * i + P], ident_b[:, :], future_b[:, :], start=False, stop=False)

            def p_tile(i, j):
                c = P_OFF[i] + P * j
                return B["p0"][:, c:c + P]

            def stacked_values(g, g_v, r, h):
                claim(g)
                pe.wait_ge(dve_evac, DN[g_v])
                pe.wait_ge(tr_lo, r)
                for j in range(NT):
                    c = slice(T * j, T * j + T - P * j)
                    v = B["v_hl"][:, j, P * h:P * h + P]
                    o = lin[:, g % 4, P * j:T]
                    pe.matmul(o, v, B["pt_hi"][:, h % 2, c], start=(j == 0), stop=False)
                    mm = pe.matmul(o, v, B["pt_lo"][:, h % 2, c], start=False, stop=(j == NT - 1))
                mm.then_inc(lin_step, 1)

            def attention(name, tiles, scores, turn, values, first):
                span = FILL_SPAN[name]
                for m in range(tiles + 5):
                    if m < tiles:
                        scores(m)
                    if 0 <= m - 3 < tiles:
                        turn(m - 3)
                    if m // span < 2 * len(first):
                        n0, k = divmod(m // span, 2), m % span
                        t_product(FILLING[name][n0[0]], first[n0[0]] + n0[1], KT * k // span, KT * (k + 1) // span,
                                  hh, hl)
                    if values_head(m) is not None:
                        values(values_head(m))

            pe.wait_ge(consts_made, 1)
            for t in range(NT):
                turn_tile("norm1", t, B["h_m"][:, t % 2, :])
            pe.wait_ge(tr_lo, R0["norm1"] + 8)
            hh, hl = B["h_hi"], B["h_lo"]
            t_groups("fa", 0, 1, hh, hl, per_unit=1)
            for name in ("qa", "ka"):
                t_groups(name, 0, 2, hh, hl)
            m_pair("va", 0, 0, hh, hl)
            pe.wait_ge(c_ready, 1)

            def fox_scores(m):
                h, i = m // 4, m % 4
                if i == 0:
                    heads_ready("qa", "ka", h)

                def extra(o, n):
                    mask(o, i)
                    pe.matmul(o, pick[:, h:h + 1].to_broadcast([P, P]), c_row[:, 0:n], start=False, stop=False)

                stacked_scores(S0["fox"] + m, h, i, extra)

            def fox_turn(m):
                pe.wait_ge(s_norm, V0["fox"] + m + 1)
                turn_probs(R0["fox"] + m, lambda j: p_tile(m % 4, j), m % 4 + 1)

            attention("fox", 32, fox_scores, fox_turn,
                      lambda h: stacked_values(G["fox_pv"][h], G["va"][3], R0["fox"] + 4 * h + 4, h), [2, 2, 0, 2])
            for name in ("qb", "kb"):
                t_groups(name, 0, 4, hh, hl)
            m_pair("vb", 0, 0, hh, hl)

            pe.wait_ge(rope_lo, 8)
            pe.wait_ge(dve_evac, DN[G["vb"][3]])

            def diff_scores(w):
                h, i = w // 4, w % 4
                for m in range(2):
                    stacked_scores(S0["diff"] + 2 * w + m, 2 * h + m, i, lambda o, n: mask(o, i))

            def diff_turn(w):
                pe.wait_ge(pd_done, w + 1)
                turn_probs(R0["diff"] + w, lambda j: p_tile(w % 4, j), w % 4 + 1)

            def diff_values(h):
                g = G["diff_pv"][h]
                claim(g)
                pe.wait_ge(tr_lo, R0["diff"] + 4 * h + 4)
                for j in range(NT):
                    c = slice(T * j, T * j + T - P * j)
                    v = B["v_hl"][:, j, :]
                    mm = three(lin[:, g % 4, P * j:T], v[:, P * h:P * h + P], v[:, T + P * h:T + P * h + P],
                               B["pt_hi"][:, h % 2, c], B["pt_lo"][:, h % 2, c], j == 0, j == NT - 1)
                mm.then_inc(lin_step, 1)

            attention("diff", 16, diff_scores, diff_turn, diff_values, [0, 2])
            for h in range(4):
                g = G["subln"][h]
                claim(g)
                pe.wait_ge(sq_t, h + 1)
                pe.matmul(bank(g), ones[:, :], B["t_sq"][:, h % 2, :], start=True, stop=True).then_inc(lin_step, 1)
            with pe.Fori(0, 2) as it:
                off = gate_offsets(it)
                for c in range(2):
                    for n in range(4):
                        gate_group(3 * c + n // 2, 8 * c + n, n % 2, off)
                    pe.wait_ge(y_lo_s, 8)
                    branch_unit(U["gates"][3 * c + 2], G["gates"][8 * c + 4], off)
            for j in range(2):
                m_pair("out1", 2 * j, 4 * j, B["m_hi"], B["m_lo"], ready=lambda kh: pe.wait_ge(mg_lo, 4 * kh + 4))

            g = G["bias"][0]
            claim(g)
            pe.wait_ge(gla_in, 48)
            pe.wait_ge(small_in, 16 * 5)
            pe.matmul(lin[0:8, g % 4, 0:BIAS_COLS], rp_table[0:32, :], B["one_hot"][0:32, :], start=True, stop=True)\
                .then_inc(lin_step, 1)
            for t in range(NT):
                turn_tile("mix", t, B["h_m"][:, t % 2, :])
            pe.wait_ge(tr_lo, R0["mix"] + 8)
            t_groups("glr", 0, 1, hh, hl, per_unit=1)
            t_groups("qg", 0, 2, hh, hl)
            pe.wait_ge(act_evac, AN[G["glr"][0]])
            for dt in range(2):
                g = G["gup"][dt]
                claim(g)
                pe.matmul(bank(g), B["g_up"][0:16, P * dt:P * dt + P], B["g_lr"][0:16, :], start=True, stop=True)\
                    .then_inc(lin_step, 1)
            t_groups("kg", 0, 2, hh, hl)
            m_pair("vg", 0, 0, hh, hl)
            t_groups("rg", 0, 4, hh, hl)
            for lev in range(len(LEVELS) + 1):
                for h in range(4):
                    g = G["levels"][4 * lev + h]
                    rows = slice(HD * (h % 2), HD * (h % 2) + HD)
                    claim(g)
                    if lev < len(LEVELS):
                        pe.wait_ge(gz_done, lev + 1)
                        key = query = B["g_z"][rows, lev % 2, h // 2, :]
                    else:
                        key, query = B["g_k"][rows, h // 2, :], B["g_q"][rows, h // 2, :]
                    for t in range(NT):
                        c = slice(P * t, P * t + P)
                        mm = pe.matmul(lin[:, g % 4, c], key[:, c], query[:, c], start=True, stop=True)
                    mm.then_inc(lin_step, 1)
            pe.wait_ge(gz_done, len(LEVELS) + 1)
            for h in range(4):
                rows = slice(HD * (h % 2), HD * (h % 2) + HD)
                kd, kx, qe = B["g_kd"][rows, h // 2, :], B["g_kx"][rows, h // 2], B["g_qe"][rows, h // 2, :]
                own = [kd[:, P * j:P * j + P] for j in range(3)]
                for part, pairs in enumerate(([(own[0], 1), (kx[:, 0], 2), (kx[:, 1], 3)],
                                              [(own[1], 2), (kx[:, 2], 3), (own[2], 3)])):
                    g = G["cross"][2 * h + part]
                    claim(g)
                    for n, (key, i) in enumerate(pairs):
                        mm = pe.matmul(lin[:, g % 4, P * n:P * n + P], key, qe[:, P * i:P * i + P],
                                       start=True, stop=True)
                    mm.then_inc(lin_step, 1)
            for h in range(4):
                g = G["gla_pv"][h]
                claim(g)
                pe.wait_ge(act_evac, AN[G["cross"][2 * h + 1]])
                pe.wait_ge(dve_evac, DN[G["levels"][4 * len(LEVELS) + h]])
                for j in range(NT):
                    mm = pe.matmul(lin[:, g % 4, P * j:T], B["g_v"][:, j, P * h:P * h + P],
                                   B["g_a"][:, h, T * j:T * j + T - P * j], start=(j == 0), stop=(j == NT - 1))
                mm.then_inc(lin_step, 1)
            for h in range(4):
                g = G["gnorm"][h]
                claim(g)
                pe.wait_ge(sq_t, 4 + h + 1)
                pe.matmul(bank(g), ones[:, :], B["g_d"][:, 0, h % 2, :], start=True, stop=True).then_inc(lin_step, 1)
            for name in ("qa2", "ka2"):
                t_groups(name, 0, 2, hh, hl)
            m_pair("va2", 0, 0, hh, hl)

            pe.wait_ge(bias_in, 16)

            def moba_scores(m):
                h, i = m // 4, m % 4
                near = max(i - 1, 0)
                if i == 0:
                    heads_ready("qa2", "ka2", h)

                def extra(o, n):
                    pe.matmul(o[:, P * near:n], flip[:, :], bias_tiles[:, h, 256 - (n - P * near):256],
                              start=False, stop=False)

                stacked_scores(S0["moba"] + m, h, i, extra)

            def moba_turn(m):
                pe.wait_ge(s_norm, V0["moba"] + m + 1)
                turn_probs(R0["moba"] + m, lambda j: p_tile(m % 4, j), m % 4 + 1)

            attention("moba", 32, moba_scores, moba_turn,
                      lambda h: stacked_values(G["moba_pv"][h], G["va2"][3], R0["moba"] + 4 * h + 4, h), [2, 2])
            for j in range(2):
                m_pair("out2", 2 * j, 4 * j, B["y_hi"], B["y_lo"], ready=lambda kh: pe.wait_ge(y_lo_s, 4 * kh + 12))

            for t in range(2):
                turn_tile("mem", t, B["h_m2"][:, t, :])
            pe.wait_ge(tr_lo, R0["mem"] + 4)
            t_groups("kx", 0, 8, B["mem_hi"], B["mem_lo"], cols=MEM)
            for j in range(2):
                m_pair("vx", 2 * j, 2 * j, B["mem_hi"], B["mem_lo"], tiles=2)
            for t in range(NT):
                turn_tile("nx", t, B["h_m2"][:, t % 2, :])
            pe.wait_ge(tr_lo, R0["nx"] + 8)
            t_groups("xq", 0, 4, hh, hl)

            def x_scores(m):
                h, i = m // 4, m % 4
                s = S0["x"] + m
                if i == 0:
                    pe.wait_ge(dve_evac, DN[G["xq"][2 * h + 1]])
                pe.wait_ge(s_exp, s - 1)
                for kk in range(2):
                    f = 2 * h + kk
                    c = slice(P * i, P * i + P)
                    mm = three(sc[:, s % 2, 0:MEM], B["xq_hi"][:, f, c], B["xq_lo"][:, f, c], B["xk_hi"][:, f, :],
                               B["xk_lo"][:, f, :], kk == 0, kk == 1)
                mm.then_inc(s_done, 1)

            def x_turn(m):
                pe.wait_ge(s_norm, V0["x"] + m + 1)
                turn_probs(R0["x"] + m, lambda j: B["xp"][:, m % 4, P * j:P * j + P], 2)

            def x_values(h):
                pe.wait_ge(tr_lo, R0["x"] + 4 * h + 4)
                for dv in range(2):
                    g = G["x_pv"][2 * h + dv]
                    claim(g)
                    for j in range(2):
                        c = slice(256 * h + P * dv, 256 * h + P * dv + P)
                        k = slice(T * j, T * j + T)
                        mm = three(bank(g), B["xv_hi"][:, j, c], B["xv_lo"][:, j, c], B["xpt_hi"][:, h % 2, k],
                                   B["xpt_lo"][:, h % 2, k], j == 0, j == 1)
                    mm.then_inc(lin_step, 1)

            attention("x", 16, x_scores, x_turn, x_values, [4, 6])
            for j in range(2):
                m_pair("xo", 2 * j, 4 * j, hh, hl,
                       ready=lambda kh: pe.wait_ge(dve_evac, DN[G["x_pv"][4 * kh + 3]]))

            for t in range(NT):
                turn_tile("nmlp", t, B["h_m2"][:, t % 2, :])
            pe.wait_ge(tr_lo, R0["nmlp"] + 8)
            with pe.Fori(0, FF_CHUNKS) as it:
                off = mlp_offsets(it)
                t_groups("mlp", 0, 8, hh, hl, off=off)
                for j in range(2):
                    m_pair("mlp", 4 + 2 * j, 8 + 4 * j, B["u_hi"], B["u_lo"], off,
                           ready=lambda kh: pe.wait_ge(u_lo_s, it * 8 + (4 * kh + 4)))

        @block.scalar
        def _(act):
            own = [0]

            def link(ins):
                own[0] += 1
                ins.then_inc(act_self, 1)
                act.wait_ge(act_self, own[0])

            def step(g, off=HERE):
                act.wait_ge(lin_step, ST[g] + off.step)

            def bank(g, cols=T):
                return lin[:, g % 4, 0:cols]

            def after_vector(g, off=HERE):
                act.wait_ge(dve_evac, DN[g] + off.dve)

            def load(dst, src, s):
                act.dma_start(dst, src).then_inc(s, 16)

            def row(name):
                return a[name][0:1, :].partition_broadcast(P) if len(a[name].shape) == 2 else \
                    a[name].rearrange("(o d) -> o d", o=1).partition_broadcast(P)

            def column(name):
                return a[name].rearrange("l d -> d l")

            def square_sum(q, n, x, junk, half=0):
                if q > 0:
                    act.wait_ge(sq_done, q)
                act.activation(junk, x, ACT.Square, accum_out=sumsq[:, n, half:half + 1]).then_inc(sq_done, 1)

            def turned_hi(r, out):
                act.wait_ge(tr_done, r + 1)
                act.activation(out, tr[:, r % 2, :].rearrange("p (b c) -> p b c", b=4), ACT.Copy).then_inc(tr_hi, 1)

            def turned_tile_hi(name, t, buf):
                for half in range(2):
                    turned_hi(R0[name] + 2 * t + half, buf[:, 4 * half:4 * half + 4, P * t:P * t + P])

            def q_hi(x, c, scale):
                act.activation(B["q_st"][0:64, 2 * c, :], x[0:64], ACT.Copy, scale=scale)
                return act.activation(B["q_st"][64:128, 2 * c + 1, :], x[64:128], ACT.Copy, scale=scale)

            def k_hi(x, c):
                for head in range(2):
                    rows = slice(64 * head, 64 * head + 64)
                    for half in range(2):
                        ins = act.activation(B["k_hh"][64 * half:64 * half + 64, 2 * c + head, :], x[rows], ACT.Copy)
                return ins

            def exponentials(s, p, n):
                act.wait_ge(s_max, s + 1)
                act.activation(p, sc[:, s % 2, 0:n], ACT.Exp, bias=neg_max[:, s:s + 1],
                               accum_out=denom[:, s:s + 1]).then_inc(s_exp, 1)

            def probs_hi(r, m, g_pv):
                h, i = m // 4, m % 4
                act.wait_ge(tr_done, r + 1)
                if h >= 2:
                    step(g_pv[h - 2])
                act.activation(blocks(B["pt_hi"], h % 2, i),
                               tr[:, r % 2, 0:P * (i + 1)].rearrange("p (j c) -> p j c", c=P), ACT.Copy)\
                    .then_inc(tr_hi, 1)

            def attention(name, tiles, hi, exps, values, fill):
                for m in range(tiles + 6):
                    if 0 <= m - 4 < tiles:
                        hi(m - 4)
                    if m < tiles:
                        exps(m)
                    if m >= 1 and fill_ends(name, m - 1) is not None:
                        fill(fill_ends(name, m - 1))
                    if m >= 9 and m % 4 == 1:
                        values((m - 9) // 4)

            def lower_half(g, tmp):
                act.activation(tmp, lin[64:128, g % 4, :], ACT.Copy).then_inc(act_evac, 1)

            def soft_log(x, t1, t2, done):
                link(act.activation(t1, x, ACT.Abs))
                link(act.activation(t2, t1, ACT.Exp, scale=-1.0))
                act.activation(t1, t2, ACT.Ln, bias=ones[0:t1.shape[0], 0:1]).then_inc(done, 1)

            def copy_lin(g, out, scale=1.0):
                step(g)
                act.activation(out, bank(g), ACT.Copy, scale=scale).then_inc(act_evac, 1)

            def head_roots(g0, y, sq, root, eps, free):
                for h in range(4):
                    if h >= 2:
                        step(g0 + h - 2)
                    act.activation(sq[:, h % 2, :], y[:, h, :], ACT.Square).then_inc(sq_t, 1)
                for h in range(4):
                    step(g0 + h)
                    if h >= 2:
                        act.wait_ge(y_norm, free + h - 1)
                    act.activation(root[:, h % 2, :], bank(g0 + h), ACT.Sqrt, scale=1.0 / P, bias=eps)\
                        .then_inc(act_evac, 1)

            load(B["gain"][:, 0, :], row("g_pre"), gain_in[0])
            for n, name in enumerate(("lambda_q1", "lambda_k1", "lambda_q2", "lambda_k2")):
                load(B["lam_v"][:, n, :], row(name), small_in2)
            with nc.allow_non_contiguous_dma(reason="one column of a few hundred bytes each"):
                load(b_forget[0:8, :], column("b_forget"), small_in)
                load(g_subln[:, :], column("g_subln"), small_in)
                load(b_gate[:, :], a["b_gate_2"].rearrange("l (t p) -> p (l t)", p=P), small_in)
                load(g_gain[:, :], column("g_norm_2"), small_in)
            load(rp_table[0:32, :], a["rp_table_2"], small_in)

            act.wait_ge(consts_made, 1)
            for t in range(NT):
                act.wait_ge(x_in_s[t], 16)
                square_sum(Q0["norm1"] + t, N0["norm1"] + t, B["x_m"][:, t, :], B["junk"][:, :])
            act.wait_ge(lam_ready, 1)
            act.activation(lam_e[:, :], lam_d[:, :], ACT.Exp).then_inc(lam_exp, 1)
            for t in range(NT):
                turned_tile_hi("norm1", t, B["h_hi"])
            act.wait_ge(dve_evac, DN[G["fa"][0]])
            soft_log(B["y_0"][0:8, 0, :], B["y_0"][0:8, 1, :], B["y_0"][0:8, 2, :], fa_ln)
            def queries_hi(name, c):
                step(G[name][c])
                q_hi(bank(G[name][c]), c, HD ** -0.5).then_inc(act_evac, 1)

            def keys_hi(name, c):
                step(G[name][c])
                k_hi(bank(G[name][c]), c).then_inc(act_evac, 1)

            for c in range(2):
                queries_hi("qa", c)
            for c in range(2):
                keys_hi("ka", c)

            def v_heads(name):
                g0 = G[name][0]
                for t in range(NT):
                    step(g0 + t)
                    out = B["v_hl"][:, t, :].rearrange("p (h s d) -> p h s d", h=8, s=2)[:, :, 0, :]
                    act.activation(out, bank(g0 + t).rearrange("p (h d) -> p h d", h=8), ACT.Copy)\
                        .then_inc(act_evac, 1)

            v_heads("va")

            def causal_exps(name, r0):
                def f(m):
                    i, n = m % 4, P * (m % 4 + 1)
                    if m >= 4:
                        act.wait_ge(tr_done, R0[name] + m - 3)
                    exponentials(S0[name] + m, B["p0"][:, P_OFF[i]:P_OFF[i] + n], n)
                return f

            def stacked_out(name, tmp):
                def f(h):
                    g = G[name]
                    step(g[h])
                    if h >= 2:
                        after_vector(g[h - 2])
                    lower_half(g[h], tmp[0:64, h % 2, :])
                return f

            def fox_fill(k):
                if k < 4:
                    (queries_hi, keys_hi)[k // 2](("qa", "ka")[k // 2], 2 + k % 2)
                else:
                    copy_lin(G["za"][k - 4], B["y_1"][:, k - 4, :])

            attention("fox", 32, lambda m: probs_hi(R0["fox"] + m, m, G["fox_pv"]), causal_exps("fox", R0["fox"]),
                      stacked_out("fox_pv", fox_tmp), fox_fill)
            act.wait_ge(act_evac, AN[G["za"][3]])
            act.activation(B["y_1"][:, :, :], B["y_1"][:, :, :], ACT.Silu).then_inc(za_silu, 1)

            load(B["rope_c"][:, :], a["rope_cos"], rope_in)
            load(B["rope_s"][:, :], a["rope_sin"], rope_in)

            def rope_hi_part(c):
                act.wait_ge(rope_done, c + 1)
                x = B["t_a"][:, c % 2, :]
                ins = q_hi(x, c, HD ** -0.5) if c < 4 else k_hi(x, c - 4)
                ins.then_inc(rope_hi, 1)

            for c in range(8):
                g = G["qb"][0] + c
                step(g)
                if c >= 2:
                    act.wait_ge(rope_done, c - 1)
                for quarter in range(4):
                    rows = slice(32 * quarter, 32 * quarter + 32)
                    other = 32 * (quarter ^ 1)
                    ins = act.activation(B["t_b"][rows, c % 2, :], lin[other:other + 32, g % 4, :], ACT.Copy)
                ins.then_inc(act_evac, 1)
                if c >= 1:
                    rope_hi_part(c - 1)
            rope_hi_part(7)
            for t in range(NT):
                step(G["vb"][t])
                act.activation(B["v_hl"][:, t, 0:T], bank(G["vb"][t]), ACT.Copy).then_inc(act_evac, 1)

            def diff_exps(w):
                i, n = w % 4, P * (w % 4 + 1)
                if w >= 4:
                    act.wait_ge(tr_done, R0["diff"] + w - 3)
                for m, buf in enumerate((B["p0"], B["px"])):
                    exponentials(S0["diff"] + 2 * w + m, buf[:, P_OFF[i]:P_OFF[i] + n], n)

            def diff_fill(k):
                copy_lin(G["zb"][k], B["z_b"][:, k, :])

            def diff_out(h):
                if h == 0:
                    act.wait_ge(ya_gated, 4)
                copy_lin(G["diff_pv"][h], B["y_1"][:, h, :])

            attention("diff", 16, lambda w: probs_hi(R0["diff"] + w, w, G["diff_pv"]), diff_exps, diff_out, diff_fill)
            head_roots(G["subln"][0], B["y_1"], B["t_sq"], B["t_r"], eps_n[:, 0:1], 0)
            act.activation(B["z_b"][:, :, :], B["z_b"][:, :, :], ACT.Silu).then_inc(zb_silu, 1)

            def split_y(k):
                src = B["y_0"][:, k, :] if k < 4 else B["y_1"][:, k - 4, :]
                act.activation(B["y_hi"][:, k, :], src, ACT.Copy).then_inc(y_hi_s, 1)

            act.wait_ge(yb_gated, 4)
            for k in range(8):
                split_y(k)
            with act.Fori(0, 2) as it:
                off = gate_offsets(it)
                for c in range(2):
                    g = G["gates"][8 * c]
                    for n in range(4):
                        act.wait_ge(lin_step, ST[g + n] + off.step)
                        act.wait_ge(dve_evac, DN[g - 1] + off.dve)
                        act.activation(B["t_g"][:, n, :], bank(g + n), ACT.Sigmoid).then_inc(act_evac, 1)
                    for n in range(2):
                        act.wait_ge(mg_sum, it * 4 + (2 * c + n + 1))
                        act.activation(B["m_hi"][:, bass.ds(it * 4 + (2 * c + n), 1), :],
                                       B["t_c"][:, n:n + 1, :], ACT.Copy).then_inc(mg_hi, 1)

            act.wait_ge(y_lo_s, 8)
            load(B["gain"][:, 0, :], row("g_post"), gain_in[1])
            load(B["gain"][:, 1, :], row("norm_mix_2"), gain_in[2])
            act.wait_ge(mg_lo, 8)
            for t in range(NT):
                load(B["x_m"][:, t, :], x_in[:, t, :], x_again)
            for j in range(2):
                for t in range(NT):
                    g = G["out1"][4 * j + t]
                    step(g)
                    if g > G["out1"][0]:
                        act.wait_ge(act_evac, AN[g] - 1)
                    act.activation(B["junk"][:, 0:T], bank(g), ACT.Square,
                                   accum_out=sumsq[:, N0["post"] + t, j:j + 1]).then_inc(act_evac, 1)
            load(B["one_hot"][0:32, :], a["bucket_one_hot"], gla_in)
            load(B["g_up"][0:16, :], a["w_gate_up_2"][0], gla_in)
            load(B["g_mask"][:, :, :], a["level_masks"], gla_in)
            for t in range(NT):
                act.wait_ge(x1_ready, t + 1)
                square_sum(Q0["mix"] + t, N0["mix"] + t, B["x_m"][:, t, :], B["junk"][:, :])
                act.dma_start(x1_dram[:, t, :], B["x_m"][:, t, :]).then_inc(x1_parked, 16)
            act.wait_ge(beta_ready, 1)
            act.dma_start(bias_dram, B["beta"][0:8, :]).then_inc(beta_out, 16)
            for t in range(NT):
                turned_tile_hi("mix", t, B["h_hi"])
            act.wait_ge(beta_out, 16)
            with nc.allow_non_contiguous_dma(reason="overlapping rows: entry (p, c) is distance entry 1 + p + c"):
                act.dma_start(bias_tiles, bass.AP(bias_dram.tensor, 1, [[1, P], [BIAS_COLS, 8], [1, 256]]))\
                    .then_inc(bias_in, 16)
            step(G["glr"][0])
            act.activation(B["g_lr"][0:16, :], lin[0:16, G["glr"][0] % 4, :], ACT.Copy).then_inc(act_evac, 1)
            for c in range(2):
                copy_lin(G["qg"][c], B["g_q"][:, c, :], HD ** -0.5)
            act.wait_ge(dve_evac, DN[G["gup"][1]])
            soft_log(B["g_x"][:, :, :], B["g_d"][:, 0], B["g_d"][:, 1], gla_ln)
            for c in range(2):
                copy_lin(G["kg"][c], B["g_k"][:, c, :])

            def level_exp(lev):
                act.wait_ge(gd_done, lev + 1)
                d = B["g_d"][:, lev % 2]
                act.activation(d, d, ACT.Exp).then_inc(ge_done, 1)

            for lev in range(2):
                level_exp(lev)
            for t in range(NT):
                copy_lin(G["vg"][t], B["g_v"][:, t, :])
            for lev in range(2, 4):
                level_exp(lev)
            for c in range(4):
                g = G["rg"][c]
                step(g)
                act.activation(B["y_0"][:, c, :], bank(g), ACT.Silu).then_inc(act_evac, 1)
            for lev in range(4, len(LEVELS) + 2):
                level_exp(lev)
            act.wait_ge(gd_done, len(LEVELS) + 2)
            act.activation(g_tail[:, :, :], B["g_b"][:, :, P - 1:T:P], ACT.Exp).then_inc(ge_done, 1)
            act.wait_ge(gla_const, 1)
            for h in range(4):
                g = G["cross"][2 * h]
                step(g)
                act.activation(B["g_a"][:, h, P:4 * P], lin[:, g % 4, 0:3 * P], ACT.Copy).then_inc(act_evac, 1)
                step(g + 1)
                c = PT_STRIDE + 2 * P
                act.activation(B["g_a"][:, h, c:c + 2 * P], lin[:, (g + 1) % 4, 0:2 * P], ACT.Copy)
                c = 2 * PT_STRIDE + 3 * P
                act.activation(B["g_a"][:, h, c:c + P], lin[:, (g + 1) % 4, 2 * P:3 * P], ACT.Copy)\
                    .then_inc(act_evac, 1)
            for h in range(4):
                copy_lin(G["gla_pv"][h], B["y_1"][:, h, :])
            act.wait_ge(act_evac, AN[G["gla_pv"][3]])
            head_roots(G["gnorm"][0], B["y_1"], B["g_d"][:, 0], B["g_d"][:, 1], eps_n[:, 1:2], 4)
            act.wait_ge(y_norm, 8)
            for c in range(2):
                queries_hi("qa2", c)
            for c in range(2):
                keys_hi("ka2", c)
            v_heads("va2")
            attention("moba", 32, lambda m: probs_hi(R0["moba"] + m, m, G["moba_pv"]),
                      causal_exps("moba", R0["moba"]), stacked_out("moba_pv", B["z_b"][:, 0:2, :]),
                      lambda k: (queries_hi, keys_hi)[k // 2](("qa2", "ka2")[k // 2], 2 + k % 2))
            for t in range(2):
                load(B["h_m2"][:, t, :], mem_in[:, t, :], mem_in_s)
            load(B["gain2"][:, 0, :], row("norm_mem_2"), gain_in[3])
            load(B["gain2"][:, 1, :], row("norm_xattn_2"), gain_in[3])
            after_vector(G["moba_pv"][7])
            for k in range(8):
                split_y(k)
            act.wait_ge(y_lo_s, 16)
            load(B["x_res"][:, :, :], x1_dram, x1_back)
            act.wait_ge(mem_in_s, 32)
            for t in range(2):
                square_sum(Q0["mem"] + t, N0["mem"] + t, B["h_m2"][:, t, :], B["junk2"][:, :])
            for t in range(NT):
                after_vector(G["out2"][4 + t])
                square_sum(Q0["nx"] + t, N0["nx"] + t, B["x_res"][:, t, :], B["junk2"][:, :])
                if t < 2:
                    turned_tile_hi("mem", t, B["mem_hi"])
            act.wait_ge(h_ready, H0["mem"] + 2)
            load(B["gain2"][:, 0, :], row("norm_mlp_2"), gain_in[4])
            for c in range(8):
                step(G["kx"][c])
                act.activation(B["xk_hi"][:, c, :], bank(G["kx"][c], MEM), ACT.Copy).then_inc(act_evac, 1)
            for j in range(2):
                for t in range(2):
                    copy_lin(G["vx"][2 * j + t], B["xv_hi"][:, t, T * j:T * j + T])
            for t in range(NT):
                turned_tile_hi("nx", t, B["h_hi"])
            act.wait_ge(h_ready, H0["nx"] + 4)
            load(B["gain2"][:, 1, :], row("norm_final_2"), gain_in[5])
            def x_queries_hi(c):
                copy_lin(G["xq"][c], B["xq_hi"][:, c, :], (D // 4) ** -0.5)

            for c in range(4):
                x_queries_hi(c)

            def x_exps(m):
                if m >= 4:
                    act.wait_ge(tr_done, R0["x"] + m - 3)
                exponentials(S0["x"] + m, B["xp"][:, m % 4, :], MEM)

            def x_hi(m):
                h, i, r = m // 4, m % 4, R0["x"] + m
                act.wait_ge(tr_done, r + 1)
                if h >= 2:
                    step(G["x_pv"][2 * (h - 2) + 1])
                out = B["xpt_hi"][:, h % 2, :].rearrange("p (j q) -> p j q", j=2)[:, :, P * i:P * i + P]
                act.activation(out, tr[:, r % 2, 0:MEM].rearrange("p (j c) -> p j c", j=2), ACT.Copy)\
                    .then_inc(tr_hi, 1)

            def x_out_hi(h):
                for dv in range(2):
                    copy_lin(G["x_pv"][2 * h + dv], B["h_hi"][:, 2 * h + dv, :])

            attention("x", 16, x_hi, x_exps, x_out_hi, lambda k: x_queries_hi(4 + k))
            for t in range(NT):
                after_vector(G["xo"][4 + t])
                square_sum(Q0["nmlp"] + t, N0["nmlp"] + t, B["x_res"][:, t, :], B["junk2"][:, :])
            for t in range(NT):
                turned_tile_hi("nmlp", t, B["h_hi"])
            with act.Fori(0, FF_CHUNKS) as it:
                off = mlp_offsets(it)
                for c in range(8):
                    g = G["mlp"][c]
                    act.wait_ge(lin_step, ST[g] + off.step)
                    act.wait_ge(dve_evac, (DN[g - 2] if c >= 2 else DN[G["mlp"][0] - 1]) + off.dve)
                    act.activation(B["relu"][:, c % 2, :], bank(g), ACT.Relu).then_inc(act_evac, 1)
                    act.wait_ge(dve_evac, DN[g] + off.dve)
                    act.activation(B["u_hi"][:, c, :], B["u_f"][:, c % 2, :], ACT.Copy).then_inc(u_hi_s, 1)
            for t in range(NT):
                act.wait_ge(dve_evac, DN[len(K_) - 4 + t])
                square_sum(Q0["final"] + t, N0["final"] + t, B["x_res"][:, t, :], B["junk2"][:, :])

        @block.vector
        def _(dve):
            own = [0]

            def link(ins):
                own[0] += 1
                ins.then_inc(dve_self, 1)
                dve.wait_ge(dve_self, own[0])

            def step(g, off=HERE):
                dve.wait_ge(lin_step, ST[g] + off.step)

            def bank(g, cols=T):
                return lin[:, g % 4, 0:cols]

            def after_scalar(g, off=HERE):
                dve.wait_ge(act_evac, AN[g] + off.act)

            def variance(n, halves=1):
                src = sumsq[:, n, 0:1]
                if halves == 2:
                    link(dve.tensor_tensor(src, src, sumsq[:, n, 1:2], ALU.add))
                dve.tensor_scalar(var[:, n:n + 1], src, 1.0 / D, EPS, ALU.mult, ALU.add).then_inc(var_done, 1)

            def normed(name, t, out, x, gain):
                if t >= 2:
                    dve.wait_ge(tr_done, R0[name] + 2 * (t - 1))
                dve.wait_ge(rstd_done, N0[name] + t + 1)
                n = N0[name] + t
                dve.scalar_tensor_tensor(out, x, rstd[:, n:n + 1], gain, ALU.mult, ALU.mult).then_inc(h_ready, 1)

            def turned_tile_lo(name, t, hi, lo):
                for half in range(2):
                    r = R0[name] + 2 * t + half
                    k, c = slice(4 * half, 4 * half + 4), slice(P * t, P * t + P)
                    dve.wait_ge(tr_hi, r + 1)
                    dve.tensor_tensor(lo[:, k, c], tr[:, r % 2, :].rearrange("p (b c) -> p b c", b=4),
                                      as_f32(hi[:, k, c]), ALU.subtract).then_inc(tr_lo, 1)

            def lo_part(out, x, hi, scale=1.0):
                if scale == 1.0:
                    return dve.tensor_tensor(out, x, as_f32(hi), ALU.subtract)
                return dve.scalar_tensor_tensor(out, x, scale, as_f32(hi), ALU.mult, ALU.subtract)

            def q_lo(x, c, scale):
                q = B["q_st"]
                lo_part(q[64:128, 2 * c, :], x[0:64], q[0:64, 2 * c, :], scale)
                return lo_part(q[0:64, 2 * c + 1, :], x[64:128], q[64:128, 2 * c + 1, :], scale)

            def k_lo(x, c):
                for head in range(2):
                    rows = slice(64 * head, 64 * head + 64)
                    ins = lo_part(B["k_lo"][rows, c, :], x[rows], B["k_hh"][rows, 2 * c + head, :])
                return ins

            def queries_lo(name, c):
                after_scalar(G[name][c])
                q_lo(bank(G[name][c]), c, HD ** -0.5).then_inc(dve_evac, 1)

            def keys_lo(name, c):
                after_scalar(G[name][c])
                k_lo(bank(G[name][c]), c).then_inc(dve_evac, 1)

            def row_max(s, n):
                dve.wait_ge(s_done, s + 1)
                dve.reduce_max(neg_max[:, s:s + 1], sc[:, s % 2, 0:n], AX, negate=True).then_inc(s_max, 1)

            def invert(s):
                dve.wait_ge(s_exp, s + 1)
                dve.reciprocal(rden[:, s:s + 1], denom[:, s:s + 1]).then_inc(s_rec, 1)

            def probs_lo(r, m):
                h, i = m // 4, m % 4
                dve.wait_ge(tr_hi, r + 1)
                dve.tensor_tensor(blocks(B["pt_lo"], h % 2, i),
                                  tr[:, r % 2, 0:P * (i + 1)].rearrange("p (j c) -> p j c", c=P),
                                  as_f32(blocks(B["pt_hi"], h % 2, i)), ALU.subtract).then_inc(tr_lo, 1)

            def attention(name, tiles, maxima, lo, inverses, values, fill):
                for m in range(tiles + 6):
                    if m < tiles:
                        maxima(m)
                    if 0 <= m - 4 < tiles:
                        lo(m - 4)
                    if 0 <= m - 1 < tiles:
                        inverses(m - 1)
                    if m >= 1 and fill_ends(name, m - 1) is not None:
                        fill(fill_ends(name, m - 1))
                    if m >= 9 and m % 4 == 1:
                        values((m - 9) // 4)

            def stacked_out(name, tmp):
                def f(h):
                    g = G[name][h]
                    after_scalar(g)
                    dve.tensor_tensor(B["y_0"][64 * (h % 2):64 * (h % 2) + 64, h // 2, :], lin[0:64, g % 4, :],
                                      tmp[0:64, h % 2, :], ALU.add).then_inc(dve_evac, 1)
                return f

            def causal_max(name):
                return lambda m: row_max(S0[name] + m, P * (m % 4 + 1))

            def soft_sum(x, t1, done, ready):
                dve.wait_ge(done, ready)
                link(dve.scalar_tensor_tensor(x, x, 0.0, t1, ALU.min, ALU.subtract))

            def v_heads(name):
                g0 = G[name][0]
                for t in range(NT):
                    after_scalar(g0 + t)
                    v = B["v_hl"][:, t, :].rearrange("p (h s d) -> p h s d", h=8, s=2)
                    dve.tensor_tensor(v[:, :, 1, :], bank(g0 + t).rearrange("p (h d) -> p h d", h=8),
                                      as_f32(v[:, :, 0, :]), ALU.subtract).then_inc(dve_evac, 1)

            def head_norms(g0, y, root):
                for h in range(4):
                    after_scalar(g0 + h)
                    link(dve.reciprocal(root[:, h % 2, :], root[:, h % 2, :]))
                    dve.tensor_tensor(y[:, h, :], y[:, h, :], root[:, h % 2, :], ALU.mult).then_inc(y_norm, 1)

            def split_y(k):
                src = B["y_0"][:, k % 8, :] if k % 8 < 4 else B["y_1"][:, k % 8 - 4, :]
                dve.wait_ge(y_hi_s, k + 1)
                lo_part(B["y_lo"][:, k % 8, :], src, B["y_hi"][:, k % 8, :]).then_inc(y_lo_s, 1)

            dve.wait_ge(consts_made, 1)
            dve.wait_ge(small_in, 16 * 5)
            dve.tensor_tensor(pick[:, :], ident[:, 0:8], ident[:, 32:40], ALU.add)
            link(dve.tensor_scalar(g_subln[:, :], g_subln[:, :], 1.0 - LAM_INIT, None, ALU.mult))
            for t in range(NT):
                dve.wait_ge(sq_done, Q0["norm1"] + t + 1)
                variance(N0["norm1"] + t)
            dve.wait_ge(small_in2, 16 * 4)
            pairs = B["lam_v"][:, :, :].rearrange("p (a b) d -> p a b d", b=2)
            link(dve.tensor_tensor(pairs[:, :, 0, :], pairs[:, :, 0, :], pairs[:, :, 1, :], ALU.mult))
            dve.tensor_reduce(lam_d[:, :], pairs[:, :, 0, :], AX, ALU.add).then_inc(lam_ready, 1)
            dve.wait_ge(gain_in[0], 16)
            for t in range(NT):
                normed("norm1", t, B["h_m"][:, t % 2, :], B["x_m"][:, t, :], B["gain"][:, 0, :])
                if t >= 1:
                    turned_tile_lo("norm1", t - 1, B["h_hi"], B["h_lo"])
            turned_tile_lo("norm1", 3, B["h_hi"], B["h_lo"])
            dve.wait_ge(lam_exp, 1)
            link(dve.scalar_tensor_tensor(neg_lam[:, :], lam_e[:, 1:2], LAM_INIT, lam_e[:, 0:1], ALU.subtract,
                                          ALU.subtract))
            g = G["fa"][0]
            step(g)
            fx, ft, fc = (B["y_0"][0:8, n, :] for n in (0, 1, 3))
            f_one = B["y_1"][0:8, 0, :]
            dve.wait_ge(h_ready, H0["norm1"] + 4)
            dve.memset(f_one, 1.0)
            dve.tensor_scalar(fx, lin[0:8, g % 4, :], b_forget[0:8, :], None, ALU.add).then_inc(dve_evac, 1)
            soft_sum(fx, ft, fa_ln, 1)
            link(dve.tensor_tensor_scan(fc, f_one, fx, 0.0, ALU.mult, ALU.add))
            link(dve.tensor_scalar(c_row[0:8, :], fc, -1.0, None, ALU.mult))
            dve.scalar_tensor_tensor(c_row[32:40, :], fc, -1.0, as_f32(c_row[0:8, :]), ALU.mult, ALU.subtract)\
                .then_inc(c_ready, 1)
            for c in range(2):
                queries_lo("qa", c)
            for c in range(2):
                keys_lo("ka", c)
            v_heads("va")

            def fox_fill(k):
                if k < 4:
                    (queries_lo, keys_lo)[k // 2](("qa", "ka")[k // 2], 2 + k % 2)

            attention("fox", 32, causal_max("fox"), lambda m: probs_lo(R0["fox"] + m, m),
                      lambda m: invert(S0["fox"] + m), stacked_out("fox_pv", fox_tmp), fox_fill)
            dve.wait_ge(dve_evac, DN[G["fox_pv"][7]])
            dve.wait_ge(za_silu, 1)
            for c in range(4):
                y = B["y_0"][:, c, :]
                dve.tensor_tensor(y, y, B["y_1"][:, c, :], ALU.mult).then_inc(ya_gated, 1)
            dve.wait_ge(rope_in, 32)

            def rope_lo_part(c):
                dve.wait_ge(rope_hi, c + 1)
                x = B["t_a"][:, c % 2, :]
                ins = q_lo(x, c, HD ** -0.5) if c < 4 else k_lo(x, c - 4)
                ins.then_inc(rope_lo, 1)

            for c in range(8):
                g = G["qb"][0] + c
                after_scalar(g)
                if c >= 2:
                    dve.wait_ge(rope_lo, c - 1)
                x = B["t_a"][:, c % 2, :]
                dve.tensor_tensor(x, bank(g), B["rope_c"][:, :], ALU.mult).then_inc(dve_evac, 1)
                if c >= 1:
                    rope_lo_part(c - 1)
                dve.wait_ge(rot_mul, c + 1)
                dve.wait_ge(dve_evac, DN[g])
                dve.tensor_tensor(x, x, B["t_b"][:, c % 2, :], ALU.add).then_inc(rope_done, 1)
            rope_lo_part(7)
            for t in range(NT):
                after_scalar(G["vb"][t])
                v = B["v_hl"][:, t, :]
                lo_part(v[:, T:2 * T], bank(G["vb"][t]), v[:, 0:T]).then_inc(dve_evac, 1)

            def diff_max(w):
                for m in range(2):
                    row_max(S0["diff"] + 2 * w + m, P * (w % 4 + 1))

            def diff_invert(w):
                s = S0["diff"] + 2 * w
                dve.wait_ge(s_exp, s + 2)
                dve.reciprocal(rden[:, s:s + 2], denom[:, s:s + 2]).then_inc(s_rec, 1)
                dve.wait_ge(s_rec, V0["diff"] + w + 1)
                link(dve.tensor_scalar(rden[:, s + 1:s + 2], rden[:, s + 1:s + 2], neg_lam[:, :], None, ALU.mult))

            def difference(w):
                i, s = w % 4, S0["diff"] + 2 * w
                c = slice(P_OFF[i], P_OFF[i] + P * (i + 1))
                dve.wait_ge(s_norm, V0["diff"] + w + 1)
                dve.scalar_tensor_tensor(B["p0"][:, c], B["px"][:, c], rden[:, s + 1:s + 2], B["p0"][:, c],
                                         ALU.mult, ALU.add).then_inc(pd_done, 1)

            for w in range(16 + 4):
                if 0 <= w - 2 < 16:
                    difference(w - 2)
                if w < 16:
                    diff_max(w)
                if 0 <= w - 4 < 16:
                    probs_lo(R0["diff"] + w - 4, w - 4)
                if 0 <= w - 1 < 16:
                    diff_invert(w - 1)
            head_norms(G["subln"][0], B["y_1"], B["t_r"])
            dve.wait_ge(y_norm, 4)
            dve.wait_ge(zb_silu, 1)
            for c in range(4):
                y = B["y_1"][:, c, :]
                dve.scalar_tensor_tensor(y, y, g_subln[:, :], B["z_b"][:, c, :], ALU.mult, ALU.mult)\
                    .then_inc(yb_gated, 1)
            for k in range(8):
                split_y(k)
            with dve.Fori(0, 2) as it:
                off = gate_offsets(it)
                for c in range(2):
                    for n in range(2):
                        g = G["gates"][8 * c + 4 + 2 * n]
                        dve.wait_ge(act_evac, AN[g] + off.act)
                        for br, buf in enumerate(("t_a", "t_b")):
                            step(g + br, off)
                            dve.tensor_tensor(B[buf][:, n, :], bank(g + br), B["t_g"][:, 2 * br + n, :], ALU.mult)\
                                .then_inc(dve_evac, 1)
                        dve.wait_ge(dve_evac, DN[g + 1] + off.dve)
                        dve.tensor_tensor(B["t_c"][:, n, :], B["t_a"][:, n, :], B["t_b"][:, n, :], ALU.add)\
                            .then_inc(mg_sum, 1)
                        dve.wait_ge(mg_hi, it * 4 + (2 * c + n + 1))
                        tile = bass.ds(it * 4 + (2 * c + n), 1)
                        dve.tensor_tensor(B["m_lo"][:, tile, :], B["t_c"][:, n:n + 1, :],
                                          as_f32(B["m_hi"][:, tile, :]), ALU.subtract).then_inc(mg_lo, 1)
            dve.wait_ge(mg_lo, 8)
            for j in range(2):
                for t in range(NT):
                    g = G["out1"][4 * j + t]
                    after_scalar(g)
                    dve.tensor_copy(B["y_m"][:, t, T * j:T * j + T], bank(g)).then_inc(dve_evac, 1)
            for t in range(NT):
                variance(N0["post"] + t, halves=2)
            dve.wait_ge(gain_in[1], 16)
            dve.wait_ge(gain_in[2], 16)
            dve.wait_ge(x_again, 64)
            dve.wait_ge(dve_evac, DN[G["out1"][7]])
            for t in range(NT):
                n = N0["post"] + t
                dve.wait_ge(rstd_done, n + 1)
                y = B["y_m"][:, t, :]
                link(dve.scalar_tensor_tensor(y, y, rstd[:, n:n + 1], B["gain"][:, 0, :], ALU.mult, ALU.mult))
                dve.tensor_tensor(B["x_m"][:, t, :], B["x_m"][:, t, :], y, ALU.add).then_inc(x1_ready, 1)
            for t in range(NT):
                dve.wait_ge(sq_done, Q0["mix"] + t + 1)
                variance(N0["mix"] + t)
            g = G["bias"][0]
            step(g)
            link(dve.tensor_copy(B["g_x"][0:8, 0, 0:1], lin[0:8, g % 4, 0:1]))
            dve.tensor_scalar(B["beta"][0:8, :], lin[0:8, g % 4, 0:BIAS_COLS], B["g_x"][0:8, 0, 0:1], None,
                              ALU.subtract).then_inc(dve_evac, 1)
            dve.wait_ge(dve_evac, DN[g])
            dve.memset(B["beta"][0:8, 257:BIAS_COLS], FAR).then_inc(beta_ready, 1)
            for t in range(NT):
                normed("mix", t, B["h_m"][:, t % 2, :], B["x_m"][:, t, :], B["gain"][:, 1, :])
                if t >= 1:
                    turned_tile_lo("mix", t - 1, B["h_hi"], B["h_lo"])
            turned_tile_lo("mix", 3, B["h_hi"], B["h_lo"])
            for dt in range(2):
                g = G["gup"][dt]
                step(g)
                dve.tensor_scalar(B["g_x"][:, dt, :], bank(g), b_gate[:, dt:dt + 1], None, ALU.add)\
                    .then_inc(dve_evac, 1)
            soft_sum(B["g_x"][:, :, :], B["g_d"][:, 0], gla_ln, 1)
            link(dve.tensor_scalar(B["g_x"][:, :, :], B["g_x"][:, :, :], 1.0 / 16.0, None, ALU.mult))
            dve.wait_ge(gla_const, 1)
            for dt in range(2):
                link(dve.tensor_tensor_scan(B["g_b"][:, dt, :], B["g_keep"][:, :], B["g_x"][:, dt, :], 0.0,
                                            ALU.mult, ALU.add))

            def halves(buf, s):
                v = buf.rearrange("p t q -> p (t q)").rearrange("p (n c) -> p n c", c=2 * s)
                return v[:, :, 0:s], v[:, :, s:2 * s]

            def level_distance(lev):
                s = LEVELS[lev]
                n = 2 * T // (2 * s)
                first, second = halves(B["g_b"][:, :, :], s)
                middle = first[:, :, s - 1:s].to_broadcast([P, n, s])
                d_first, d_second = halves(B["g_d"][:, lev % 2], s)
                if lev >= 2:
                    dve.wait_ge(gz_done, lev - 1)
                dve.tensor_tensor(d_first, middle, first, ALU.subtract)
                dve.tensor_tensor(d_second, second, middle, ALU.subtract).then_inc(gd_done, 1)

            def level_operands(lev):
                s = LEVELS[lev]
                dve.wait_ge(ge_done, lev + 1)
                if lev >= 2:
                    step(G["levels"][4 * (lev - 2) + 3])
                e_first, e_second = halves(B["g_d"][:, lev % 2], s)
                z_first, z_second = halves(B["g_z"][:, lev % 2], s)
                dve.tensor_tensor(z_first, e_first, halves(B["g_k"][:, :, :], s)[0], ALU.mult)
                dve.tensor_tensor(z_second, e_second, halves(B["g_q"][:, :, :], s)[1], ALU.mult).then_inc(gz_done, 1)

            def level_scores(lev):
                for h in range(4):
                    g = G["levels"][4 * lev + h]
                    step(g)
                    if lev > 0:
                        dve.wait_ge(dve_evac, DN[g - 4])
                    dve.copy_predicated(diagonal(B["g_a"], h),
                                        B["g_mask"][:, lev:lev + 1, :].to_broadcast([P, NT, P]),
                                        bank(g).rearrange("p (t q) -> p t q", q=P)).then_inc(dve_evac, 1)

            for lev in range(2):
                level_distance(lev)
            dve.wait_ge(act_evac, AN[G["kg"][1]])
            dve.wait_ge(gla_in, 48)
            for lev in range(2):
                level_operands(lev)
            for lev in range(2, 4):
                level_distance(lev)
            for lev in range(len(LEVELS)):
                level_scores(lev)
                if lev + 2 < len(LEVELS):
                    level_operands(lev + 2)
                if lev + 4 < len(LEVELS):
                    level_distance(lev + 4)
                if lev == 4:
                    dve.wait_ge(gz_done, len(LEVELS) - 1)
                    last = B["g_b"][:, :, P - 1:T:P].rearrange("p t (n o) -> p t n o", o=1)
                    b4 = B["g_b"][:, :, :].rearrange("p t (n c) -> p t n c", c=P)
                    for dt in range(2):
                        ins = dve.tensor_tensor(B["g_d"][:, 1, dt, :].rearrange("p (n c) -> p n c", c=P),
                                                last[:, dt].to_broadcast([P, NT, P]), b4[:, dt], ALU.subtract)
                    ins.then_inc(gd_done, 1)
            level_scores(len(LEVELS))
            dve.wait_ge(gz_done, len(LEVELS))
            dve.tensor_copy(B["g_d"][:, 0], B["g_b"][:, :, :]).then_inc(gd_done, 1)
            dve.wait_ge(ge_done, len(LEVELS) + 3)
            dve.tensor_tensor(B["g_qe"][:, :, :], B["g_d"][:, 0], B["g_q"][:, :, :], ALU.mult)
            link(dve.tensor_tensor(B["g_kd"][:, :, :], B["g_d"][:, 1], B["g_k"][:, :, :], ALU.mult))
            for dt in range(2):
                kd, kx = B["g_kd"][:, dt, :], B["g_kx"][:, dt]
                link(dve.tensor_scalar(kx[:, 0, :], kd[:, 0:P], g_tail[:, dt, 1:2], None, ALU.mult))
                dve.tensor_scalar(kx[:, 1, :], kx[:, 0, :], g_tail[:, dt, 2:3], None, ALU.mult)
                ins = dve.tensor_scalar(kx[:, 2, :], kd[:, P:2 * P], g_tail[:, dt, 2:3], None, ALU.mult)
            ins.then_inc(gz_done, 1)
            head_norms(G["gnorm"][0], B["y_1"], B["g_d"][:, 1])
            dve.wait_ge(y_norm, 8)
            for h in range(4):
                y = B["y_1"][:, h, :]
                link(dve.scalar_tensor_tensor(y, y, g_gain[:, :], B["y_0"][:, h, :], ALU.mult, ALU.mult))
            for c in range(2):
                queries_lo("qa2", c)
            for c in range(2):
                keys_lo("ka2", c)
            v_heads("va2")
            attention("moba", 32, causal_max("moba"), lambda m: probs_lo(R0["moba"] + m, m),
                      lambda m: invert(S0["moba"] + m), stacked_out("moba_pv", B["z_b"][:, 0:2, :]),
                      lambda k: (queries_lo, keys_lo)[k // 2](("qa2", "ka2")[k // 2], 2 + k % 2))
            for k in range(8, 16):
                split_y(k)
            for t in range(2):
                dve.wait_ge(sq_done, Q0["mem"] + t + 1)
                variance(N0["mem"] + t)
            dve.wait_ge(gain_in[3], 32)
            for t in range(2):
                normed("mem", t, B["h_m2"][:, t, :], B["h_m2"][:, t, :], B["gain2"][:, 0, :])

            def add_to_x(g, t, j, off=HERE):
                step(g, off)
                x = B["x_res"][:, t, T * j:T * j + T]
                dve.tensor_tensor(x, x, bank(g), ALU.add).then_inc(dve_evac, 1)

            dve.wait_ge(x1_back, 16)
            for j in range(2):
                for t in range(NT):
                    add_to_x(G["out2"][4 * j + t], t, j)
            for t in range(NT):
                dve.wait_ge(sq_done, Q0["nx"] + t + 1)
                variance(N0["nx"] + t)
                if t < 2:
                    turned_tile_lo("mem", t, B["mem_hi"], B["mem_lo"])
            for t in range(2):
                if t == 0:
                    dve.wait_ge(tr_done, R0["mem"] + 4)
                normed("nx", t, B["h_m2"][:, t, :], B["x_res"][:, t, :], B["gain2"][:, 1, :])
            for c in range(8):
                after_scalar(G["kx"][c])
                lo_part(B["xk_lo"][:, c, :], bank(G["kx"][c], MEM), B["xk_hi"][:, c, :]).then_inc(dve_evac, 1)
            for j in range(2):
                for t in range(2):
                    g, c = G["vx"][2 * j + t], slice(T * j, T * j + T)
                    after_scalar(g)
                    lo_part(B["xv_lo"][:, t, c], bank(g), B["xv_hi"][:, t, c]).then_inc(dve_evac, 1)
            for t in range(2, NT):
                normed("nx", t, B["h_m2"][:, t % 2, :], B["x_res"][:, t, :], B["gain2"][:, 1, :])
                turned_tile_lo("nx", t - 2, B["h_hi"], B["h_lo"])
            for t in range(2, NT):
                turned_tile_lo("nx", t, B["h_hi"], B["h_lo"])
            def x_queries_lo(c):
                g = G["xq"][c]
                after_scalar(g)
                lo_part(B["xq_lo"][:, c, :], bank(g), B["xq_hi"][:, c, :], (D // 4) ** -0.5).then_inc(dve_evac, 1)

            for c in range(4):
                x_queries_lo(c)

            def x_lo(m):
                h, i, r = m // 4, m % 4, R0["x"] + m
                dve.wait_ge(tr_hi, r + 1)
                hi, lo = (b[:, h % 2, :].rearrange("p (j q) -> p j q", j=2)[:, :, P * i:P * i + P]
                          for b in (B["xpt_hi"], B["xpt_lo"]))
                dve.tensor_tensor(lo, tr[:, r % 2, 0:MEM].rearrange("p (j c) -> p j c", j=2), as_f32(hi),
                                  ALU.subtract).then_inc(tr_lo, 1)

            def x_out_lo(h):
                for dv in range(2):
                    g = G["x_pv"][2 * h + dv]
                    after_scalar(g)
                    lo_part(B["h_lo"][:, 2 * h + dv, :], bank(g), B["h_hi"][:, 2 * h + dv, :]).then_inc(dve_evac, 1)

            attention("x", 16, lambda m: row_max(S0["x"] + m, MEM), x_lo, lambda m: invert(S0["x"] + m), x_out_lo,
                      lambda k: x_queries_lo(4 + k))
            for j in range(2):
                for t in range(NT):
                    add_to_x(G["xo"][4 * j + t], t, j)
            for t in range(NT):
                dve.wait_ge(sq_done, Q0["nmlp"] + t + 1)
                variance(N0["nmlp"] + t)
            dve.wait_ge(gain_in[4], 16)
            dve.wait_ge(gain_in[5], 16)
            for t in range(NT):
                if t == 0:
                    dve.wait_ge(tr_done, R0["nx"] + 8)
                normed("nmlp", t, B["h_m2"][:, t % 2, :], B["x_res"][:, t, :], B["gain2"][:, 0, :])
                if t >= 1:
                    turned_tile_lo("nmlp", t - 1, B["h_hi"], B["h_lo"])
            turned_tile_lo("nmlp", 3, B["h_hi"], B["h_lo"])
            with dve.Fori(0, FF_CHUNKS) as it:
                off = mlp_offsets(it)
                for c in range(8):
                    g = G["mlp"][c]
                    dve.wait_ge(act_evac, AN[g] + off.act)
                    u = B["u_f"][:, c % 2, :]
                    r = B["relu"][:, c % 2, :]
                    dve.scalar_tensor_tensor(u, bank(g), 0.0, r, ALU.max, ALU.mult).then_inc(dve_evac, 1)
                    dve.wait_ge(u_hi_s, it * 8 + (c + 1))
                    lo_part(B["u_lo"][:, c, :], u, B["u_hi"][:, c, :]).then_inc(u_lo_s, 1)
                for j in range(2):
                    for t in range(NT):
                        add_to_x(G["mlp"][8 + 4 * j + t], t, j, off)
            for t in range(NT):
                dve.wait_ge(sq_done, Q0["final"] + t + 1)
                variance(N0["final"] + t)
            for t in range(NT):
                n = N0["final"] + t
                dve.wait_ge(rstd_done, n + 1)
                x = B["x_res"][:, t, :]
                dve.scalar_tensor_tensor(x, x, rstd[:, n:n + 1], B["gain2"][:, 1, :], ALU.mult, ALU.mult)\
                    .then_inc(final_ready, 1)


INPUTS = ["x", "g_pre", "w_in", "b_forget", "lambda_q1", "lambda_k1", "lambda_q2", "lambda_k2", "g_subln",
          "w_branch", "w_out", "g_post", "mem_2", "rp_table_2", "norm_mix_2", "w_in_2", "w_gate_up_2", "b_gate_2",
          "g_norm_2", "w_out_2", "norm_xattn_2", "norm_mem_2", "w_xq_2", "w_xkv_2", "w_xo_2", "norm_mlp_2",
          "w_up_2", "w_down_2", "norm_final_2"]


def kernel(**inputs):
    import concourse.bacc as bacc
    from concourse.bass_utils import run_bass_kernel_spmd as run

    nc = bacc.Bacc("TRN2", target_bir_lowering=False, num_devices=1)
    arrays = {name: np.ascontiguousarray(inputs[name]) for name in INPUTS}
    arrays |= shape_constants()
    tensors = {name: nc.dram_tensor(f"in_{name}", v.shape, mybir.dt.from_np(v.dtype), kind="ExternalInput").ap()
               for name, v in arrays.items()}
    tensors["x1_dram"] = nc.dram_tensor("x1_dram", (T, D), F32, kind="Internal").ap()
    tensors["bias_dram"] = nc.dram_tensor("bias_dram", (8, BIAS_COLS), F32, kind="Internal").ap()
    out = nc.dram_tensor("out_0", (1, T, D), F32, kind="ExternalOutput").ap()
    two_blocks_kernel(nc, tensors, out)
    result = run(nc, [{f"in_{name}": v for name, v in arrays.items()}], core_ids=[0])
    return result.results[0]["out_0"]
```

```python
from contextlib import ExitStack
import math

import numpy as np

import concourse.bass as bass
from concourse import mybir

F32 = mybir.dt.float32
F32R = mybir.dt.float32r
BF16 = mybir.dt.bfloat16
I32 = mybir.dt.int32
ALU = mybir.AluOpType
ACT = mybir.ActivationFunctionType
AX = mybir.AxisListType.X

P = 128
T = 512
NT = T // P
D = 1024
KT = D // P
MEM = 256
HD = 64
FF_CHUNKS = 4
EPS = 1e-6
SUBLN_EPS = 1e-5
LAM_INIT = 0.8 - 0.6 * math.exp(-0.3 * 0)
FAR = -1.0e30
PT_STRIDE = 384
PT_COLS = PT_STRIDE * 3 + T
P_OFF = [0, 128, 384, 768]
P_COLS = 1280
BIAS_COLS = 384
LEVELS = [64, 32, 16, 8, 4, 2, 1]

C1 = {"qa": 0, "ka": 512, "va": 1024, "fa": 1536, "za": 1544, "qb": 2056, "kb": 2568, "vb": 3080, "zb": 3592,
      "gA": 4104, "gB": 5128}
C2 = {"qa": 0, "ka": 512, "va": 1024, "qg": 1536, "kg": 1792, "vg": 2048, "glr": 2560, "rg": 2576}


class Plan:

    def __init__(self):
        self.units, self.groups = {}, {}
        self.unit_name, self.unit_last_step = [], []
        self.group_step, self.kind, self.act_n, self.dve_n = [], [], [], []
        self.steps = 0

    def unit(self, name):
        of_phase = self.units.setdefault(name, [])
        self.unit_name.append((name, len(of_phase)))
        of_phase.append(len(self.unit_last_step))
        self.unit_last_step.append(self.steps)

    def group(self, name, kind, n=1):
        for _ in range(n):
            self.groups.setdefault(name, []).append(len(self.kind))
            self.kind.append(kind)
            self.act_n.append((self.act_n[-1] if self.act_n else 0) + ("A" in kind))
            self.dve_n.append((self.dve_n[-1] if self.dve_n else 0) + ("D" in kind))
            self.steps += 1
            self.group_step.append(self.steps)

    def t_units(self, name, kind, units=1, groups=2):
        for _ in range(units):
            self.group(name, kind, groups)
            self.unit(name)

    def m_units(self, name, kind, pairs=1, tiles=NT):
        for _ in range(pairs):
            self.steps += 1
            self.unit(name)
            self.group(name, kind, tiles)
            self.unit(name)

    def attention(self, name, kind, tiles, per_head, filling):
        for m in range(tiles + 5):
            if fill_ends(filling, m) is not None:
                at = filling_at(filling, m)
                phase, groups = FILLING[filling][at.unit][0], FILLING[filling][at.unit][4]
                self.group(phase, FILL_KIND[phase])
                if at.group == groups - 1:
                    self.unit(phase)
            if values_head(m) is not None:
                self.group(name, kind, per_head)


FILLING = {"fox": [("qa", 2, 0, 4, 2), ("ka", 2, 8, 4, 2), ("za", 0, 16, 4, 2), ("za", 2, 24, 4, 2)],
           "diff": [("zb", 0, 0, 4, 2), ("zb", 2, 8, 4, 2)],
           "moba": [("qa2", 2, 0, 4, 2), ("ka2", 2, 8, 4, 2), ("out2g", 0, 21, 2, 4), ("out2g", 4, 29, 2, 4)],
           "x": [("xq", 4, 0, 2, 2), ("xq", 6, 4, 3, 2), ("xo_a", 0, 13, 1, 4), ("xo_a", 4, 17, 1, 4)]}
FILL_KIND = {"qa": "AD", "ka": "AD", "za": "A", "zb": "A", "qa2": "AD", "ka2": "AD", "out2g": "D", "xq": "AD",
             "xo_a": "D"}


class FillingAt:

    def __init__(self, unit, group, part, place):
        self.unit, self.group, self.part, self.place = unit, group, part, place


def filling_at(attention, m):
    place = 0
    for u, (_, _, first, span, groups) in enumerate(FILLING[attention]):
        if first <= m < first + groups * span:
            group, part = divmod(m - first, span)
            return FillingAt(u, group, part, place + group)
        place += groups
    return None


HI_BY_SCALAR = [("kx", 2), ("kx", 3), ("vx", 0), ("vx", 1), ("vx", 2), ("vx", 3)]


def fill_ends(attention, m):
    at = filling_at(attention, m)
    return at.place if at is not None and at.part == FILLING[attention][at.unit][3] - 1 else None


def values_head(m):
    return (m - 8) // 4 if m >= 8 and m % 4 == 0 else None


def make_plan():
    p = Plan()
    p.t_units("fa", "D", groups=1)
    p.t_units("qa", "AD")
    p.t_units("ka", "AD")
    p.m_units("va", "AD")
    p.attention("fox_pv", "AD", 32, 1, "fox")
    p.t_units("qb", "AD", 2)
    p.t_units("kb", "AD", 2)
    p.m_units("vb", "AD")
    p.attention("diff_pv", "A", 16, 1, "diff")
    p.group("subln", "A", 4)
    for _ in range(4):
        p.t_units("gates", "A", 2)
        p.t_units("gates", "D", groups=4)
    p.m_units("out1", "AD", 2)
    p.group("bias", "D")
    p.t_units("glr", "A", groups=1)
    p.t_units("qg", "A")
    p.group("gup", "D", 2)
    p.t_units("kg", "A")
    p.m_units("vg", "A")
    p.group("cross", "A", 8)
    for lev in range(len(LEVELS) + 1):
        p.group("levels", "D", 4)
        if lev % 2 == 1:
            p.group("rg", "A")
        if lev % 4 == 3:
            p.unit("rg")
    p.group("gla_pv", "A", 4)
    p.group("gnorm", "A", 4)
    p.t_units("qa2", "AD")
    p.t_units("ka2", "AD")
    p.m_units("va2", "AD")
    p.attention("moba_pv", "AD", 32, 1, "moba")
    p.t_units("out2", "D", 2, groups=4)
    p.t_units("kx", "AD", 4)
    p.m_units("vx", "AD", 2, tiles=2)
    p.t_units("xq", "AD", 2)
    p.attention("x_pv", "AD", 16, 2, "x")
    p.t_units("xo_b", "D", 2, groups=4)
    for _ in range(FF_CHUNKS):
        p.t_units("mlp", "AD", 4)
        p.m_units("mlp", "D", 2)
    return p


PLAN = make_plan()
S0 = {"fox": 0, "diff": 32, "moba": 64, "x": 96}
R0 = {"norm1": 0, "fox": 8, "diff": 40, "mix": 56, "moba": 64, "mem": 96, "nx": 100, "x": 108, "nmlp": 124}
H0 = {"norm1": 0, "mix": 4, "mem": 8, "nx": 10, "nmlp": 14}
Q0 = {"norm1": 0, "mix": 4, "mem": 8, "nx": 10, "nmlp": 14, "final": 18}
V0 = {"fox": 0, "diff": 32, "moba": 48, "x": 80}
N0 = {"norm1": 0, "mix": 4, "mem": 8, "nx": 10, "nmlp": 14, "final": 18, "post": 22}


def shape_constants():
    half = HD // 2
    inv_freq = np.float32(10000.0) ** (-np.arange(0, HD, 2, dtype=np.float32) / np.float32(HD))
    angle = (np.arange(T, dtype=np.float32)[None, :] * inv_freq.astype(np.float32)[:, None]).astype(np.float64)
    rope_cos = np.tile(np.cos(angle), (P // half, 1)).astype(np.float32)
    rope_sin = np.tile(np.concatenate([-np.sin(angle), np.sin(angle)]), (P // HD, 1)).astype(np.float32)
    dist = np.maximum(256 - np.arange(BIAS_COLS), 0)
    large = 16 + (np.log(np.maximum(dist, 1).astype(np.float32) / np.float32(16)) / np.float32(math.log(128 / 16))
                  * np.float32(16)).astype(np.int32)
    bucket = np.where(dist < 16, dist, np.minimum(large, 31))
    one_hot = (np.arange(32)[:, None] == bucket[None, :]).astype(np.float32)
    j, i = np.arange(P)[:, None], np.arange(P)[None, :]
    masks = [(j // (2 * s) == i // (2 * s)) & (j % (2 * s) < s) & (i % (2 * s) >= s) for s in LEVELS] + [j == i]
    level_masks = np.stack(masks, axis=1).astype(np.int32)
    return {"rope_cos": rope_cos, "rope_sin": rope_sin, "bucket_one_hot": one_hot, "level_masks": level_masks}


class Offsets:

    def __init__(self, unit=0, step=0, act=0, dve=0):
        self.unit, self.step, self.act, self.dve = unit, step, act, dve


HERE = Offsets()


def gate_offsets(i):
    return Offsets(unit=i * 6, step=i * 16, act=i * 8, dve=i * 8)


def mlp_offsets(i):
    return Offsets(unit=i * 8, step=i * 18, act=i * 8, dve=i * 16)


def two_blocks_kernel(nc, a, out):
    w_in = a["w_in"][0]
    w_in_2 = a["w_in_2"][0]
    w_branch = a["w_branch"].rearrange("l b w d -> (l b w) d")
    w_out = a["w_out"][0]
    w_out_2 = a["w_out_2"][0]
    w_xq, w_xkv, w_xo = a["w_xq_2"][0], a["w_xkv_2"][0], a["w_xo_2"][0]
    w_up, w_down = a["w_up_2"][0], a["w_down_2"][0]
    x_in = a["x"].rearrange("b (t p) d -> p (b t) d", p=P)
    mem_in = a["mem_2"].rearrange("b (t p) d -> p (b t) d", p=P)
    x_out = out.rearrange("b (t p) d -> p (b t) d", p=P)
    x1_dram = a["x1_dram"].rearrange("(t p) d -> p t d", p=P)
    bias_dram = a["bias_dram"]
    G, K_, ST, AN, DN = PLAN.groups, PLAN.kind, PLAN.group_step, PLAN.act_n, PLAN.dve_n
    U = PLAN.units

    with ExitStack() as ctx:
        def region(*sets):
            made, size = {}, 0
            for bufs in sets:
                with ExitStack() as one:
                    used = 0
                    for name, shape, dt in bufs:
                        made[name] = one.enter_context(nc.sbuf_tensor(name, shape, dt))
                        used += math.prod(shape[1:]) * {F32: 4, F32R: 4, BF16: 2, I32: 4}[dt]
                    size = max(size, used)
            ctx.enter_context(nc.sbuf_tensor(f"region_of_{sets[0][0][0]}", [P, (size + 31) // 32 * 8], F32))
            return made

        def sb(name, shape, dt):
            return ctx.enter_context(nc.sbuf_tensor(name, shape, dt))

        def sem(name):
            return ctx.enter_context(nc.semaphore(name))

        w_raw = [sb(f"w_raw{i}", [P, 2048], F32) for i in range(2)]
        w_hi = [sb(f"w_hi{i}", [P, 2048], F32R) for i in range(2)]
        w_lo = [sb(f"w_lo{i}", [P, 2048], F32R) for i in range(2)]
        B = {}
        act8 = [P, KT, T]
        B |= region(
            [("h_hi", act8, F32R), ("h_lo", act8, F32R)],
            [("yg_hi", [P, 4, T], F32R), ("yg_lo", [P, 4, T], F32R), ("x_acc", [P, NT, D], F32)])
        B |= region(
            [("q_st", act8, F32R), ("k_hh", act8, F32R), ("k_lo", [P, 4, T], F32R),
             ("v_hl", [P, NT, 2 * T], F32R), ("z_b", [P, 4, T], F32)],
            [("y_hi", act8, F32R), ("y_lo", act8, F32R), ("m_hi", act8, F32R), ("m_lo", act8, F32R)],
            [("g_q", [P, 2, T], F32), ("g_k", [P, 2, T], F32), ("g_b", [P, 2, T], F32), ("g_d", [P, 2, 2, T], F32),
             ("g_z", [P, 2, 2, T], F32), ("g_qe", [P, 2, T], F32), ("g_kd", [P, 2, T], F32),
             ("g_kx", [P, 2, 3, P], F32), ("g_v", [P, NT, T], F32), ("g_keep", [P, T], F32),
             ("g_mask", [P, len(LEVELS) + 1, P], I32), ("g_up", [P, 256], F32), ("g_lr", [P, T], F32),
             ("g_x", [P, 2, T], F32), ("beta", [P, BIAS_COLS], F32), ("one_hot", [P, BIAS_COLS], F32)],
            [("xq_hi", act8, F32R), ("xq_lo", act8, F32R), ("xk_hi", [P, KT, MEM], F32R),
             ("xk_lo", [P, KT, MEM], F32R), ("xv_hi", [P, 2, D], F32R), ("xv_lo", [P, 2, D], F32R)],
            [("u_hi", act8, F32R), ("u_lo", act8, F32R)])
        small = [P, T]
        B |= region(
            [("pt_hi", [P, 2, PT_COLS], F32R), ("pt_lo", [P, 2, PT_COLS], F32R), ("p0", [P, P_COLS], F32),
             ("px", [P, P_COLS + 2 * T], F32)],
            [("x_m", [P, NT, D], F32), ("h_m", [P, 2, D], F32), ("y_m", [P, NT, D], F32)],
            [("rope_c", small, F32), ("rope_s", small, F32), ("t_a", [P, 2, T], F32), ("t_b", [P, 2, T], F32),
             ("t_c", [P, 2, T], F32), ("t_sq", [P, 2, T], F32), ("t_r", [P, 2, T], F32), ("t_g", [P, 4, T], F32)],
            [("g_a", [P, 4, PT_COLS], F32)],
            [("h_m2", [P, 2, D], F32), ("gain2", [P, 2, D], F32), ("junk2", [P, D], BF16),
             ("mem_hi", [P, KT, MEM], F32R), ("mem_lo", [P, KT, MEM], F32R)],
            [("pad_x", [P, 4608], F32), ("xpt_hi", [P, 2, 2 * T], F32R), ("xpt_lo", [P, 2, 2 * T], F32R),
             ("xp", [P, NT, MEM], F32)],
            [("pad_f", [P, 4608], F32), ("relu", [P, 2, T], F32), ("u_f", [P, 2, T], F32)])
        B |= region(
            [("y_0", [P, NT, T], F32), ("y_1", [P, NT, T], F32)],
            [("gain", [P, 2, D], F32), ("junk", [P, D], BF16), ("junk_y", [P, T], BF16), ("lam_v", [P, 4, HD], F32)],
            [("x_res", [P, NT, D], F32)])
        ident = sb("ident", [P, P], F32)
        flip = sb("flip", [P, P], F32)
        ones = sb("ones", [P, P], F32)
        ident_b = sb("ident_b", [P, P], BF16)
        future_b = sb("future_b", [P, P], BF16)
        pick = sb("pick", [P, 8], F32R)
        c_row = sb("c_row", [P, T], F32R)
        b_forget = sb("b_forget", [P, 1], F32)
        g_subln = sb("g_subln", [P, 1], F32)
        b_gate = sb("b_gate", [P, 2], F32)
        g_gain = sb("g_gain", [P, 1], F32)
        rp_table = sb("rp_table", [P, 8], F32)
        lam_d = sb("lam_d", [P, 2], F32)
        lam_e = sb("lam_e", [P, 2], F32)
        neg_lam = sb("neg_lam", [P, 1], F32)
        minus_half = sb("minus_half", [P, 1], F32)
        eps_n = sb("eps_n", [P, 2], F32)
        sumsq = sb("sumsq", [P, 26, 2], F32)
        var = sb("var", [P, 26], F32)
        rstd = sb("rstd", [P, 26], F32)
        neg_max = sb("neg_max", [P, 112], F32)
        denom = sb("denom", [P, 112], F32)
        rden = sb("rden", [P, 112], F32)
        g_tail = sb("g_tail", [P, 2, NT], F32)

        lin = ctx.enter_context(nc.psum_tensor("lin", [P, 4, T], F32))
        sc = ctx.enter_context(nc.psum_tensor("sc", [P, 2, T], F32))
        tr = ctx.enter_context(nc.psum_tensor("tr", [P, 2, T], F32))

        w_loaded = [sem(f"w_loaded{i}") for i in range(2)]
        w_slot_free = sem("w_slot_free")
        w_claimed = sem("w_claimed")
        w_split = sem("w_split")
        w_scalar_hi = sem("w_scalar_hi")
        lin_step = sem("lin_step")
        act_evac = sem("act_evac")
        dve_evac = sem("dve_evac")
        consts_made = sem("consts_made")
        small_in = sem("small_in")
        x_in_s = [sem(f"x_in{t}") for t in range(NT)]
        sq_done = sem("sq_done")
        var_done = sem("var_done")
        rstd_done = sem("rstd_done")
        h_ready = sem("h_ready")
        tr_done = sem("tr_done")
        tr_hi = sem("tr_hi")
        tr_lo = sem("tr_lo")
        s_done = sem("s_done")
        s_max = sem("s_max")
        s_exp = sem("s_exp")
        s_rec = sem("s_rec")
        s_norm = sem("s_norm")
        pd_done = sem("pd_done")
        y_norm = sem("y_norm")
        dve_self = sem("dve_self")
        act_self = sem("act_self")
        pool_self = sem("pool_self")
        small_in2 = sem("small_in2")
        gain_in = [sem(f"gain_in{i}") for i in range(6)]
        lam_exp = sem("lam_exp")
        lam_ready = sem("lam_ready")
        fa_ln = sem("fa_ln")
        c_ready = sem("c_ready")
        rg_silu = sem("rg_silu")
        za_silu = sem("za_silu")
        zb_silu = sem("zb_silu")
        ya_gated = sem("ya_gated")
        yb_gated = sem("yb_gated")
        rope_in = sem("rope_in")
        rot_mul = sem("rot_mul")
        rope_done = sem("rope_done")
        rope_hi = sem("rope_hi")
        rope_lo = sem("rope_lo")
        sq_t = sem("sq_t")
        y_hi_s = sem("y_hi_s")
        y_lo_s = sem("y_lo_s")
        mg_sum = sem("mg_sum")
        mg_hi = sem("mg_hi")
        mg_lo = sem("mg_lo")
        x_again = sem("x_again")
        post_var = sem("post_var")
        post_root = sem("post_root")
        x1_ready = sem("x1_ready")
        x1_parked = sem("x1_parked")
        x1_back = sem("x1_back")
        gla_in = sem("gla_in")
        gla_const = sem("gla_const")
        beta_ready = sem("beta_ready")
        beta_out = sem("beta_out")
        bias_in = sem("bias_in")
        gla_ln = sem("gla_ln")
        gd_done = sem("gd_done")
        ge_done = sem("ge_done")
        gz_done = sem("gz_done")
        mem_in_s = sem("mem_in_s")
        u_hi_s = sem("u_hi_s")
        u_lo_s = sem("u_lo_s")
        final_ready = sem("final_ready")
        out_done = sem("out_done")

        def as_f32(ap):
            return ap.bitcast(F32)

        def blocks(buf, slot, i):
            base = buf[:, slot, P * i:P * i + P]
            return bass.AP(base.tensor, base.offset, [list(base.ap[0]), [PT_STRIDE, i + 1], [1, P]])

        def diagonal(buf, slot):
            return buf[:, slot, :].rearrange("p (a b) -> p a b", b=P)[:, 0:13:4, :]

        bias_tiles = B["px"][:, 0:8 * 256].rearrange("p (h c) -> p h c", h=8)
        fox_tmp = B["px"][:, P_COLS:P_COLS + 2 * T].rearrange("p (s t) -> p s t", s=2)

        def t_source(w, c0, width=256):
            return w[:, c0:c0 + width].rearrange("(k p) n -> p k n", p=P)

        def m_source(w, c0, n):
            r, c = T * (n % 2), c0 + T * (n // 2)
            return w[r:r + T, c:c + T].rearrange("(k p) n -> p k n", p=P)

        def source(name, n):
            if name in ("fa", "glr"):
                return t_source(*((w_in, C1[name]) if name == "fa" else (w_in_2, C2[name])), P)
            if name in ("qa", "ka", "za", "qb", "kb", "zb"):
                return t_source(w_in, C1[name] + 256 * n)
            if name in ("qg", "kg", "rg", "qa2", "ka2"):
                return t_source(w_in_2, C2[name[0:2]] + 256 * n)
            if name in ("out2g", "out2"):
                r = T if name == "out2g" else 0
                return w_out_2[r:r + T, T * n:T * n + T].rearrange("(k p) n -> p k n", p=P)
            if name in ("xo_a", "xo_b"):
                r = 0 if name == "xo_a" else T
                return w_xo[r:r + T, T * n:T * n + T].rearrange("(k p) n -> p k n", p=P)
            if name in ("kx", "xq"):
                return t_source(w_xkv if name == "kx" else w_xq, 256 * n)
            w, c0 = {"va": (w_in, C1["va"]), "vb": (w_in, C1["vb"]), "out1": (w_out, 0), "vg": (w_in_2, C2["vg"]),
                     "va2": (w_in_2, C2["va"]), "vx": (w_xkv, D)}[name]
            return m_source(w, c0, n)

        assert U["mlp"][0] % 2 == 0 and U["gates"][0] % 2 == 1

        block = ctx.enter_context(nc.Block())

        @block.sync
        def _(sp):
            def load_unit(u, src, off=None):
                if u >= 2:
                    sp.wait_ge(w_split, 2 * (u - 1) + 2 * (off or HERE).unit)
                if off is not None:
                    sp.sem_inc(w_slot_free, 1)
                k, n = src.shape[1], src.shape[2]
                dst = w_raw[u % 2][:, 0:k * n].rearrange("p (k n) -> p k n", k=k)
                sp.dma_start(dst, src).then_inc(w_loaded[u % 2], 16)

            for t in range(NT):
                sp.dma_start(B["x_m"][:, t, :], x_in[:, t, :]).then_inc(x_in_s[t], 16)
            for u in range(U["gates"][0]):
                load_unit(u, source(*PLAN.unit_name[u]))
            with sp.Fori(0, 2) as i:
                off = gate_offsets(i)
                for c in range(2):
                    for n, w, c0 in ((0, w_in, C1["gA"]), (1, w_in, C1["gB"]), (2, w_branch, 0)):
                        cols = bass.ds(i * 512 + (c0 + 256 * c), 256)
                        load_unit(U["gates"][3 * c + n], w[:, cols].rearrange("(k p) n -> p k n", p=P), off)
            for u in range(U["out1"][0], U["mlp"][0]):
                load_unit(u, source(*PLAN.unit_name[u]))
            with sp.Fori(0, FF_CHUNKS) as i:
                off = mlp_offsets(i)
                for c in range(4):
                    cols = bass.ds(i * D + 256 * c, 256)
                    load_unit(U["mlp"][c], w_up[:, cols].rearrange("(k p) n -> p k n", p=P), off)
                for j in range(2):
                    for kh in range(2):
                        rows = bass.ds(i * D + T * kh, T)
                        src = w_down[rows, T * j:T * j + T].rearrange("(k p) n -> p k n", p=P)
                        load_unit(U["mlp"][4 + 2 * j + kh], src, off)
            for t in range(NT):
                sp.wait_ge(final_ready, t + 1)
                sp.dma_start(x_out[:, t, :], B["x_res"][:, t, :]).then_inc(out_done, 16)
            sp.wait_ge(out_done, 16 * NT)
            sp.wait_ge(x1_parked, 16 * NT)
            sp.wait_ge(beta_out, 16)

        @block.gpsimd
        def _(pool):
            own = [0]

            def link(ins):
                own[0] += 1
                ins.then_inc(pool_self, 1)
                pool.wait_ge(pool_self, own[0])

            def unit_cols(u):
                return KT * P if PLAN.unit_name[u][0] in ("fa", "glr") else 2048

            def split_piece(u, n):
                if n == 0:
                    pool.wait_ge(w_loaded[u % 2], 16 * (u // 2 + 1))
                    pool.wait_ge(lin_step, PLAN.unit_last_step[u - 2])
                if n == 4:
                    pool.wait_ge(w_split, 2 * u + 1)
                c = slice(T * (n % 4), T * (n % 4) + T)
                raw, hi, lo = (b[u % 2][:, c] for b in (w_raw, w_hi, w_lo))
                if n < 4:
                    ins = pool.tensor_scalar(hi, raw, 1.0, 1.0, ALU.mult, ALU.mult)
                else:
                    ins = pool.tensor_tensor(lo, raw, as_f32(hi), ALU.subtract)
                if n % 4 == 3:
                    ins.then_inc(w_split, 1)

            def split_between(tiles, jobs, norm):
                for m in range(tiles):
                    norm(m)
                    for u, first, pieces in jobs:
                        k = m - first
                        if 0 <= k < len(pieces):
                            for n in range(sum(pieces[:k]), sum(pieces[:k + 1])):
                                split_piece(u, n)

            def split_unit(u, off=None, left=None):
                o = off or HERE
                pool.wait_ge(w_loaded[u % 2], 16 * (u // 2 + 1) + o.unit * 8)
                if u >= 2:
                    pool.wait_ge(lin_step, (left or PLAN.unit_last_step[u - 2]) + o.step)
                if off is not None:
                    pool.sem_inc(w_claimed, 1)
                by_scalar = PLAN.unit_name[u] in HI_BY_SCALAR
                raw, hi, lo = (b[u % 2][:, 0:unit_cols(u)] for b in (w_raw, w_hi, w_lo))
                if by_scalar:
                    pool.wait_ge(w_scalar_hi, HI_BY_SCALAR.index(PLAN.unit_name[u]) + 1)
                    pool.tensor_tensor(lo, raw, as_f32(hi), ALU.subtract).then_inc(w_split, 2)
                    return
                pool.tensor_scalar(hi, raw, 1.0, 1.0, ALU.mult, ALU.mult).then_inc(w_split, 1)
                pool.wait_ge(w_split, 2 * u + 1 + o.unit * 2)
                pool.tensor_tensor(lo, raw, as_f32(hi), ALU.subtract).then_inc(w_split, 1)

            def root(n):
                pool.wait_ge(var_done, n + 1)
                pool.tensor_tensor(rstd[:, n:n + 1], var[:, n:n + 1], minus_half[:, :], ALU.pow)\
                    .then_inc(rstd_done, 1)

            def normalise(v, s, p):
                pool.wait_ge(s_rec, v + 1)
                pool.tensor_scalar(p, p, rden[:, s:s + 1], 1.0, ALU.mult, ALU.mult).then_inc(s_norm, 1)

            for buf, value in ((ident[:, :], 0.0), (flip[:, :], 0.0), (ones[:, :], 1.0), (ident_b[:, :], 0.0),
                               (future_b[:, :], 0.0), (as_f32(c_row[:, :]), 0.0), (minus_half[:, :], -0.5),
                               (eps_n[:, 0:1], SUBLN_EPS), (eps_n[:, 1:2], EPS)):
                link(pool.memset(buf, value))
            for buf, sign, base in ((ident, -1, 0), (flip, 1, 1 - P), (ident_b, -1, 0)):
                link(pool.affine_select(out=buf[:, :], in_=buf[:, :], compare_op=ALU.not_equal, fill=1.0,
                                        base=base, pattern=[[sign, P]], channel_multiplier=1))
            pool.affine_select(out=future_b[:, :], in_=future_b[:, :], compare_op=ALU.is_ge, fill=FAR, base=0,
                               pattern=[[-1, P]], channel_multiplier=1).then_inc(consts_made, 1)

            for t in range(NT):
                root(N0["norm1"] + t)
            split_unit(0)
            for u in range(1, U["qa"][1] + 1):
                split_unit(u)

            def causal_norm(name):
                def f(m):
                    i, n = m % 4, P * (m % 4 + 1)
                    normalise(V0[name] + m, S0[name] + m, B["p0"][:, P_OFF[i]:P_OFF[i] + n])
                return f

            split_between(32, [(U["ka"][1] + n, 8 * n, (2, 2, 1, 1, 1, 1)) for n in range(4)], causal_norm("fox"))
            split_unit(U["qb"][1])
            for c in range(8):
                pool.wait_ge(act_evac, AN[G["qb"][0] + c])
                if c == 0:
                    pool.wait_ge(rope_in, 32)
                t_b = B["t_b"][:, c % 2, :]
                pool.tensor_tensor(t_b, t_b, B["rope_s"][:, :], ALU.mult).then_inc(rot_mul, 1)
                if c % 2 == 1:
                    split_unit(U["kb"][0] + c // 2)
            split_unit(U["zb"][0])

            def diff_norm(w):
                i, n = w % 4, P * (w % 4 + 1)
                normalise(V0["diff"] + w, S0["diff"] + 2 * w, B["p0"][:, P_OFF[i]:P_OFF[i] + n])

            split_between(16, [(U["zb"][1] + n, 8 * n, (2, 2, 1, 1, 1, 1)) for n in range(2)], diff_norm)
            with pool.Fori(0, 2) as it:
                for c in range(1, 7):
                    split_unit(U["gates"][c], off=gate_offsets(it),
                               left=ST[G["subln"][3]] if c == 1 else None)
            for u in range(U["out1"][1], U["glr"][0] + 1):
                split_unit(u)
            for n in range(NT + 2):
                if n < NT:
                    r = N0["post"] + n
                    pool.wait_ge(post_var, n + 1)
                    pool.tensor_tensor(rstd[:, r:r + 1], var[:, r:r + 1], minus_half[:, :], ALU.pow)\
                        .then_inc(post_root, 1)
                if 0 <= n - 2 < NT:
                    root(N0["mix"] + n - 2)
            split_unit(U["glr"][0] + 1)
            pool.wait_ge(lin_step, ST[G["out1"][7]])
            link(pool.memset(B["g_keep"][:, :], 1.0))
            link(pool.memset(B["g_keep"][:, 0:T:P], 0.0))
            pool.wait_ge(x1_parked, 16 * NT)
            pool.wait_ge(tr_done, R0["mix"] + 8)
            for h in range(4):
                ins = pool.memset(diagonal(B["g_a"], h), 0.0)
            ins.then_inc(gla_const, 1)
            for u in range(U["glr"][0] + 2, U["qa2"][1] + 1):
                split_unit(u)
            split_between(32, [(U["ka2"][1] + n, 8 * n, (2, 2, 1, 1, 1, 1)) for n in range(3)]
                          + [(U["out2"][0], 29, (3, 3, 2))], causal_norm("moba"))
            for t in range(2):
                root(N0["mem"] + t)
            split_unit(U["out2"][1])
            split_unit(U["kx"][0])
            for t in range(3):
                root(N0["nx"] + t)
            split_unit(U["kx"][1])
            root(N0["nx"] + 3)
            for u in range(U["kx"][2], U["xq"][2] + 1):
                split_unit(u)

            def x_norm(m):
                normalise(V0["x"] + m, S0["x"] + m, B["xp"][:, m % 4, :])

            split_between(13, [(U["xq"][3] + n, first, (3, 3, 2)) for n, first in enumerate((0, 4, 10))], x_norm)
            for m in range(13, 16):
                x_norm(m)
            for u in range(U["xo_b"][0], U["mlp"][1]):
                split_unit(u)
            for t in range(NT):
                root(N0["nmlp"] + t)
            split_unit(U["mlp"][1])
            with pool.Fori(0, FF_CHUNKS - 1) as it:
                for c in range(2, 10):
                    split_unit(U["mlp"][c], off=mlp_offsets(it))
            for c in range(2, 8):
                split_unit(U["mlp"][8 * (FF_CHUNKS - 1) + c])
            for t in range(NT):
                root(N0["final"] + t)

        @block.tensor
        def _(pe):
            def bank(g, cols=T):
                return lin[:, g % 4, 0:cols]

            def claim(g, off=HERE):
                k = g - 4
                if k < 0:
                    return
                if "D" in K_[k]:
                    pe.wait_ge(dve_evac, DN[k] + off.dve)
                else:
                    pe.wait_ge(act_evac, AN[k] + off.act)

            def three(o, lh, ll, rh, rl, start, stop):
                pe.matmul(o, lh, rh, start=start, stop=False)
                pe.matmul(o, lh, rl, start=False, stop=False)
                return pe.matmul(o, ll, rh, start=False, stop=stop)

            def t_product(name, n, k0, k1, rh, rl, off=HERE, per_unit=2, cols=T):
                g, u, c = G[name][n], U[name][n // per_unit], slice(P * (n % per_unit), P * (n % per_unit) + P)
                if k0 == 0:
                    claim(g, off)
                    pe.wait_ge(w_split, 2 * u + 2 + off.unit * 2)
                wh, wl = (b[u % 2][:, 0:KT * P * per_unit].rearrange("p (k n) -> p k n", k=KT) for b in (w_hi, w_lo))
                for k in range(k0, k1):
                    mm = three(bank(g, cols), wh[:, k, c], wl[:, k, c], rh[:, k, 0:cols], rl[:, k, 0:cols],
                               k == 0, k == KT - 1)
                if k1 == KT:
                    mm.then_inc(lin_step, 1)

            def gate_group(unit, group, n, off):
                g, u, c = G["gates"][group], U["gates"][unit], slice(P * n, P * n + P)
                if group < 4:
                    pe.wait_ge(act_evac, AN[g - 4] + off.act)
                    pe.wait_ge(dve_evac, DN[G["subln"][3]] - 3 + group + off.dve)
                else:
                    claim(g, off)
                pe.wait_ge(w_split, 2 * u + 2 + off.unit * 2)
                wh, wl = (b[u % 2][:, :].rearrange("p (k n) -> p k n", k=KT) for b in (w_hi, w_lo))
                for k in range(KT):
                    mm = three(bank(g), wh[:, k, c], wl[:, k, c], hh[:, k, :], hl[:, k, :], k == 0, k == KT - 1)
                mm.then_inc(lin_step, 1)

            def m_product(name, n, k0, k1, lh, ll, first_k=0, ready=lambda k: None):
                g, u, c = G[name][n], U[name][n // 4], slice(P * (n % 4), P * (n % 4) + P)
                if k0 == 0:
                    claim(g)
                    pe.wait_ge(w_split, 2 * u + 2)
                wh, wl = (b[u % 2][:, :].rearrange("p (k n) -> p k n", k=4) for b in (w_hi, w_lo))
                for k in range(k0, k1):
                    ready(k)
                    f = first_k + k
                    mm = three(bank(g), lh[:, f, c], ll[:, f, c], wh[:, k, :], wl[:, k, :], k == 0, k == 3)
                if k1 == 4:
                    mm.then_inc(lin_step, 1)

            def t_groups(name, n0, n1, rh, rl, **kw):
                for n in range(n0, n1):
                    t_product(name, n, 0, KT, rh, rl, **kw)

            def branch_unit(u, g, off):
                pe.wait_ge(w_split, 2 * u + 2 + off.unit * 2)
                wh, wl = (b[u % 2][:, :].rearrange("p (k n) -> p k n", k=KT) for b in (w_hi, w_lo))
                for n in range(2):
                    for br in range(2):
                        q = g + 2 * n + br
                        claim(q, off)
                        pe.wait_ge(y_lo_s, 4 * br + 4)
                        for k in range(4 * br, 4 * br + 4):
                            c = slice(P * n, P * n + P)
                            mm = three(bank(q), wh[:, k, c], wl[:, k, c], B["y_hi"][:, k, :], B["y_lo"][:, k, :],
                                       k % 4 == 0, k % 4 == 3)
                        mm.then_inc(lin_step, 1)

            def m_pair(name, u0, g0, lh, ll, off=HERE, tiles=NT, ready=lambda kh: None):
                u, g = U[name][u0], G[name][g0]
                for kh in range(2):
                    ready(kh)
                    pe.wait_ge(w_split, 2 * (u + kh) + 2 + off.unit * 2)
                    wh, wl = (b[(u + kh) % 2][:, :].rearrange("p (k n) -> p k n", k=4) for b in (w_hi, w_lo))
                    for t in range(tiles):
                        if kh == 0:
                            claim(g + t, off)
                        for k in range(4):
                            c = slice(P * t, P * t + P)
                            f = 4 * kh + k
                            mm = three(bank(g + t), lh[:, f, c], ll[:, f, c], wh[:, k, :], wl[:, k, :],
                                       f == 0, f == 7)
                        if kh == 1 or t == tiles - 1:
                            mm.then_inc(lin_step, 1)

            def turn_tile(name, t, src):
                pe.wait_ge(h_ready, H0[name] + t + 1)
                for half in range(2):
                    r = R0[name] + 2 * t + half
                    if r >= 2:
                        pe.wait_ge(tr_lo, r - 1)
                    for b in range(4):
                        c = P * (4 * half + b)
                        mm = pe.transpose(tr[:, r % 2, P * b:P * b + P], src[:, c:c + P], ident[:, :])
                    mm.then_inc(tr_done, 1)

            def turn_probs(r, src, n):
                if r >= 2:
                    pe.wait_ge(tr_lo, r - 1)
                for j in range(n):
                    mm = pe.transpose(tr[:, r % 2, P * j:P * j + P], src(j), ident[:, :])
                mm.then_inc(tr_done, 1)

            def stacked_scores(s, h, i, extra=None):
                if s >= 2:
                    pe.wait_ge(s_exp, s - 1)
                n = P * (i + 1)
                o = sc[:, s % 2, 0:n]
                q = B["q_st"][:, h, P * i:P * i + P]
                rows = slice(64 * (h % 2), 64 * (h % 2) + 64)
                pe.matmul(o, q, B["k_hh"][:, h, 0:n], start=True, stop=False)
                extra(o, n)
                pe.matmul(o, q[rows], B["k_lo"][rows, h // 2, 0:n], start=False, stop=True).then_inc(s_done, 1)

            def heads_ready(q, k, h):
                pe.wait_ge(dve_evac, max(DN[G[q][h // 2]], DN[G[k][h // 2]]))

            def mask(o, i):
                pe.matmul(o[:, P * i:P * i + P], ident_b[:, :], future_b[:, :], start=False, stop=False)

            def p_tile(i, j):
                c = P_OFF[i] + P * j
                return B["p0"][:, c:c + P]

            def stacked_values(g, g_v, r, h):
                claim(g)
                pe.wait_ge(dve_evac, DN[g_v])
                pe.wait_ge(tr_lo, r)
                for j in range(NT):
                    c = slice(T * j, T * j + T - P * j)
                    v = B["v_hl"][:, j, P * h:P * h + P]
                    o = lin[:, g % 4, P * j:T]
                    pe.matmul(o, v, B["pt_hi"][:, h % 2, c], start=(j == 0), stop=False)
                    mm = pe.matmul(o, v, B["pt_lo"][:, h % 2, c], start=False, stop=(j == NT - 1))
                mm.then_inc(lin_step, 1)

            def attention(name, tiles, scores, turn, values):
                for m in range(tiles + 5):
                    if m < tiles:
                        scores(m)
                    if 0 <= m - 3 < tiles:
                        turn(m - 3)
                    at = filling_at(name, m)
                    if at is not None:
                        phase, n0, _, span, _ = FILLING[name][at.unit]
                        if phase == "out2g":
                            ready = (lambda k: pe.wait_ge(y_lo_s, 9 + k)) if at.place == 4 else (lambda k: None)
                            m_product(phase, n0 + at.group, 4 * at.part // span, 4 * (at.part + 1) // span,
                                      B["yg_hi"], B["yg_lo"], ready=ready)
                        elif phase == "xo_a":
                            if at.place == 4:
                                pe.wait_ge(dve_evac, DN[G["x_pv"][3]])
                            m_product(phase, n0 + at.group, 0, 4, hh, hl)
                        else:
                            t_product(phase, n0 + at.group, KT * at.part // span, KT * (at.part + 1) // span, hh, hl)
                    if values_head(m) is not None:
                        values(values_head(m))

            pe.wait_ge(consts_made, 1)
            for t in range(NT):
                turn_tile("norm1", t, B["h_m"][:, t % 2, :])
            pe.wait_ge(tr_lo, R0["norm1"] + 8)
            hh, hl = B["h_hi"], B["h_lo"]
            t_groups("fa", 0, 1, hh, hl, per_unit=1)
            for name in ("qa", "ka"):
                t_groups(name, 0, 2, hh, hl)
            m_pair("va", 0, 0, hh, hl)
            pe.wait_ge(c_ready, 1)

            def fox_scores(m):
                h, i = m // 4, m % 4
                if i == 0:
                    heads_ready("qa", "ka", h)

                def extra(o, n):
                    mask(o, i)
                    pe.matmul(o, pick[:, h:h + 1].to_broadcast([P, P]), c_row[:, 0:n], start=False, stop=False)

                stacked_scores(S0["fox"] + m, h, i, extra)

            def fox_turn(m):
                pe.wait_ge(s_norm, V0["fox"] + m + 1)
                turn_probs(R0["fox"] + m, lambda j: p_tile(m % 4, j), m % 4 + 1)

            attention("fox", 32, fox_scores, fox_turn,
                      lambda h: stacked_values(G["fox_pv"][h], G["va"][3], R0["fox"] + 4 * h + 4, h))
            for name in ("qb", "kb"):
                t_groups(name, 0, 4, hh, hl)
            m_pair("vb", 0, 0, hh, hl)

            pe.wait_ge(rope_lo, 8)
            pe.wait_ge(dve_evac, DN[G["vb"][3]])

            def diff_scores(w):
                h, i = w // 4, w % 4
                for m in range(2):
                    stacked_scores(S0["diff"] + 2 * w + m, 2 * h + m, i, lambda o, n: mask(o, i))

            def diff_turn(w):
                pe.wait_ge(pd_done, w + 1)
                turn_probs(R0["diff"] + w, lambda j: p_tile(w % 4, j), w % 4 + 1)

            def diff_values(h):
                g = G["diff_pv"][h]
                claim(g)
                pe.wait_ge(tr_lo, R0["diff"] + 4 * h + 4)
                for j in range(NT):
                    c = slice(T * j, T * j + T - P * j)
                    v = B["v_hl"][:, j, :]
                    mm = three(lin[:, g % 4, P * j:T], v[:, P * h:P * h + P], v[:, T + P * h:T + P * h + P],
                               B["pt_hi"][:, h % 2, c], B["pt_lo"][:, h % 2, c], j == 0, j == NT - 1)
                mm.then_inc(lin_step, 1)

            attention("diff", 16, diff_scores, diff_turn, diff_values)
            for h in range(4):
                g = G["subln"][h]
                claim(g)
                pe.wait_ge(sq_t, h + 1)
                pe.matmul(bank(g), ones[:, :], B["t_sq"][:, h % 2, :], start=True, stop=True).then_inc(lin_step, 1)
            with pe.Fori(0, 2) as it:
                off = gate_offsets(it)
                for c in range(2):
                    for n in range(4):
                        gate_group(3 * c + n // 2, 8 * c + n, n % 2, off)
                    branch_unit(U["gates"][3 * c + 2], G["gates"][8 * c + 4], off)
            for j in range(2):
                m_pair("out1", 2 * j, 4 * j, B["m_hi"], B["m_lo"], ready=lambda kh: pe.wait_ge(mg_lo, 4 * kh + 4))

            for t in range(NT):
                turn_tile("mix", t, B["h_m"][:, t % 2, :])
            g = G["bias"][0]
            claim(g)
            pe.wait_ge(gla_in, 48)
            pe.wait_ge(small_in, 16 * 5)
            pe.matmul(lin[0:8, g % 4, 0:BIAS_COLS], rp_table[0:32, :], B["one_hot"][0:32, :], start=True, stop=True)\
                .then_inc(lin_step, 1)
            pe.wait_ge(tr_lo, R0["mix"] + 8)
            t_groups("glr", 0, 1, hh, hl, per_unit=1)
            t_groups("qg", 0, 2, hh, hl)
            pe.wait_ge(act_evac, AN[G["glr"][0]])
            for dt in range(2):
                g = G["gup"][dt]
                claim(g)
                pe.matmul(bank(g), B["g_up"][0:16, P * dt:P * dt + P], B["g_lr"][0:16, :], start=True, stop=True)\
                    .then_inc(lin_step, 1)
            t_groups("kg", 0, 2, hh, hl)
            m_pair("vg", 0, 0, hh, hl)
            pe.wait_ge(gz_done, 1)
            for h in range(4):
                rows = slice(HD * (h % 2), HD * (h % 2) + HD)
                kd, kx, qe = B["g_kd"][rows, h // 2, :], B["g_kx"][rows, h // 2], B["g_qe"][rows, h // 2, :]
                own = [kd[:, P * j:P * j + P] for j in range(3)]
                for part, pairs in enumerate(([(own[0], 1), (kx[:, 0], 2), (kx[:, 1], 3)],
                                              [(own[1], 2), (kx[:, 2], 3), (own[2], 3)])):
                    g = G["cross"][2 * h + part]
                    claim(g)
                    for n, (key, i) in enumerate(pairs):
                        mm = pe.matmul(lin[:, g % 4, P * n:P * n + P], key, qe[:, P * i:P * i + P],
                                       start=True, stop=True)
                    mm.then_inc(lin_step, 1)
            for lev in range(len(LEVELS) + 1):
                for h in range(4):
                    g = G["levels"][4 * lev + h]
                    rows = slice(HD * (h % 2), HD * (h % 2) + HD)
                    claim(g)
                    if lev < len(LEVELS):
                        pe.wait_ge(gz_done, lev + 2)
                        key = query = B["g_z"][rows, lev % 2, h // 2, :]
                    else:
                        key, query = B["g_k"][rows, h // 2, :], B["g_q"][rows, h // 2, :]
                    for t in range(NT):
                        c = slice(P * t, P * t + P)
                        mm = pe.matmul(lin[:, g % 4, c], key[:, c], query[:, c], start=True, stop=True)
                    mm.then_inc(lin_step, 1)
                if lev % 2 == 1:
                    t_product("rg", lev // 2, 0, KT, hh, hl)
            for h in range(4):
                g = G["gla_pv"][h]
                claim(g)
                pe.wait_ge(act_evac, AN[G["cross"][2 * h + 1]])
                pe.wait_ge(dve_evac, DN[G["levels"][4 * len(LEVELS) + h]])
                for j in range(NT):
                    mm = pe.matmul(lin[:, g % 4, P * j:T], B["g_v"][:, j, P * h:P * h + P],
                                   B["g_a"][:, h, T * j:T * j + T - P * j], start=(j == 0), stop=(j == NT - 1))
                mm.then_inc(lin_step, 1)
            for h in range(4):
                g = G["gnorm"][h]
                claim(g)
                pe.wait_ge(sq_t, 4 + h + 1)
                pe.matmul(bank(g), ones[:, :], B["g_d"][:, 0, h % 2, :], start=True, stop=True).then_inc(lin_step, 1)
            for name in ("qa2", "ka2"):
                t_groups(name, 0, 2, hh, hl)
            m_pair("va2", 0, 0, hh, hl)

            pe.wait_ge(bias_in, 16)

            def moba_scores(m):
                h, i = m // 4, m % 4
                near = max(i - 1, 0)
                if i == 0:
                    heads_ready("qa2", "ka2", h)

                def extra(o, n):
                    pe.matmul(o[:, P * near:n], flip[:, :], bias_tiles[:, h, 256 - (n - P * near):256],
                              start=False, stop=False)

                stacked_scores(S0["moba"] + m, h, i, extra)

            def moba_turn(m):
                pe.wait_ge(s_norm, V0["moba"] + m + 1)
                turn_probs(R0["moba"] + m, lambda j: p_tile(m % 4, j), m % 4 + 1)

            attention("moba", 32, moba_scores, moba_turn,
                      lambda h: stacked_values(G["moba_pv"][h], G["va2"][3], R0["moba"] + 4 * h + 4, h))
            for n in range(8):
                m_product("out2", n, 0, 4, B["y_hi"], B["y_lo"],
                          ready=(lambda k: pe.wait_ge(y_lo_s, 13 + k)) if n == 0 else (lambda k: None))
                if n == 3:
                    for t in range(2):
                        turn_tile("mem", t, B["h_m2"][:, t, :])

            pe.wait_ge(tr_lo, R0["mem"] + 4)
            for t in range(NT):
                t_groups("kx", 2 * t, 2 * t + 2, B["mem_hi"], B["mem_lo"], cols=MEM)
                turn_tile("nx", t, B["h_m2"][:, t % 2, :])
            for j in range(2):
                m_pair("vx", 2 * j, 2 * j, B["mem_hi"], B["mem_lo"], tiles=2)
            pe.wait_ge(tr_lo, R0["nx"] + 8)
            t_groups("xq", 0, 4, hh, hl)

            def x_scores(m):
                h, i = m // 4, m % 4
                s = S0["x"] + m
                if i == 0:
                    pe.wait_ge(dve_evac, DN[G["xq"][2 * h + 1]])
                pe.wait_ge(s_exp, s - 1)
                for kk in range(2):
                    f = 2 * h + kk
                    c = slice(P * i, P * i + P)
                    mm = three(sc[:, s % 2, 0:MEM], B["xq_hi"][:, f, c], B["xq_lo"][:, f, c], B["xk_hi"][:, f, :],
                               B["xk_lo"][:, f, :], kk == 0, kk == 1)
                mm.then_inc(s_done, 1)

            def x_turn(m):
                pe.wait_ge(s_norm, V0["x"] + m + 1)
                turn_probs(R0["x"] + m, lambda j: B["xp"][:, m % 4, P * j:P * j + P], 2)

            def x_values(h):
                pe.wait_ge(tr_lo, R0["x"] + 4 * h + 4)
                for dv in range(2):
                    g = G["x_pv"][2 * h + dv]
                    claim(g)
                    for j in range(2):
                        c = slice(256 * h + P * dv, 256 * h + P * dv + P)
                        k = slice(T * j, T * j + T)
                        mm = three(bank(g), B["xv_hi"][:, j, c], B["xv_lo"][:, j, c], B["xpt_hi"][:, h % 2, k],
                                   B["xpt_lo"][:, h % 2, k], j == 0, j == 1)
                    mm.then_inc(lin_step, 1)

            attention("x", 16, x_scores, x_turn, x_values)
            pe.wait_ge(dve_evac, DN[G["x_pv"][7]])
            for n in range(8):
                m_product("xo_b", n, 0, 4, hh, hl, first_k=4)

            for t in range(NT):
                turn_tile("nmlp", t, B["h_m2"][:, t % 2, :])
            pe.wait_ge(tr_lo, R0["nmlp"] + 8)
            with pe.Fori(0, FF_CHUNKS) as it:
                off = mlp_offsets(it)
                t_groups("mlp", 0, 8, hh, hl, off=off)
                for j in range(2):
                    m_pair("mlp", 4 + 2 * j, 8 + 4 * j, B["u_hi"], B["u_lo"], off,
                           ready=lambda kh: pe.wait_ge(u_lo_s, it * 8 + (4 * kh + 4)))

        @block.scalar
        def _(act):
            own = [0]

            def link(ins):
                own[0] += 1
                ins.then_inc(act_self, 1)
                act.wait_ge(act_self, own[0])

            def step(g, off=HERE):
                act.wait_ge(lin_step, ST[g] + off.step)

            def bank(g, cols=T):
                return lin[:, g % 4, 0:cols]

            def after_vector(g, off=HERE):
                act.wait_ge(dve_evac, DN[g] + off.dve)

            def load(dst, src, s):
                act.dma_start(dst, src).then_inc(s, 16)

            def row(name):
                return a[name][0:1, :].partition_broadcast(P) if len(a[name].shape) == 2 else \
                    a[name].rearrange("(o d) -> o d", o=1).partition_broadcast(P)

            def column(name):
                return a[name].rearrange("l d -> d l")

            def square_sum(q, n, x, junk, half=0):
                if q > 0:
                    act.wait_ge(sq_done, q)
                act.activation(junk, x, ACT.Square, accum_out=sumsq[:, n, half:half + 1]).then_inc(sq_done, 1)

            def turned_hi(r, out):
                act.wait_ge(tr_done, r + 1)
                act.activation(out, tr[:, r % 2, :].rearrange("p (b c) -> p b c", b=4), ACT.Copy).then_inc(tr_hi, 1)

            def turned_tile_hi(name, t, buf):
                for half in range(2):
                    turned_hi(R0[name] + 2 * t + half, buf[:, 4 * half:4 * half + 4, P * t:P * t + P])

            def q_hi(x, c, scale):
                act.activation(B["q_st"][0:64, 2 * c, :], x[0:64], ACT.Copy, scale=scale)
                return act.activation(B["q_st"][64:128, 2 * c + 1, :], x[64:128], ACT.Copy, scale=scale)

            def k_hi(x, c):
                for head in range(2):
                    rows = slice(64 * head, 64 * head + 64)
                    for half in range(2):
                        ins = act.activation(B["k_hh"][64 * half:64 * half + 64, 2 * c + head, :], x[rows], ACT.Copy)
                return ins

            def exponentials(s, p, n):
                act.wait_ge(s_max, s + 1)
                act.activation(p, sc[:, s % 2, 0:n], ACT.Exp, bias=neg_max[:, s:s + 1],
                               accum_out=denom[:, s:s + 1]).then_inc(s_exp, 1)

            def probs_hi(r, m, g_pv):
                h, i = m // 4, m % 4
                act.wait_ge(tr_done, r + 1)
                if h >= 2:
                    step(g_pv[h - 2])
                act.activation(blocks(B["pt_hi"], h % 2, i),
                               tr[:, r % 2, 0:P * (i + 1)].rearrange("p (j c) -> p j c", c=P), ACT.Copy)\
                    .then_inc(tr_hi, 1)

            def attention(name, tiles, hi, exps, values, fill):
                for m in range(tiles + 6):
                    if 0 <= m - 4 < tiles:
                        hi(m - 4)
                    if m < tiles:
                        exps(m)
                    if m >= 1 and fill_ends(name, m - 1) is not None:
                        fill(fill_ends(name, m - 1))
                    if m >= 9 and m % 4 == 1:
                        values((m - 9) // 4)

            def lower_half(g, tmp):
                act.activation(tmp, lin[64:128, g % 4, :], ACT.Copy).then_inc(act_evac, 1)

            def soft_log(x, t1, t2, done):
                link(act.activation(t1, x, ACT.Abs))
                link(act.activation(t2, t1, ACT.Exp, scale=-1.0))
                act.activation(t1, t2, ACT.Ln, bias=ones[0:t1.shape[0], 0:1]).then_inc(done, 1)

            def copy_lin(g, out, scale=1.0):
                step(g)
                act.activation(out, bank(g), ACT.Copy, scale=scale).then_inc(act_evac, 1)

            def head_roots(g0, y, sq, root, eps, free):
                for h in range(4):
                    if h >= 2:
                        step(g0 + h - 2)
                    act.activation(sq[:, h % 2, :], y[:, h, :], ACT.Square).then_inc(sq_t, 1)
                for h in range(4):
                    step(g0 + h)
                    if h >= 2:
                        act.wait_ge(y_norm, free + h - 1)
                    act.activation(root[:, h % 2, :], bank(g0 + h), ACT.Sqrt, scale=1.0 / P, bias=eps)\
                        .then_inc(act_evac, 1)

            load(B["gain"][:, 0, :], row("g_pre"), gain_in[0])
            for n, name in enumerate(("lambda_q1", "lambda_k1", "lambda_q2", "lambda_k2")):
                load(B["lam_v"][:, n, :], row(name), small_in2)
            with nc.allow_non_contiguous_dma(reason="one column of a few hundred bytes each"):
                load(b_forget[0:8, :], column("b_forget"), small_in)
                load(g_subln[:, :], column("g_subln"), small_in)
                load(b_gate[:, :], a["b_gate_2"].rearrange("l (t p) -> p (l t)", p=P), small_in)
                load(g_gain[:, :], column("g_norm_2"), small_in)
            load(rp_table[0:32, :], a["rp_table_2"], small_in)

            act.wait_ge(consts_made, 1)
            link(act.activation(lam_e[:, 0:1], ones[:, 0:1], ACT.Square))
            for t in range(NT):
                act.wait_ge(x_in_s[t], 16)
                square_sum(Q0["norm1"] + t, N0["norm1"] + t, B["x_m"][:, t, :], B["junk"][:, :])
            for t in range(NT):
                turned_tile_hi("norm1", t, B["h_hi"])
            act.wait_ge(lam_ready, 1)
            act.activation(lam_e[:, :], lam_d[:, :], ACT.Exp).then_inc(lam_exp, 1)
            act.wait_ge(dve_evac, DN[G["fa"][0]])
            soft_log(B["y_0"][0:8, 0, :], B["y_0"][0:8, 1, :], B["y_0"][0:8, 2, :], fa_ln)

            def queries_hi(name, c):
                step(G[name][c])
                q_hi(bank(G[name][c]), c, HD ** -0.5).then_inc(act_evac, 1)

            def keys_hi(name, c):
                step(G[name][c])
                k_hi(bank(G[name][c]), c).then_inc(act_evac, 1)

            for c in range(2):
                queries_hi("qa", c)
            for c in range(2):
                keys_hi("ka", c)

            def v_heads(name):
                g0 = G[name][0]
                for t in range(NT):
                    step(g0 + t)
                    out = B["v_hl"][:, t, :].rearrange("p (h s d) -> p h s d", h=8, s=2)[:, :, 0, :]
                    act.activation(out, bank(g0 + t).rearrange("p (h d) -> p h d", h=8), ACT.Copy)\
                        .then_inc(act_evac, 1)

            v_heads("va")

            def causal_exps(name, r0):
                def f(m):
                    i, n = m % 4, P * (m % 4 + 1)
                    if m >= 4:
                        act.wait_ge(tr_done, R0[name] + m - 3)
                    exponentials(S0[name] + m, B["p0"][:, P_OFF[i]:P_OFF[i] + n], n)
                return f

            def stacked_out(name, tmp):
                def f(h):
                    g = G[name]
                    step(g[h])
                    if h >= 2:
                        after_vector(g[h - 2])
                    lower_half(g[h], tmp[0:64, h % 2, :])
                return f

            def fox_fill(k):
                if k < 4:
                    (queries_hi, keys_hi)[k // 2](("qa", "ka")[k // 2], 2 + k % 2)
                else:
                    copy_lin(G["za"][k - 4], B["y_1"][:, k - 4, :])

            attention("fox", 32, lambda m: probs_hi(R0["fox"] + m, m, G["fox_pv"]), causal_exps("fox", R0["fox"]),
                      stacked_out("fox_pv", fox_tmp), fox_fill)
            act.wait_ge(act_evac, AN[G["za"][3]])
            act.activation(B["y_1"][:, :, :], B["y_1"][:, :, :], ACT.Silu).then_inc(za_silu, 1)

            load(B["rope_c"][:, :], a["rope_cos"], rope_in)
            load(B["rope_s"][:, :], a["rope_sin"], rope_in)

            def rope_hi_part(c):
                act.wait_ge(rope_done, c + 1)
                x = B["t_a"][:, c % 2, :]
                ins = q_hi(x, c, HD ** -0.5) if c < 4 else k_hi(x, c - 4)
                ins.then_inc(rope_hi, 1)

            for c in range(8):
                g = G["qb"][0] + c
                step(g)
                if c >= 2:
                    act.wait_ge(rope_done, c - 1)
                for quarter in range(4):
                    rows = slice(32 * quarter, 32 * quarter + 32)
                    other = 32 * (quarter ^ 1)
                    ins = act.activation(B["t_b"][rows, c % 2, :], lin[other:other + 32, g % 4, :], ACT.Copy)
                ins.then_inc(act_evac, 1)
                if c >= 1:
                    rope_hi_part(c - 1)
            rope_hi_part(7)
            for t in range(NT):
                step(G["vb"][t])
                act.activation(B["v_hl"][:, t, 0:T], bank(G["vb"][t]), ACT.Copy).then_inc(act_evac, 1)

            def diff_exps(w):
                i, n = w % 4, P * (w % 4 + 1)
                if w >= 4:
                    act.wait_ge(tr_done, R0["diff"] + w - 3)
                for m, buf in enumerate((B["p0"], B["px"])):
                    exponentials(S0["diff"] + 2 * w + m, buf[:, P_OFF[i]:P_OFF[i] + n], n)

            def diff_fill(k):
                copy_lin(G["zb"][k], B["z_b"][:, k, :])

            def split_y(n, k):
                if n < 8:
                    act.wait_ge((ya_gated, yb_gated)[k // 4], k % 4 + 1)
                src = B["y_0"][:, k, :] if k < 4 else B["y_1"][:, k - 4, :]
                out = B["yg_hi"][:, k - 4, :] if 8 <= n < 12 else B["y_hi"][:, k, :]
                act.activation(out, src, ACT.Copy).then_inc(y_hi_s, 1)

            def diff_out(h):
                if h == 3:
                    for k in range(4):
                        split_y(k, k)
                if h == 0:
                    act.wait_ge(ya_gated, 4)
                copy_lin(G["diff_pv"][h], B["y_1"][:, h, :])

            attention("diff", 16, lambda w: probs_hi(R0["diff"] + w, w, G["diff_pv"]), diff_exps, diff_out, diff_fill)
            head_roots(G["subln"][0], B["y_1"], B["t_sq"], B["t_r"], eps_n[:, 0:1], 0)
            act.activation(B["z_b"][:, :, :], B["z_b"][:, :, :], ACT.Silu).then_inc(zb_silu, 1)

            for k in range(4, 8):
                split_y(k, k)
            with act.Fori(0, 2) as it:
                off = gate_offsets(it)
                for c in range(2):
                    g = G["gates"][8 * c]
                    for n in range(4):
                        act.wait_ge(lin_step, ST[g + n] + off.step)
                        act.wait_ge(dve_evac, DN[g - 1] + off.dve)
                        act.activation(B["t_g"][:, n, :], bank(g + n), ACT.Sigmoid).then_inc(act_evac, 1)
                    for n in range(2):
                        act.wait_ge(mg_sum, it * 4 + (2 * c + n + 1))
                        act.activation(B["m_hi"][:, bass.ds(it * 4 + (2 * c + n), 1), :],
                                       B["t_c"][:, n:n + 1, :], ACT.Copy).then_inc(mg_hi, 1)

            act.wait_ge(y_lo_s, 8)
            load(B["gain"][:, 0, :], row("g_post"), gain_in[1])
            load(B["gain"][:, 1, :], row("norm_mix_2"), gain_in[2])
            act.wait_ge(mg_lo, 8)
            for t in range(NT):
                load(B["x_m"][:, t, :], x_in[:, t, :], x_again)

            def out_tile(j, t):
                g = G["out1"][4 * j + t]
                step(g)
                act.wait_ge(act_evac, AN[g] - 1)
                act.activation(B["junk_y"][:, :], bank(g), ACT.Square,
                               accum_out=sumsq[:, N0["post"] + t, j:j + 1]).then_inc(act_evac, 1)

            for t in range(NT):
                out_tile(0, t)
            for n in range(NT + 4):
                if n < NT:
                    out_tile(1, n)
                if n == NT:
                    load(B["one_hot"][0:32, :], a["bucket_one_hot"], gla_in)
                    load(B["g_up"][0:16, :], a["w_gate_up_2"][0], gla_in)
                    load(B["g_mask"][:, :, :], a["level_masks"], gla_in)
                if 0 <= n - 2 < NT:
                    t = n - 2
                    act.wait_ge(x1_ready, t + 1)
                    square_sum(Q0["mix"] + t, N0["mix"] + t, B["x_m"][:, t, :], B["junk"][:, :])
                    act.dma_start(x1_dram[:, t, :], B["x_m"][:, t, :]).then_inc(x1_parked, 16)
                if 0 <= n - 4 < NT:
                    turned_tile_hi("mix", n - 4, B["h_hi"])
            act.wait_ge(beta_ready, 1)
            act.dma_start(bias_dram, B["beta"][0:8, :]).then_inc(beta_out, 16)
            act.wait_ge(beta_out, 16)
            with nc.allow_non_contiguous_dma(reason="overlapping rows: entry (p, c) is distance entry 1 + p + c"):
                act.dma_start(bias_tiles, bass.AP(bias_dram.tensor, 1, [[1, P], [BIAS_COLS, 8], [1, 256]]))\
                    .then_inc(bias_in, 16)
            step(G["glr"][0])
            act.activation(B["g_lr"][0:16, :], lin[0:16, G["glr"][0] % 4, :], ACT.Copy).then_inc(act_evac, 1)
            for c in range(2):
                copy_lin(G["qg"][c], B["g_q"][:, c, :], HD ** -0.5)
            act.wait_ge(dve_evac, DN[G["gup"][1]])
            soft_log(B["g_x"][:, :, :], B["g_d"][:, 0], B["g_d"][:, 1], gla_ln)
            for c in range(2):
                copy_lin(G["kg"][c], B["g_k"][:, c, :])

            def level_exp(lev):
                act.wait_ge(gd_done, lev + 3)
                d = B["g_d"][:, lev % 2]
                act.activation(d, d, ACT.Exp).then_inc(ge_done, 1)

            for n in range(2):
                act.wait_ge(gd_done, n + 1)
                act.activation(B["g_d"][:, n], B["g_d"][:, n], ACT.Exp).then_inc(ge_done, 1)
            act.activation(g_tail[:, :, :], B["g_b"][:, :, P - 1:T:P], ACT.Exp).then_inc(ge_done, 1)
            for lev in range(2):
                level_exp(lev)
            for t in range(NT):
                copy_lin(G["vg"][t], B["g_v"][:, t, :])
            for lev in range(2, 4):
                level_exp(lev)
            act.wait_ge(gla_const, 1)
            for h in range(4):
                g = G["cross"][2 * h]
                step(g)
                act.activation(B["g_a"][:, h, P:4 * P], lin[:, g % 4, 0:3 * P], ACT.Copy).then_inc(act_evac, 1)
                step(g + 1)
                c = PT_STRIDE + 2 * P
                act.activation(B["g_a"][:, h, c:c + 2 * P], lin[:, (g + 1) % 4, 0:2 * P], ACT.Copy)
                c = 2 * PT_STRIDE + 3 * P
                act.activation(B["g_a"][:, h, c:c + P], lin[:, (g + 1) % 4, 2 * P:3 * P], ACT.Copy)\
                    .then_inc(act_evac, 1)
            for lev in range(len(LEVELS) + 1):
                if lev + 4 < len(LEVELS):
                    level_exp(lev + 4)
                if lev % 2 == 1:
                    copy_lin(G["rg"][lev // 2], B["y_0"][:, lev // 2, :])
            act.wait_ge(act_evac, AN[G["rg"][3]])
            act.activation(B["y_0"][:, :, :], B["y_0"][:, :, :], ACT.Silu).then_inc(rg_silu, 1)
            for h in range(4):
                copy_lin(G["gla_pv"][h], B["y_1"][:, h, :])
            act.wait_ge(act_evac, AN[G["gla_pv"][3]])
            head_roots(G["gnorm"][0], B["y_1"], B["g_d"][:, 0], B["g_d"][:, 1], eps_n[:, 1:2], 4)
            act.wait_ge(y_norm, 8)
            for c in range(2):
                queries_hi("qa2", c)
            for c in range(2):
                keys_hi("ka2", c)
            v_heads("va2")

            def moba_exps(m):
                causal_exps("moba", R0["moba"])(m)
                if m == 16:
                    step(G["ka2"][3])
                    load(B["x_acc"][:, :, :], x1_dram, x1_back)
                if 17 <= m < 21:
                    split_y(8 + m - 17, 4 + m - 17)

            def moba_out(h):
                stacked_out("moba_pv", B["z_b"][:, 0:2, :])(h)
                if h == 6:
                    after_vector(G["moba_pv"][5])
                    for k in range(3):
                        split_y(12 + k, k)

            attention("moba", 32, lambda m: probs_hi(R0["moba"] + m, m, G["moba_pv"]), moba_exps, moba_out,
                      lambda k: (queries_hi, keys_hi)[k // 2](("qa2", "ka2")[k // 2], 2 + k % 2) if k < 4 else None)
            for t in range(2):
                load(B["h_m2"][:, t, :], mem_in[:, t, :], mem_in_s)
            load(B["gain2"][:, 0, :], row("norm_mem_2"), gain_in[3])
            load(B["gain2"][:, 1, :], row("norm_xattn_2"), gain_in[3])
            after_vector(G["moba_pv"][7])
            split_y(15, 3)
            act.wait_ge(mem_in_s, 32)
            for t in range(2):
                square_sum(Q0["mem"] + t, N0["mem"] + t, B["h_m2"][:, t, :], B["junk2"][:, :])
            for t in range(2):
                turned_tile_hi("mem", t, B["mem_hi"])
            act.wait_ge(h_ready, H0["mem"] + 2)
            load(B["gain2"][:, 0, :], row("norm_mlp_2"), gain_in[4])
            for t in range(NT):
                after_vector(G["out2"][4 + t])
                square_sum(Q0["nx"] + t, N0["nx"] + t, B["x_res"][:, t, :], B["junk2"][:, :])

            def unit_hi(name, n):
                u = U[name][n]
                act.wait_ge(w_loaded[u % 2], 16 * (u // 2 + 1))
                act.wait_ge(lin_step, PLAN.unit_last_step[u - 2])
                act.activation(w_hi[u % 2][:, :], w_raw[u % 2][:, :], ACT.Copy).then_inc(w_scalar_hi, 1)

            for t in range(NT):
                for c in (2 * t, 2 * t + 1):
                    step(G["kx"][c])
                    act.activation(B["xk_hi"][:, c, :], bank(G["kx"][c], MEM), ACT.Copy).then_inc(act_evac, 1)
                unit_hi(*HI_BY_SCALAR[t])
                turned_tile_hi("nx", t, B["h_hi"])
            for j in range(2):
                unit_hi("vx", 2 + j)
                for t in range(2):
                    copy_lin(G["vx"][2 * j + t], B["xv_hi"][:, t, T * j:T * j + T])
            act.wait_ge(h_ready, H0["nx"] + 4)
            load(B["gain2"][:, 1, :], row("norm_final_2"), gain_in[5])

            def x_queries_hi(c):
                copy_lin(G["xq"][c], B["xq_hi"][:, c, :], (D // 4) ** -0.5)

            for c in range(4):
                x_queries_hi(c)

            def x_exps(m):
                if m >= 4:
                    act.wait_ge(tr_done, R0["x"] + m - 3)
                exponentials(S0["x"] + m, B["xp"][:, m % 4, :], MEM)

            def x_hi(m):
                h, i, r = m // 4, m % 4, R0["x"] + m
                act.wait_ge(tr_done, r + 1)
                if h >= 2:
                    step(G["x_pv"][2 * (h - 2) + 1])
                out = B["xpt_hi"][:, h % 2, :].rearrange("p (j q) -> p j q", j=2)[:, :, P * i:P * i + P]
                act.activation(out, tr[:, r % 2, 0:MEM].rearrange("p (j c) -> p j c", j=2), ACT.Copy)\
                    .then_inc(tr_hi, 1)

            def x_out_hi(h):
                for dv in range(2):
                    copy_lin(G["x_pv"][2 * h + dv], B["h_hi"][:, 2 * h + dv, :])

            attention("x", 16, x_hi, x_exps, x_out_hi, lambda k: x_queries_hi(4 + k) if k < 4 else None)
            for n in range(NT + 2):
                if n < NT:
                    after_vector(G["xo_b"][4 + n])
                    square_sum(Q0["nmlp"] + n, N0["nmlp"] + n, B["x_res"][:, n, :], B["junk2"][:, :])
                if 0 <= n - 2 < NT:
                    turned_tile_hi("nmlp", n - 2, B["h_hi"])
            with act.Fori(0, FF_CHUNKS) as it:
                off = mlp_offsets(it)
                for c in range(8):
                    g = G["mlp"][c]
                    act.wait_ge(lin_step, ST[g] + off.step)
                    act.wait_ge(dve_evac, (DN[g - 2] if c >= 2 else DN[G["mlp"][0] - 1]) + off.dve)
                    act.activation(B["relu"][:, c % 2, :], bank(g), ACT.Relu).then_inc(act_evac, 1)
                    act.wait_ge(dve_evac, DN[g] + off.dve)
                    act.activation(B["u_hi"][:, c, :], B["u_f"][:, c % 2, :], ACT.Copy).then_inc(u_hi_s, 1)
            for t in range(NT):
                act.wait_ge(dve_evac, DN[len(K_) - 4 + t])
                square_sum(Q0["final"] + t, N0["final"] + t, B["x_res"][:, t, :], B["junk2"][:, :])

        @block.vector
        def _(dve):
            own = [0]

            def link(ins):
                own[0] += 1
                ins.then_inc(dve_self, 1)
                dve.wait_ge(dve_self, own[0])

            def step(g, off=HERE):
                dve.wait_ge(lin_step, ST[g] + off.step)

            def bank(g, cols=T):
                return lin[:, g % 4, 0:cols]

            def after_scalar(g, off=HERE):
                dve.wait_ge(act_evac, AN[g] + off.act)

            def variance(n, halves=1, done=var_done):
                src = sumsq[:, n, 0:1]
                if halves == 2:
                    link(dve.tensor_tensor(src, src, sumsq[:, n, 1:2], ALU.add))
                dve.tensor_scalar(var[:, n:n + 1], src, 1.0 / D, EPS, ALU.mult, ALU.add).then_inc(done, 1)

            def normed(name, t, out, x, gain):
                if t >= 2:
                    dve.wait_ge(tr_done, R0[name] + 2 * (t - 1))
                dve.wait_ge(rstd_done, N0[name] + t + 1)
                n = N0[name] + t
                dve.scalar_tensor_tensor(out, x, rstd[:, n:n + 1], gain, ALU.mult, ALU.mult).then_inc(h_ready, 1)

            def turned_tile_lo(name, t, hi, lo):
                for half in range(2):
                    r = R0[name] + 2 * t + half
                    k, c = slice(4 * half, 4 * half + 4), slice(P * t, P * t + P)
                    dve.wait_ge(tr_hi, r + 1)
                    dve.tensor_tensor(lo[:, k, c], tr[:, r % 2, :].rearrange("p (b c) -> p b c", b=4),
                                      as_f32(hi[:, k, c]), ALU.subtract).then_inc(tr_lo, 1)

            def lo_part(out, x, hi, scale=1.0):
                if scale == 1.0:
                    return dve.tensor_tensor(out, x, as_f32(hi), ALU.subtract)
                return dve.scalar_tensor_tensor(out, x, scale, as_f32(hi), ALU.mult, ALU.subtract)

            def q_lo(x, c, scale):
                q = B["q_st"]
                lo_part(q[64:128, 2 * c, :], x[0:64], q[0:64, 2 * c, :], scale)
                return lo_part(q[0:64, 2 * c + 1, :], x[64:128], q[64:128, 2 * c + 1, :], scale)

            def k_lo(x, c):
                for head in range(2):
                    rows = slice(64 * head, 64 * head + 64)
                    ins = lo_part(B["k_lo"][rows, c, :], x[rows], B["k_hh"][rows, 2 * c + head, :])
                return ins

            def queries_lo(name, c):
                after_scalar(G[name][c])
                q_lo(bank(G[name][c]), c, HD ** -0.5).then_inc(dve_evac, 1)

            def keys_lo(name, c):
                after_scalar(G[name][c])
                k_lo(bank(G[name][c]), c).then_inc(dve_evac, 1)

            def row_max(s, n):
                dve.wait_ge(s_done, s + 1)
                dve.reduce_max(neg_max[:, s:s + 1], sc[:, s % 2, 0:n], AX, negate=True).then_inc(s_max, 1)

            def invert(s):
                dve.wait_ge(s_exp, s + 1)
                dve.reciprocal(rden[:, s:s + 1], denom[:, s:s + 1]).then_inc(s_rec, 1)

            def probs_lo(r, m):
                h, i = m // 4, m % 4
                dve.wait_ge(tr_hi, r + 1)
                dve.tensor_tensor(blocks(B["pt_lo"], h % 2, i),
                                  tr[:, r % 2, 0:P * (i + 1)].rearrange("p (j c) -> p j c", c=P),
                                  as_f32(blocks(B["pt_hi"], h % 2, i)), ALU.subtract).then_inc(tr_lo, 1)

            def attention(name, tiles, maxima, lo, inverses, values, fill):
                for m in range(tiles + 6):
                    if m < tiles:
                        maxima(m)
                    if 0 <= m - 4 < tiles:
                        lo(m - 4)
                    if 0 <= m - 1 < tiles:
                        inverses(m - 1)
                    if m >= 1 and fill_ends(name, m - 1) is not None:
                        fill(fill_ends(name, m - 1))
                    if m >= 9 and m % 4 == 1:
                        values((m - 9) // 4)

            def stacked_out(name, tmp):
                def f(h):
                    g = G[name][h]
                    after_scalar(g)
                    dve.tensor_tensor(B["y_0"][64 * (h % 2):64 * (h % 2) + 64, h // 2, :], lin[0:64, g % 4, :],
                                      tmp[0:64, h % 2, :], ALU.add).then_inc(dve_evac, 1)
                return f

            def causal_max(name):
                return lambda m: row_max(S0[name] + m, P * (m % 4 + 1))

            def soft_sum(x, t1, done, ready):
                dve.wait_ge(done, ready)
                link(dve.scalar_tensor_tensor(x, x, 0.0, t1, ALU.min, ALU.subtract))

            def v_heads(name):
                g0 = G[name][0]
                for t in range(NT):
                    after_scalar(g0 + t)
                    v = B["v_hl"][:, t, :].rearrange("p (h s d) -> p h s d", h=8, s=2)
                    dve.tensor_tensor(v[:, :, 1, :], bank(g0 + t).rearrange("p (h d) -> p h d", h=8),
                                      as_f32(v[:, :, 0, :]), ALU.subtract).then_inc(dve_evac, 1)

            def head_norms(g0, y, root):
                for h in range(4):
                    after_scalar(g0 + h)
                    link(dve.reciprocal(root[:, h % 2, :], root[:, h % 2, :]))
                    dve.tensor_tensor(y[:, h, :], y[:, h, :], root[:, h % 2, :], ALU.mult).then_inc(y_norm, 1)

            def split_y(n, k):
                src = B["y_0"][:, k, :] if k < 4 else B["y_1"][:, k - 4, :]
                dve.wait_ge(y_hi_s, n + 1)
                if 8 <= n < 12:
                    lo_part(B["yg_lo"][:, k - 4, :], src, B["yg_hi"][:, k - 4, :]).then_inc(y_lo_s, 1)
                else:
                    lo_part(B["y_lo"][:, k, :], src, B["y_hi"][:, k, :]).then_inc(y_lo_s, 1)

            dve.wait_ge(consts_made, 1)
            dve.wait_ge(gain_in[0], 16)
            for n in range(NT + 2):
                if n < NT:
                    dve.wait_ge(sq_done, Q0["norm1"] + n + 1)
                    variance(N0["norm1"] + n)
                if 0 <= n - 1 < NT:
                    t = n - 1
                    normed("norm1", t, B["h_m"][:, t % 2, :], B["x_m"][:, t, :], B["gain"][:, 0, :])
                if 0 <= n - 2 < NT:
                    turned_tile_lo("norm1", n - 2, B["h_hi"], B["h_lo"])
            dve.tensor_tensor(pick[:, :], ident[:, 0:8], ident[:, 32:40], ALU.add)
            dve.wait_ge(small_in, 16 * 5)
            link(dve.tensor_scalar(g_subln[:, :], g_subln[:, :], 1.0 - LAM_INIT, None, ALU.mult))
            dve.wait_ge(small_in2, 16 * 4)
            pairs = B["lam_v"][:, :, :].rearrange("p (a b) d -> p a b d", b=2)
            link(dve.tensor_tensor(pairs[:, :, 0, :], pairs[:, :, 0, :], pairs[:, :, 1, :], ALU.mult))
            dve.tensor_reduce(lam_d[:, :], pairs[:, :, 0, :], AX, ALU.add).then_inc(lam_ready, 1)
            dve.wait_ge(lam_exp, 1)
            link(dve.scalar_tensor_tensor(neg_lam[:, :], lam_e[:, 1:2], LAM_INIT, lam_e[:, 0:1], ALU.subtract,
                                          ALU.subtract))
            g = G["fa"][0]
            step(g)
            fx, ft, fc = (B["y_0"][0:8, n, :] for n in (0, 1, 3))
            f_one = B["y_1"][0:8, 0, :]
            dve.wait_ge(h_ready, H0["norm1"] + 4)
            dve.memset(f_one, 1.0)
            dve.tensor_scalar(fx, lin[0:8, g % 4, :], b_forget[0:8, :], None, ALU.add).then_inc(dve_evac, 1)
            soft_sum(fx, ft, fa_ln, 1)
            link(dve.tensor_tensor_scan(fc, f_one, fx, 0.0, ALU.mult, ALU.add))
            link(dve.tensor_scalar(c_row[0:8, :], fc, -1.0, None, ALU.mult))
            dve.scalar_tensor_tensor(c_row[32:40, :], fc, -1.0, as_f32(c_row[0:8, :]), ALU.mult, ALU.subtract)\
                .then_inc(c_ready, 1)
            for c in range(2):
                queries_lo("qa", c)
            for c in range(2):
                keys_lo("ka", c)
            v_heads("va")

            def fox_fill(k):
                if k < 4:
                    (queries_lo, keys_lo)[k // 2](("qa", "ka")[k // 2], 2 + k % 2)

            attention("fox", 32, causal_max("fox"), lambda m: probs_lo(R0["fox"] + m, m),
                      lambda m: invert(S0["fox"] + m), stacked_out("fox_pv", fox_tmp), fox_fill)
            dve.wait_ge(dve_evac, DN[G["fox_pv"][7]])
            dve.wait_ge(za_silu, 1)
            for c in range(4):
                y = B["y_0"][:, c, :]
                dve.tensor_tensor(y, y, B["y_1"][:, c, :], ALU.mult).then_inc(ya_gated, 1)
            dve.wait_ge(rope_in, 32)

            def rope_lo_part(c):
                dve.wait_ge(rope_hi, c + 1)
                x = B["t_a"][:, c % 2, :]
                ins = q_lo(x, c, HD ** -0.5) if c < 4 else k_lo(x, c - 4)
                ins.then_inc(rope_lo, 1)

            for c in range(8):
                g = G["qb"][0] + c
                after_scalar(g)
                if c >= 2:
                    dve.wait_ge(rope_lo, c - 1)
                x = B["t_a"][:, c % 2, :]
                dve.tensor_tensor(x, bank(g), B["rope_c"][:, :], ALU.mult).then_inc(dve_evac, 1)
                if c >= 1:
                    rope_lo_part(c - 1)
                dve.wait_ge(rot_mul, c + 1)
                dve.wait_ge(dve_evac, DN[g])
                dve.tensor_tensor(x, x, B["t_b"][:, c % 2, :], ALU.add).then_inc(rope_done, 1)
            rope_lo_part(7)
            for t in range(NT):
                after_scalar(G["vb"][t])
                v = B["v_hl"][:, t, :]
                lo_part(v[:, T:2 * T], bank(G["vb"][t]), v[:, 0:T]).then_inc(dve_evac, 1)

            def diff_max(w):
                for m in range(2):
                    row_max(S0["diff"] + 2 * w + m, P * (w % 4 + 1))

            def diff_invert(w):
                s = S0["diff"] + 2 * w
                dve.wait_ge(s_exp, s + 2)
                dve.reciprocal(rden[:, s:s + 2], denom[:, s:s + 2]).then_inc(s_rec, 1)
                dve.wait_ge(s_rec, V0["diff"] + w + 1)
                link(dve.tensor_scalar(rden[:, s + 1:s + 2], rden[:, s + 1:s + 2], neg_lam[:, :], None, ALU.mult))

            def difference(w):
                i, s = w % 4, S0["diff"] + 2 * w
                c = slice(P_OFF[i], P_OFF[i] + P * (i + 1))
                dve.wait_ge(s_norm, V0["diff"] + w + 1)
                dve.scalar_tensor_tensor(B["p0"][:, c], B["px"][:, c], rden[:, s + 1:s + 2], B["p0"][:, c],
                                         ALU.mult, ALU.add).then_inc(pd_done, 1)

            for w in range(16 + 5):
                if 0 <= w - 5 < 16:
                    probs_lo(R0["diff"] + w - 5, w - 5)
                if 0 <= w - 2 < 16:
                    difference(w - 2)
                if w < 16:
                    diff_max(w)
                if 0 <= w - 1 < 16:
                    diff_invert(w - 1)
            for k in range(4):
                split_y(k, k)
            head_norms(G["subln"][0], B["y_1"], B["t_r"])
            dve.wait_ge(y_norm, 4)
            dve.wait_ge(zb_silu, 1)
            for c in range(4):
                y = B["y_1"][:, c, :]
                dve.scalar_tensor_tensor(y, y, g_subln[:, :], B["z_b"][:, c, :], ALU.mult, ALU.mult)\
                    .then_inc(yb_gated, 1)
            for k in range(4, 8):
                split_y(k, k)
            with dve.Fori(0, 2) as it:
                off = gate_offsets(it)
                for c in range(2):
                    for n in range(2):
                        g = G["gates"][8 * c + 4 + 2 * n]
                        dve.wait_ge(act_evac, AN[g] + off.act)
                        for br, buf in enumerate(("t_a", "t_b")):
                            step(g + br, off)
                            dve.tensor_tensor(B[buf][:, n, :], bank(g + br), B["t_g"][:, 2 * br + n, :], ALU.mult)\
                                .then_inc(dve_evac, 1)
                        dve.wait_ge(dve_evac, DN[g + 1] + off.dve)
                        dve.tensor_tensor(B["t_c"][:, n, :], B["t_a"][:, n, :], B["t_b"][:, n, :], ALU.add)\
                            .then_inc(mg_sum, 1)
                        dve.wait_ge(mg_hi, it * 4 + (2 * c + n + 1))
                        tile = bass.ds(it * 4 + (2 * c + n), 1)
                        dve.tensor_tensor(B["m_lo"][:, tile, :], B["t_c"][:, n:n + 1, :],
                                          as_f32(B["m_hi"][:, tile, :]), ALU.subtract).then_inc(mg_lo, 1)
            dve.wait_ge(mg_lo, 8)
            dve.wait_ge(gain_in[1], 16)
            dve.wait_ge(gain_in[2], 16)
            dve.wait_ge(x_again, 16 * NT)

            def gained(j, t):
                g, c = G["out1"][4 * j + t], slice(T * j, T * j + T)
                after_scalar(g)
                dve.tensor_tensor(B["y_m"][:, t, c], bank(g), B["gain"][:, 0, c], ALU.mult).then_inc(dve_evac, 1)

            for t in range(NT):
                gained(0, t)
            for n in range(NT + 4):
                if 0 <= n - 1 < NT:
                    t = n - 1
                    dve.wait_ge(post_root, t + 1)
                    dve.wait_ge(dve_evac, DN[G["out1"][4 + t]])
                    x, r = B["x_m"][:, t, :], N0["post"] + t
                    dve.scalar_tensor_tensor(x, B["y_m"][:, t, :], rstd[:, r:r + 1], x, ALU.mult, ALU.add)\
                        .then_inc(x1_ready, 1)
                if n < NT:
                    after_scalar(G["out1"][4 + n])
                    variance(N0["post"] + n, halves=2, done=post_var)
                    gained(1, n)
                if 0 <= n - 2 < NT:
                    dve.wait_ge(sq_done, Q0["mix"] + n - 1)
                    variance(N0["mix"] + n - 2)
                if 0 <= n - 3 < NT:
                    t = n - 3
                    normed("mix", t, B["h_m"][:, t % 2, :], B["x_m"][:, t, :], B["gain"][:, 1, :])
                if 0 <= n - 4 < NT:
                    turned_tile_lo("mix", n - 4, B["h_hi"], B["h_lo"])
            g = G["bias"][0]
            step(g)
            link(dve.tensor_copy(B["g_x"][0:8, 0, 0:1], lin[0:8, g % 4, 0:1]))
            dve.tensor_scalar(B["beta"][0:8, :], lin[0:8, g % 4, 0:BIAS_COLS], B["g_x"][0:8, 0, 0:1], None,
                              ALU.subtract).then_inc(dve_evac, 1)
            dve.wait_ge(dve_evac, DN[g])
            dve.memset(B["beta"][0:8, 257:BIAS_COLS], FAR).then_inc(beta_ready, 1)
            for dt in range(2):
                g = G["gup"][dt]
                step(g)
                dve.tensor_scalar(B["g_x"][:, dt, :], bank(g), b_gate[:, dt:dt + 1], None, ALU.add)\
                    .then_inc(dve_evac, 1)
            soft_sum(B["g_x"][:, :, :], B["g_d"][:, 0], gla_ln, 1)
            link(dve.tensor_scalar(B["g_x"][:, :, :], B["g_x"][:, :, :], 1.0 / 16.0, None, ALU.mult))
            dve.wait_ge(gla_const, 1)
            for dt in range(2):
                link(dve.tensor_tensor_scan(B["g_b"][:, dt, :], B["g_keep"][:, :], B["g_x"][:, dt, :], 0.0,
                                            ALU.mult, ALU.add))

            def halves(buf, s):
                v = buf.rearrange("p t q -> p (t q)").rearrange("p (n c) -> p n c", c=2 * s)
                return v[:, :, 0:s], v[:, :, s:2 * s]

            def level_distance(lev):
                s = LEVELS[lev]
                n = 2 * T // (2 * s)
                first, second = halves(B["g_b"][:, :, :], s)
                middle = first[:, :, s - 1:s].to_broadcast([P, n, s])
                d_first, d_second = halves(B["g_d"][:, lev % 2], s)
                dve.wait_ge(gz_done, max(lev, 1))
                dve.tensor_tensor(d_first, middle, first, ALU.subtract)
                dve.tensor_tensor(d_second, second, middle, ALU.subtract).then_inc(gd_done, 1)

            def level_operands(lev):
                s = LEVELS[lev]
                dve.wait_ge(ge_done, lev + 4)
                if lev >= 2:
                    step(G["levels"][4 * (lev - 2) + 3])
                e_first, e_second = halves(B["g_d"][:, lev % 2], s)
                z_first, z_second = halves(B["g_z"][:, lev % 2], s)
                dve.tensor_tensor(z_first, e_first, halves(B["g_k"][:, :, :], s)[0], ALU.mult)
                dve.tensor_tensor(z_second, e_second, halves(B["g_q"][:, :, :], s)[1], ALU.mult).then_inc(gz_done, 1)

            def level_scores(lev):
                for h in range(4):
                    g = G["levels"][4 * lev + h]
                    step(g)
                    if lev > 0:
                        dve.wait_ge(dve_evac, DN[G["levels"][4 * (lev - 1) + h]])
                    dve.copy_predicated(diagonal(B["g_a"], h),
                                        B["g_mask"][:, lev:lev + 1, :].to_broadcast([P, NT, P]),
                                        bank(g).rearrange("p (t q) -> p t q", q=P)).then_inc(dve_evac, 1)

            last = B["g_b"][:, :, P - 1:T:P].rearrange("p t (n o) -> p t n o", o=1)
            b4 = B["g_b"][:, :, :].rearrange("p t (n c) -> p t n c", c=P)
            for dt in range(2):
                ins = dve.tensor_tensor(B["g_d"][:, 0, dt, :].rearrange("p (n c) -> p n c", c=P),
                                        last[:, dt].to_broadcast([P, NT, P]), b4[:, dt], ALU.subtract)
            ins.then_inc(gd_done, 1)
            dve.tensor_copy(B["g_d"][:, 1], B["g_b"][:, :, :]).then_inc(gd_done, 1)
            dve.wait_ge(act_evac, AN[G["kg"][1]])
            dve.wait_ge(ge_done, 3)
            dve.tensor_tensor(B["g_qe"][:, :, :], B["g_d"][:, 1], B["g_q"][:, :, :], ALU.mult)
            link(dve.tensor_tensor(B["g_kd"][:, :, :], B["g_d"][:, 0], B["g_k"][:, :, :], ALU.mult))
            for dt in range(2):
                kd, kx = B["g_kd"][:, dt, :], B["g_kx"][:, dt]
                link(dve.tensor_scalar(kx[:, 0, :], kd[:, 0:P], g_tail[:, dt, 1:2], None, ALU.mult))
                dve.tensor_scalar(kx[:, 1, :], kx[:, 0, :], g_tail[:, dt, 2:3], None, ALU.mult)
                ins = dve.tensor_scalar(kx[:, 2, :], kd[:, P:2 * P], g_tail[:, dt, 2:3], None, ALU.mult)
            ins.then_inc(gz_done, 1)
            for lev in range(2):
                level_distance(lev)
            dve.wait_ge(gla_in, 48)
            for lev in range(2):
                level_operands(lev)
            for lev in range(2, 4):
                level_distance(lev)
            for lev in range(len(LEVELS)):
                level_scores(lev)
                if lev + 2 < len(LEVELS):
                    level_operands(lev + 2)
                if lev + 4 < len(LEVELS):
                    level_distance(lev + 4)
            level_scores(len(LEVELS))
            head_norms(G["gnorm"][0], B["y_1"], B["g_d"][:, 1])
            dve.wait_ge(y_norm, 8)
            dve.wait_ge(rg_silu, 1)
            for h in range(4):
                y = B["y_1"][:, h, :]
                link(dve.scalar_tensor_tensor(y, y, g_gain[:, :], B["y_0"][:, h, :], ALU.mult, ALU.mult))
            for c in range(2):
                queries_lo("qa2", c)
            for c in range(2):
                keys_lo("ka2", c)
            v_heads("va2")

            def moba_max(m):
                causal_max("moba")(m)
                if 18 <= m < 22:
                    split_y(8 + m - 18, 4 + m - 18)

            def moba_fill(k):
                if k < 4:
                    (queries_lo, keys_lo)[k // 2](("qa2", "ka2")[k // 2], 2 + k % 2)
                    return
                j, t = divmod(k - 4, 4)
                step(G["out2g"][k - 4])
                if k == 4:
                    dve.wait_ge(x1_back, 16)
                x = B["x_acc"][:, t, T * j:T * j + T]
                dve.tensor_tensor(x, x, bank(G["out2g"][k - 4]), ALU.add).then_inc(dve_evac, 1)

            def moba_out(h):
                stacked_out("moba_pv", B["z_b"][:, 0:2, :])(h)
                if h == 6:
                    for k in range(3):
                        split_y(12 + k, k)

            attention("moba", 32, moba_max, lambda m: probs_lo(R0["moba"] + m, m), lambda m: invert(S0["moba"] + m),
                      moba_out, moba_fill)
            split_y(15, 3)
            for t in range(2):
                dve.wait_ge(sq_done, Q0["mem"] + t + 1)
                variance(N0["mem"] + t)
            dve.wait_ge(gain_in[3], 32)
            for t in range(2):
                normed("mem", t, B["h_m2"][:, t, :], B["h_m2"][:, t, :], B["gain2"][:, 0, :])

            def add_to_x(g, t, j, off=HERE):
                step(g, off)
                x = B["x_res"][:, t, T * j:T * j + T]
                dve.tensor_tensor(x, x, bank(g), ALU.add).then_inc(dve_evac, 1)

            def moba_part(n):
                j, t = divmod(n, 4)
                g, c = G["out2"][n], slice(T * j, T * j + T)
                step(g)
                dve.tensor_tensor(B["x_res"][:, t, c], B["x_acc"][:, t, c], bank(g), ALU.add).then_inc(dve_evac, 1)

            dve.wait_ge(y_lo_s, 16)
            dve.wait_ge(dve_evac, DN[G["out2g"][7]])
            for t in range(NT):
                moba_part(t)
            for t in range(2):
                turned_tile_lo("mem", t, B["mem_hi"], B["mem_lo"])

            def nx_tile(t):
                normed("nx", t, B["h_m2"][:, t % 2, :], B["x_res"][:, t, :], B["gain2"][:, 1, :])

            dve.wait_ge(tr_done, R0["mem"] + 4)
            for n in range(NT):
                moba_part(4 + n)
                if 0 <= n - 1 < 2:
                    nx_tile(n - 1)
                dve.wait_ge(sq_done, Q0["nx"] + n + 1)
                variance(N0["nx"] + n)
            for t in range(NT):
                for c in (2 * t, 2 * t + 1):
                    after_scalar(G["kx"][c])
                    lo_part(B["xk_lo"][:, c, :], bank(G["kx"][c], MEM), B["xk_hi"][:, c, :]).then_inc(dve_evac, 1)
                turned_tile_lo("nx", t, B["h_hi"], B["h_lo"])
                if t + 2 < NT:
                    nx_tile(t + 2)
            for j in range(2):
                for t in range(2):
                    g, c = G["vx"][2 * j + t], slice(T * j, T * j + T)
                    after_scalar(g)
                    lo_part(B["xv_lo"][:, t, c], bank(g), B["xv_hi"][:, t, c]).then_inc(dve_evac, 1)

            def x_queries_lo(c):
                g = G["xq"][c]
                after_scalar(g)
                lo_part(B["xq_lo"][:, c, :], bank(g), B["xq_hi"][:, c, :], (D // 4) ** -0.5).then_inc(dve_evac, 1)

            for c in range(4):
                x_queries_lo(c)

            def x_lo(m):
                h, i, r = m // 4, m % 4, R0["x"] + m
                dve.wait_ge(tr_hi, r + 1)
                hi, lo = (b[:, h % 2, :].rearrange("p (j q) -> p j q", j=2)[:, :, P * i:P * i + P]
                          for b in (B["xpt_hi"], B["xpt_lo"]))
                dve.tensor_tensor(lo, tr[:, r % 2, 0:MEM].rearrange("p (j c) -> p j c", j=2), as_f32(hi),
                                  ALU.subtract).then_inc(tr_lo, 1)

            def x_out_lo(h):
                for dv in range(2):
                    g = G["x_pv"][2 * h + dv]
                    after_scalar(g)
                    lo_part(B["h_lo"][:, 2 * h + dv, :], bank(g), B["h_hi"][:, 2 * h + dv, :]).then_inc(dve_evac, 1)

            def x_fill(k):
                if k < 4:
                    x_queries_lo(4 + k)
                else:
                    add_to_x(G["xo_a"][k - 4], (k - 4) % 4, (k - 4) // 4)

            attention("x", 16, lambda m: row_max(S0["x"] + m, MEM), x_lo, lambda m: invert(S0["x"] + m), x_out_lo,
                      x_fill)
            for t in range(NT):
                add_to_x(G["xo_b"][t], t, 0)
            dve.wait_ge(gain_in[4], 16)
            dve.wait_ge(gain_in[5], 16)
            dve.wait_ge(tr_done, R0["nx"] + 8)
            for n in range(NT + 2):
                if n < NT:
                    add_to_x(G["xo_b"][4 + n], n, 1)
                if 0 <= n - 1 < NT:
                    t = n - 1
                    normed("nmlp", t, B["h_m2"][:, t % 2, :], B["x_res"][:, t, :], B["gain2"][:, 0, :])
                if n < NT:
                    dve.wait_ge(sq_done, Q0["nmlp"] + n + 1)
                    variance(N0["nmlp"] + n)
                if 0 <= n - 2 < NT:
                    turned_tile_lo("nmlp", n - 2, B["h_hi"], B["h_lo"])
            with dve.Fori(0, FF_CHUNKS) as it:
                off = mlp_offsets(it)
                for c in range(8):
                    g = G["mlp"][c]
                    dve.wait_ge(act_evac, AN[g] + off.act)
                    u = B["u_f"][:, c % 2, :]
                    r = B["relu"][:, c % 2, :]
                    dve.scalar_tensor_tensor(u, bank(g), 0.0, r, ALU.max, ALU.mult).then_inc(dve_evac, 1)
                    dve.wait_ge(u_hi_s, it * 8 + (c + 1))
                    lo_part(B["u_lo"][:, c, :], u, B["u_hi"][:, c, :]).then_inc(u_lo_s, 1)
                for j in range(2):
                    for t in range(NT):
                        add_to_x(G["mlp"][8 + 4 * j + t], t, j, off)
            for n in range(NT + 1):
                if n < NT:
                    dve.wait_ge(sq_done, Q0["final"] + n + 1)
                    variance(N0["final"] + n)
                if n >= 1:
                    r = N0["final"] + n - 1
                    dve.wait_ge(rstd_done, r + 1)
                    x = B["x_res"][:, n - 1, :]
                    dve.scalar_tensor_tensor(x, x, rstd[:, r:r + 1], B["gain2"][:, 1, :], ALU.mult, ALU.mult)\
                        .then_inc(final_ready, 1)


INPUTS = ["x", "g_pre", "w_in", "b_forget", "lambda_q1", "lambda_k1", "lambda_q2", "lambda_k2", "g_subln",
          "w_branch", "w_out", "g_post", "mem_2", "rp_table_2", "norm_mix_2", "w_in_2", "w_gate_up_2", "b_gate_2",
          "g_norm_2", "w_out_2", "norm_xattn_2", "norm_mem_2", "w_xq_2", "w_xkv_2", "w_xo_2", "norm_mlp_2",
          "w_up_2", "w_down_2", "norm_final_2"]


def kernel(**inputs):
    import concourse.bacc as bacc
    from concourse.bass_utils import run_bass_kernel_spmd as run

    nc = bacc.Bacc("TRN2", target_bir_lowering=False, num_devices=1)
    arrays = {name: np.ascontiguousarray(inputs[name]) for name in INPUTS}
    arrays |= shape_constants()
    tensors = {name: nc.dram_tensor(f"in_{name}", v.shape, mybir.dt.from_np(v.dtype), kind="ExternalInput").ap()
               for name, v in arrays.items()}
    tensors["x1_dram"] = nc.dram_tensor("x1_dram", (T, D), F32, kind="Internal").ap()
    tensors["bias_dram"] = nc.dram_tensor("bias_dram", (8, BIAS_COLS), F32, kind="Internal").ap()
    out = nc.dram_tensor("out_0", (1, T, D), F32, kind="ExternalOutput").ap()
    two_blocks_kernel(nc, tensors, out)
    result = run(nc, [{f"in_{name}": v for name, v in arrays.items()}], core_ids=[0])
    return result.results[0]["out_0"]
```
